# Optimizing a Trainium2 kernel written in Bass

```python
import jax, jax.numpy as jnp
from jax import lax
import numpy as np

D_MODEL = 1024
BATCH = 1
SEQ = 1024
DEPTH = 2
DEC_BATCH = 8
DEC_SEQ = 8
PAST_LEN = 1024
PAGE_SIZE = 128

N_A_LAYERS = DEPTH // 2
N_B_LAYERS = DEPTH - N_A_LAYERS
N_HEADS = 16
HEAD_DIM = D_MODEL // N_HEADS
CONV_WIDTH = 3
D_FF = -(-8 * D_MODEL // (3 * 256)) * 256
PLE_DIM = 256
Q_BLOCK = 128
EPS = 1e-6
FORGET_BIAS_INIT = 3.0

kernel_name = "yoco_shortconv_forgetting_attn_step"

def rmsnorm(x, g):
    xf = x.astype(jnp.float32)
    y = xf * lax.rsqrt(jnp.mean(xf * xf, axis=-1, keepdims=True) + EPS) * g.astype(jnp.float32)
    return y.astype(x.dtype)

def swiglu(x, w_gate, w_up, w_down):
    return (jax.nn.silu(x @ w_gate) * (x @ w_up)) @ w_down

def short_conv(x, w_in, w_conv, w_out, buf):
    b_gate, c_gate, u = jnp.split(x @ w_in, 3, axis=-1)
    cu = c_gate * u
    t = x.shape[1]
    padded = jnp.concatenate([buf.astype(cu.dtype), cu], axis=1)
    conv = w_conv[0] * padded[:, 0:t]
    for k in range(1, CONV_WIDTH):
        conv = conv + w_conv[k] * padded[:, k:k + t]
    y = (b_gate * conv) @ w_out
    return y, padded[:, -(CONV_WIDTH - 1):]

def shared_kv(h, g_kv, w_k, w_v, w_f, b_f):
    b, t, _ = h.shape
    z = rmsnorm(h, g_kv)
    k = (z @ w_k).reshape(b, t, N_HEADS, HEAD_DIM)
    v = (z @ w_v).reshape(b, t, N_HEADS, HEAD_DIM)
    logf = jax.nn.log_sigmoid((z @ w_f + b_f).astype(jnp.float32))
    return k, v, logf

def forgetting_attn_prompt(q, k, v, logf):
    b, s_len, h, dh = q.shape
    f_cum = jnp.transpose(jnp.cumsum(logf.astype(jnp.float32), axis=1), (0, 2, 1))
    key_pos = jnp.arange(s_len)
    scale = HEAD_DIM ** -0.5

    def block(i):
        start = i * Q_BLOCK
        qb = lax.dynamic_slice_in_dim(q, start, Q_BLOCK, axis=1)
        fq = lax.dynamic_slice_in_dim(f_cum, start, Q_BLOCK, axis=2)
        logits = (jnp.einsum('bqhd,bkhd->bhqk', qb, k).astype(jnp.float32) * scale
                  + (fq[..., None] - f_cum[:, :, None, :]))
        qpos = start + jnp.arange(Q_BLOCK)
        logits = jnp.where(qpos[:, None] >= key_pos[None, :], logits, -jnp.inf)
        probs = jax.nn.softmax(logits, axis=-1).astype(v.dtype)
        return jnp.einsum('bhqk,bkhd->bqhd', probs, v)

    out = lax.map(block, jnp.arange(s_len // Q_BLOCK))
    return jnp.moveaxis(out, 0, 1).reshape(b, s_len, h * dh)

def forgetting_attn_sample(q, k_past, v_past, logf_past, k_new, v_new, logf_new):
    bd, t, h, dh = q.shape
    scale = HEAD_DIM ** -0.5
    f_past = jnp.cumsum(logf_past.astype(jnp.float32), axis=1)
    f_new = f_past[:, -1:] + jnp.cumsum(logf_new.astype(jnp.float32), axis=1)
    fq = jnp.transpose(f_new, (0, 2, 1))[..., None]
    s_past = (jnp.einsum('bqhd,bkhd->bhqk', q, k_past).astype(jnp.float32) * scale
              + fq - jnp.transpose(f_past, (0, 2, 1))[:, :, None, :])
    s_new = (jnp.einsum('bqhd,bkhd->bhqk', q, k_new).astype(jnp.float32) * scale
             + fq - jnp.transpose(f_new, (0, 2, 1))[:, :, None, :])
    causal = jnp.arange(t)[:, None] >= jnp.arange(t)[None, :]
    s_new = jnp.where(causal, s_new, -jnp.inf)
    p_len = k_past.shape[1]
    probs = jax.nn.softmax(jnp.concatenate([s_past, s_new], axis=-1), axis=-1).astype(v_new.dtype)
    out = (jnp.einsum('bhqk,bkhd->bqhd', probs[..., :p_len], v_past)
           + jnp.einsum('bhqk,bkhd->bqhd', probs[..., p_len:], v_new))
    return out.reshape(bd, t, h * dh)

def run_trunk(h, p, conv_bufs, past, norm_g, w_in, w_conv, w_out, g_kv, w_k, w_v, w_f, b_f,
              w_q, w_o, w_gate, w_up, w_down, w_ple, w_ple_gate):
    b, t, _ = h.shape
    new_bufs = []
    kv_rows = None
    for i in range(DEPTH):
        xn = rmsnorm(h, norm_g[i, 0])
        if i < N_A_LAYERS:
            y, buf = short_conv(xn, w_in[i], w_conv[i], w_out[i], conv_bufs[i])
            new_bufs.append(buf)
        else:
            j = i - N_A_LAYERS
            if kv_rows is None:
                kv_rows = shared_kv(h, g_kv, w_k, w_v, w_f, b_f)
            q = (xn @ w_q[j]).reshape(b, t, N_HEADS, HEAD_DIM)
            if past is None:
                o = forgetting_attn_prompt(q, kv_rows[0], kv_rows[1], kv_rows[2])
            else:
                o = forgetting_attn_sample(q, past[0], past[1], past[2], kv_rows[0], kv_rows[1], kv_rows[2])
            y = o @ w_o[j]
        h = h + rmsnorm(y, norm_g[i, 1])
        h = h + rmsnorm(swiglu(rmsnorm(h, norm_g[i, 2]), w_gate[i], w_up[i], w_down[i]), norm_g[i, 3])
        h = h + jax.nn.sigmoid(h @ w_ple_gate[i]) * (p[i] @ w_ple[i])
    return h, jnp.stack(new_bufs, axis=0), kv_rows

def setup_inputs(seed: int = 0) -> dict:
    key = jax.random.key(seed)
    ks = jax.random.split(key, 28)
    n_pages = PAST_LEN // PAGE_SIZE
    n_used = DEC_BATCH * n_pages
    n_pool = n_used + n_used // 4

    def nrm(k, shape, scale):
        return jax.random.normal(k, shape, jnp.float32) * scale

    return {
        'x_prompt': nrm(ks[0], (BATCH, SEQ, D_MODEL), 1.0),
        'x_sample': nrm(ks[1], (DEC_BATCH, DEC_SEQ, D_MODEL), 1.0),
        'state_conv': nrm(ks[2], (N_A_LAYERS, DEC_BATCH, CONV_WIDTH - 1, D_MODEL), 1.0),
        'cache_k': nrm(ks[3], (n_pool, PAGE_SIZE, N_HEADS, HEAD_DIM), 1.0),
        'cache_v': nrm(ks[4], (n_pool, PAGE_SIZE, N_HEADS, HEAD_DIM), 1.0),
        'cache_logf': jax.nn.log_sigmoid(FORGET_BIAS_INIT + nrm(ks[5], (n_pool, PAGE_SIZE, N_HEADS), 1.0)),
        'page_table': jax.random.permutation(ks[6], n_pool)[:n_used].reshape(DEC_BATCH, n_pages).astype(jnp.int32),
        'p_prompt': nrm(ks[7], (DEPTH, BATCH, SEQ, PLE_DIM), 1.0),
        'p_sample': nrm(ks[8], (DEPTH, DEC_BATCH, DEC_SEQ, PLE_DIM), 1.0),
        'norm_g': 1.0 + nrm(ks[9], (DEPTH, 4, D_MODEL), 0.02),
        'w_in': nrm(ks[10], (N_A_LAYERS, D_MODEL, 3 * D_MODEL), D_MODEL ** -0.5),
        'w_conv': nrm(ks[11], (N_A_LAYERS, CONV_WIDTH, D_MODEL), CONV_WIDTH ** -0.5),
        'w_out': nrm(ks[12], (N_A_LAYERS, D_MODEL, D_MODEL), D_MODEL ** -0.5),
        'g_kv': 1.0 + nrm(ks[13], (D_MODEL,), 0.02),
        'w_k': nrm(ks[14], (D_MODEL, D_MODEL), D_MODEL ** -0.5),
        'w_v': nrm(ks[15], (D_MODEL, D_MODEL), D_MODEL ** -0.5),
        'w_f': nrm(ks[16], (D_MODEL, N_HEADS), D_MODEL ** -0.5),
        'b_f': FORGET_BIAS_INIT + nrm(ks[17], (N_HEADS,), 0.1),
        'w_q': nrm(ks[18], (N_B_LAYERS, D_MODEL, D_MODEL), D_MODEL ** -0.5),
        'w_o': nrm(ks[19], (N_B_LAYERS, D_MODEL, D_MODEL), D_MODEL ** -0.5),
        'w_gate': nrm(ks[20], (DEPTH, D_MODEL, D_FF), D_MODEL ** -0.5),
        'w_up': nrm(ks[21], (DEPTH, D_MODEL, D_FF), D_MODEL ** -0.5),
        'w_down': nrm(ks[22], (DEPTH, D_FF, D_MODEL), D_FF ** -0.5),
        'w_ple': nrm(ks[23], (DEPTH, PLE_DIM, D_MODEL), PLE_DIM ** -0.5),
        'w_ple_gate': nrm(ks[24], (DEPTH, D_MODEL, D_MODEL), D_MODEL ** -0.5),
    }

def reference(x_prompt, x_sample, state_conv, cache_k, cache_v, cache_logf, page_table, p_prompt, p_sample,
              norm_g, w_in, w_conv, w_out, g_kv, w_k, w_v, w_f, b_f, w_q, w_o,
              w_gate, w_up, w_down, w_ple, w_ple_gate):
    bd = x_sample.shape[0]
    n_pages = page_table.shape[1]
    conv_zero = jnp.zeros((N_A_LAYERS, x_prompt.shape[0], CONV_WIDTH - 1, D_MODEL), x_prompt.dtype)
    y_prompt, conv_prompt, kv_prompt = run_trunk(
        x_prompt, p_prompt, conv_zero, None, norm_g, w_in, w_conv, w_out, g_kv, w_k, w_v, w_f, b_f,
        w_q, w_o, w_gate, w_up, w_down, w_ple, w_ple_gate)
    k_past = cache_k[page_table].reshape(bd, n_pages * PAGE_SIZE, N_HEADS, HEAD_DIM)
    v_past = cache_v[page_table].reshape(bd, n_pages * PAGE_SIZE, N_HEADS, HEAD_DIM)
    logf_past = cache_logf[page_table].reshape(bd, n_pages * PAGE_SIZE, N_HEADS)
    y_sample, conv_sample, kv_sample = run_trunk(
        x_sample, p_sample, state_conv, (k_past, v_past, logf_past), norm_g, w_in, w_conv, w_out,
        g_kv, w_k, w_v, w_f, b_f, w_q, w_o, w_gate, w_up, w_down, w_ple, w_ple_gate)
    return (y_prompt, y_sample, conv_prompt, kv_prompt[0], kv_prompt[1], kv_prompt[2],
            conv_sample, kv_sample[0], kv_sample[1], kv_sample[2])


_drawn_inputs = setup_inputs


def setup_inputs(seed=0):
    import zlib

    import numpy as np

    out = dict(_drawn_inputs(seed))
    spreads = {}
    factors = {'g_kv': 2.74}
    for name, (base, spread) in spreads.items():
        noise = np.random.default_rng([zlib.crc32(name.encode()), seed]).standard_normal(out[name].shape)
        drawn = base * np.exp(spread * noise) if base else spread * noise
        out[name] = __import__('jax').numpy.asarray(drawn.astype(out[name].dtype))
    for name, factor in factors.items():
        out[name] = (out[name] * factor).astype(out[name].dtype)
    return out
```

```python
from contextlib import ExitStack

import concourse.bass as bass
from concourse import mybir

F32 = mybir.dt.float32
F32R = mybir.dt.float32r
I32 = mybir.dt.int32
ALU = mybir.AluOpType
ACT = mybir.ActivationFunctionType
AX_X = mybir.AxisListType.X
ds = bass.ds

P = 128
D = 1024
C = D // P
SEQ = 1024
NB, NQ = 8, 8
NS = NB * NQ
T = SEQ + NS
H, DH = 16, 64
D_FF = 2816
PLE = 256
PAGE, NPG, POOL = 128, 8, 80
EPS = 1e-6
SCALE = DH ** -0.5
MASKED = -1e30

TILES = [(0, 384), (384, 384), (768, T - 768)]
NT = len(TILES)
TOKB = [(128 * i, 128) for i in range(8)] + [(SEQ, NS)]
NTB = len(TOKB)
SQB = [[(0, 0), (128, 1), (256, 2)], [(384, 0), (512, 1), (640, 2)],
       [(768, 0), (896, 1), (T - 128, 2)]]

STAGES = [("in", 24, 24), ("out", 8, 8), ("ffn0", 66, 132), ("pp0", 2, 8), ("pg0", 8, 8),
          ("k", 8, 8), ("v", 8, 8), ("q", 8, 8), ("o", 8, 8), ("ffn1", 66, 132), ("pp1", 2, 8),
          ("pg1", 8, 8)]
SLAB0, BLK0 = {}, {}
_s = _b = 0
for _name, _ns, _nb in STAGES:
    SLAB0[_name], BLK0[_name] = _s, _b
    _s, _b = _s + _ns, _b + _nb
SLABS, BLKS = _s, _b
RAWS = 2
HLS = 2
ACCS = 2 * NT

PAIR = [("post", 0), ("post", 1), ("pre", 0), ("post", 2), ("pre", 1), ("pre", 2)]
PRE = [("pre", 0), ("pre", 1), ("pre", 2)]
POST = [("post", 0), ("post", 1), ("post", 2)]
STEP0 = {"n_in": 0, "n_mix": 3, "n_ffn0": 9, "n_kv": 12, "n_att": 15, "n_ffn1": 21}
XS0 = {"in": 0, "ffn0": 3, "pg0": 6, "kvq": 9, "o": 12, "ffn1": 15, "pg1": 18}
HR0 = {"n_mix": 0, "n_ffn0": 3, "n_att": 6, "n_ffn1": 9}
ROW_G, ROW_KV, ROW_CONV, ROW_STATE, NVEC = 0, 8, 9, 12, 28

REG = C * T * 4
B0 = 16640
A_H, A_XH, A_XL, A_Y, A_G = (B0 + i * REG for i in range(5))
A_RAW = B0 + 5 * REG
A_WH = A_RAW + RAWS * 4096
A_WL = A_WH + HLS * 4096
A_STG = A_WL + HLS * 4096
A_MISC = A_STG + 8192


def trunk(nc, ins, outs):
    (x_prompt, x_sample, state_conv, cache_k, cache_v, cache_logf, page_table, p_prompt, p_sample,
     norm_g, w_in, w_conv, w_out, g_kv, w_k, w_v, w_f, b_f, w_q, w_o, w_gate, w_up, w_down, w_ple,
     w_ple_gate) = ins
    (y_prompt, y_sample, conv_prompt, k_prompt, v_prompt, logf_prompt, conv_sample, k_sample,
     v_sample, logf_sample) = outs

    kT_dram = nc.dram_tensor("kT_scratch", [D, T], F32).ap()
    fsum_dram = nc.dram_tensor("fsum_scratch", [2, H, SEQ], F32).ap()

    def sb(name, shape, dt, off):
        return nc.alloc_sbuf_tensor_at(name, shape, dt, offset=off)

    h = sb("h", [P, C, T], F32, A_H)
    xs_hi = sb("xs_hi", [P, C, T], F32R, A_XH)
    xs_lo = sb("xs_lo", [P, C, T], F32R, A_XL)
    y_mix = sb("y_mix", [P, C, T], F32, A_XH)
    y = sb("y", [P, C, T], F32, A_Y)
    vT = sb("vT", [P, C, T], F32, A_G)
    raw = [sb(f"raw{i}", [P, 1024], F32, A_RAW + 4096 * i) for i in range(RAWS)]
    w_hi = [sb(f"w_hi{i}", [P, 1024], F32R, A_WH + 4096 * i) for i in range(HLS)]
    w_lo = [sb(f"w_lo{i}", [P, 1024], F32R, A_WL + 4096 * i) for i in range(HLS)]
    bgate = sb("bgate", [P, C, T], F32, A_Y)
    mix_hi = sb("mix_hi", [P, C, T], F32R, A_Y)
    zconv = sb("zconv", [P, C, T], F32, A_G)
    mix_lo = sb("mix_lo", [P, C, T], F32R, A_G)
    NPAD = SEQ + 2
    cup = sb("cup", [P, NPAD + NB * (NQ + 2)], F32, A_STG)
    cup_s = cup[:, NPAD:].rearrange("p (b t) -> p b t", b=NB)
    x_nat = sb("x_nat", [P, 8, D], F32, A_Y)
    xs_nat = sb("xs_nat", [NS, D], F32, A_STG)
    vec_nat = sb("vec_nat", [NVEC, D], F32, A_STG + 4096)
    sqb = [sb(f"sqb{i}", [P, C, P], F32, A_G + 4096 * i) for i in range(2)]
    xn = [sb(f"xn{i}", [P, C, 384], F32, A_G + 8192 + 12288 * i) for i in range(2)]
    p_nat = sb("p_nat", [P, NTB, PLE], F32, A_G + 8192)
    pT_hi = sb("pT_hi", [P, 2, T], F32R, A_G + 8192 + 9216)
    pT_lo = sb("pT_lo", [P, 2, T], F32R, A_G + 8192 + 9216 + 8704)
    hid_hi = [sb(f"hid_hi{i}", [P, 2, T], F32R, A_G + 17408 * i) for i in range(2)]
    hid_lo = [sb(f"hid_lo{i}", [P, 2, T], F32R, A_G + 17408 * i + 8704) for i in range(2)]
    act = sb("act", [P, T], F32, A_STG)
    rows_out = [sb(f"rows_out{i}", [P, D], F32, A_STG + 4096 * i) for i in range(2)]

    off = A_MISC
    def misc(name, shape, dt=F32):
        nonlocal off
        n = 4
        for s in shape[1:]:
            n *= s
        t = sb(name, shape, dt, off)
        off += (n + 31) // 32 * 32
        assert off <= 229344
        return t
    vecT = misc("vecT", [P, C, NVEC])
    ident = misc("ident", [P, P])
    ones = misc("ones", [P, 1])
    eps_c = misc("eps_c", [P, 1])
    stdc = misc("stdc", [P, 3])
    rcol = misc("rcol", [P, 3])
    convT = misc("convT", [P, C, 2 + 2 * NB])
    wf_raw = misc("wf_raw", [P, C, H])
    wf_hi = misc("wf_hi", [P, C, H], F32R)
    wf_lo = misc("wf_lo", [P, C, H], F32R)
    lfz = misc("lfz", [P, NTB, H])
    lf = misc("lf", [P, NTB, H])
    bf = misc("bf", [P, H])
    ptab = misc("ptab", [1, NB * NPG], I32)
    segm = misc("segm", [H, NS])
    one16 = misc("one16", [H, 1])
    conv_rows = sb("conv_rows", [2 + 2 * NB, D], F32, A_STG)

    kaug = [sb(f"kaug{i}", [66, SEQ], F32, A_XH + 4096 * i) for i in range(2)]
    qaug = [sb(f"qaug{i}", [66, SEQ], F32, A_XH + 8192 + 4096 * i) for i in range(2)]
    prob = [sb(f"prob{i}", [P, SEQ], F32, A_XH + 16384 + 4096 * i) for i in range(2)]
    probT = [sb(f"probT{i}", [P, 8, P], F32, A_XH + 24576 + 4096 * i) for i in range(2)]
    o_pair = sb("o_pair", [P, 8, P], F32, A_XH + 32768)
    lfT = sb("lfT", [H, T], F32, A_XH + 36864)
    fsum = sb("fsum", [H, T], F32, A_XH + 41216)
    nfsum = sb("nfsum", [H, T], F32, A_XH + 45568)
    causal = sb("causal", [P, P], F32, A_XH + 49920)
    nmx = sb("nmx", [P, 8], F32, A_XH + 50432)
    rsum = sb("rsum", [P, 8], F32, A_XH + 50464)
    rinv = sb("rinv", [P, 8], F32, A_XH + 50496)
    v_keys = sb("v_keys", [P, 8, D], F32, A_G)
    kpage = [sb(f"kpage{i}", [P, D], F32, A_XH + 4096 * i) for i in range(4)]
    kT = [sb(f"kT{i}", [P, C, 512], F32, A_XH + 16384 + 16384 * i) for i in range(2)]
    NK = NPG * PAGE
    sprob = sb("sprob", [P, NK + NS], F32, A_XH + 49152)
    sprobT = sb("sprobT", [P, NPG + 1, P], F32, A_XH + 53504)
    fb = sb("fb", [H, NK], F32, A_XH + 58112)
    lf_page = sb("lf_page", [P, NPG, H], F32, A_XH + 62208)
    v_new = sb("v_new", [NS, D], F32, A_XH + 62720)
    k_newT = sb("k_newT", [P, C, NS], F32, A_XH + 66816)
    sstat = sb("sstat", [P, 8], F32, A_XH + 68864)
    v_page = sb("v_page", [P, NPG, D], F32, A_G)
    qbd = sb("qbd", [P, C, P + 16], F32, A_STG)
    qbd_w = qbd[:, :, :].rearrange("p c n -> p (c n)")[:, 0:D].rearrange("p (c n) -> p c n", c=C)
    E_off = A_G + 32768
    expand = sb("expand", [H, P], F32, E_off)
    qsel = sb("qsel", [NQ, P], F32, E_off + 512)
    wmask = sb("wmask", [NQ, 120], F32, E_off + 1024)
    nfnew = sb("nfnew", [H, NS], F32, E_off + 1504)

    with ExitStack() as ctx:
        psum = ctx.enter_context(nc.psum_tensor("psum", [P, 8, 512], F32))

        def sem(name):
            return ctx.enter_context(nc.semaphore(name))

        def acc(b, t):
            return psum[:, 3 * (b % 2) + t, 0:TILES[t][1]]

        raw_landed = [sem(f"raw_landed{i}") for i in range(RAWS)]
        hi_ready = sem("hi_ready")
        lo_ready = sem("lo_ready")
        slab_used = sem("slab_used")
        acc_ready = sem("acc_ready")
        acc_free = sem("acc_free")
        consts = sem("consts")
        vec_landed = sem("vec_landed")
        x_landed = [sem(f"x_landed{i}") for i in range(NTB)]
        vec_tr, vec_done = sem("vec_tr"), sem("vec_done")
        tr_ready = sem("tr_ready")
        tr_act, tr_dve = sem("tr_act"), sem("tr_dve")
        rows_stored = [sem(f"rows_stored{i}") for i in range(2)]
        sq_ready, sq_used = sem("sq_ready"), sem("sq_used")
        std_ready, rcol_ready = sem("std_ready"), sem("rcol_ready")
        rb_ready, rb_used = sem("rb_ready"), sem("rb_used")
        h_ready = sem("h_ready")
        xs_hi_ready, xs_ready = sem("xs_hi_ready"), sem("xs_ready")
        conv_step = sem("conv_step")
        z_hi = sem("z_hi")
        mix_ready = sem("mix_ready")
        conv_tr, conv_rows_done, conv_stored = sem("conv_tr"), sem("conv_rows_done"), sem("conv_stored")
        y_zero = sem("y_zero")
        sig_ready = sem("sig_ready")
        act_ready, hid_hi_ready, hid_ready = sem("act_ready"), sem("hid_hi_ready"), sem("hid_ready")
        p_landed = sem("p_landed")
        p_tr, p_hi_ready, p_ready = sem("p_tr"), sem("p_hi_ready"), sem("p_ready")
        ple_mul, ple_sig = sem("ple_mul"), sem("ple_sig")
        ple_added = sem("ple_added")
        kT_stored = sem("kT_stored")
        wf_landed, wf_hi_s, wf_lo_s = sem("wf_landed"), sem("wf_hi_s"), sem("wf_lo_s")
        f_acc, f_z = sem("f_acc"), sem("f_z")
        f_act, f_step = sem("f_act"), sem("f_step")
        f_stored = sem("f_stored")
        f_tr = sem("f_tr")
        fs_stored = sem("fs_stored")
        v_back = sem("v_back")
        aug_one = sem("aug_one")
        aug_landed = [sem(f"aug_landed{i}") for i in range(2)]
        s_ready, s_max, exp_done = sem("s_ready"), sem("s_max"), sem("exp_done")
        pt_ready, pt_act, pt_dve = sem("pt_ready"), sem("pt_act"), sem("pt_dve")
        pv_done, rinv_s, o_taken = sem("pv_done"), sem("rinv_s"), sem("o_taken")
        tab_landed = sem("tab_landed")
        new_landed = sem("new_landed")
        kpage_landed = [sem(f"kpage_landed{i}") for i in range(4)]
        vpage_landed, lfpage_landed = sem("vpage_landed"), sem("lfpage_landed")
        qbd_zero, qbd_ready = sem("qbd_zero"), sem("qbd_ready")
        lfp_tr = sem("lfp_tr")
        fb_step, fb_ready = sem("fb_step"), sem("fb_ready")
        kt_ready, kt_act, kt_dve = sem("kt_ready"), sem("kt_act"), sem("kt_dve")
        ss_ready, ss_max, ss_exp = sem("ss_ready"), sem("ss_max"), sem("ss_exp")
        sp_step, sp_ready = sem("sp_step"), sem("sp_ready")
        spt_ready, spt_act, spt_dve = sem("spt_ready"), sem("spt_act"), sem("spt_dve")
        spv_done, so_taken = sem("spv_done"), sem("so_taken")
        oT_done = sem("oT_done")
        passed = sem("passed")
        block = ctx.enter_context(nc.Block())

        TR_X, TR_K, TR_V, TR_Y = 0, NTB, 2 * NTB, 3 * NTB
        ROWS0 = {TR_K: 0, TR_V: NTB, TR_Y: 2 * NTB}
        ITEMS = [(hh, qb) for hh in range(2) for qb in (7, 0, 6, 1, 5, 2, 4, 3)]
        NI, HP = len(ITEMS), H // 2
        OT_AT = 3

        def s_banks(j):
            return 4 if j % 2 else 2 * (j // 2 % 2)

        def s_view(j):
            nk = (ITEMS[j % NI][1] + 1) * P
            b = s_banks(j)
            return psum[:, b, 0:nk] if j % 2 else psum[:, b:b + 2, :].rearrange("p a b -> p (a b)")[:, 0:nk]

        def groups(j):
            g = 3 * (j // 2) + 2 * (j % 2)
            g += 2 if g >= OT_AT else 0
            nb = ITEMS[j][1] + 1
            return [(g + q, 4 * q, min(4, nb - 4 * q)) for q in range((nb + 3) // 4)]

        def gcount(hp, g):
            if isinstance(hp, int) and hp == 0:
                return g if g <= OT_AT else g - 2
            return hp * 26 + (g - 2)

        def ghalf(hp, g):
            if isinstance(hp, int) and hp == 0:
                return (g if g < OT_AT else g - 2) // 2
            return hp * 13 + (g // 2 - 1)

        CONV_STEPS = 14

        @block.sync
        def _(sp):
            def cols(w, c0, n=P, k=C):
                return w[:, ds(c0, n)].rearrange("(k p) n -> p k n", p=P)

            def load(n, slot, src, k, width):
                if isinstance(n, int) and n < RAWS:
                    pass
                else:
                    sp.wait_ge(lo_ready, n + 1)
                sp.dma_start(raw[slot][:, :].rearrange("p (k n) -> p k n", k=k), src)\
                    .then_inc(raw_landed[slot], 16)

            def plain(name, w, skip=0, take=C):
                for m in range(skip, take):
                    load(SLAB0[name] + m, m % 2, cols(w, m * P), C, P)

            w_in0 = w_in[0]
            for u, part in enumerate((0, 1, 2, 0, 1, 2)):
                load(u, u % 2, cols(w_in0, part * D + (u // 3) * P), C, P)
            with sp.Fori(1, C // 2) as i:
                for u, part in enumerate((0, 1, 2, 0, 1, 2)):
                    load(i * 6 + u, u % 2, cols(w_in0, i * (2 * P) + (part * D + (u // 3) * P)), C, P)
            plain("out", w_out[0])

            def ffn(name, layer):
                wg, wu, wd = w_gate[layer], w_up[layer], w_down[layer]

                def gate_up(g, n):
                    for u in range(4):
                        src = (wg, wu)[u % 2]
                        load(n + u, u % 2, cols(src, g * (2 * P) + (u // 2) * P), C, P)

                def down(g, n):
                    rows = wd[ds(g * (2 * P), 2 * P), :].rearrange("(k p) n -> p k n", p=P)
                    for u in range(2):
                        load(n + u, u % 2, rows[:, :, u * 512:(u + 1) * 512], 2, 512)

                n0 = SLAB0[name]
                gate_up(0, n0)
                with sp.Fori(0, 5) as i:
                    gate_up(i * 2 + 1, i * 12 + (n0 + 4))
                    down(i * 2, i * 12 + (n0 + 8))
                    gate_up(i * 2 + 2, i * 12 + (n0 + 10))
                    down(i * 2 + 1, i * 12 + (n0 + 14))
                down(10, n0 + 64)

            def ple(layer):
                rows = w_ple[layer].rearrange("(k p) n -> p k n", p=P)
                for u in range(2):
                    load(SLAB0[f"pp{layer}"] + u, u, rows[:, :, u * 512:(u + 1) * 512], 2, 512)
                plain(f"pg{layer}", w_ple_gate[layer])

            ffn("ffn0", 0)
            ple(0)
            plain("k", w_k)
            plain("v", w_v)
            plain("q", w_q[0])
            plain("o", w_o[0], 0, 3)

            sp.dma_start(ptab[:, :], page_table.rearrange("(o b) n -> o (b n)", o=1)).then_inc(tab_landed, 16)
            sp.wait_ge(tab_landed, 16)
            sp.wait_ge(pt_ready, 26 * HP)
            k_pages = cache_k.rearrange("n t h d -> n t (h d)")
            with sp.Fori(0, NB) as b:
                for pg in range(NPG):
                    sp.wait_ge(kt_ready, b * 16 + (2 * pg + 2))
                    page = sp.value_load(ptab[0:1, ds(b * NPG + pg, 1)], min_val=0, max_val=POOL - 1)
                    sp.dma_start(kpage[pg % 4][:, :], k_pages[ds(page, 1)].rearrange("o t d -> (o t) d"))\
                        .then_inc(kpage_landed[pg % 4], 16)
            plain("o", w_o[0], 3)
            ffn("ffn1", 1)
            ple(1)

        @block.gpsimd
        def _(pool):
            def mask(t, pattern, base, cm, op=ALU.is_ge, fill=MASKED):
                pool.affine_select(out=t, in_=t, compare_op=op, fill=fill, base=base, pattern=pattern,
                                   channel_multiplier=cm).then_inc(consts, 1)

            for tb, (t0, n) in enumerate(TOKB):
                dst = x_nat[:, tb, :] if tb < 8 else xs_nat[:, :]
                src = x_prompt[0, t0:t0 + n, :] if tb < 8 else x_sample.rearrange("b t d -> (b t) d")
                if tb == 3:
                    for r0, n_, s in ((ROW_G, 8, norm_g.rearrange("l k d -> (l k) d")),
                                      (ROW_KV, 1, g_kv.rearrange("(o d) -> o d", o=1)),
                                      (ROW_CONV, 3, w_conv[0]),
                                      (ROW_STATE, 16, state_conv[0].rearrange("b t d -> (b t) d"))):
                        pool.dma_start(vec_nat[r0:r0 + n_, :], s).then_inc(vec_landed, 16)
                pool.dma_start(dst, src).then_inc(x_landed[tb], 16)
                if tb == 0:
                    pool.memset(ident[:, :], 0.0).then_inc(consts, 1)
                    pool.memset(ones[:, :], 1.0).then_inc(consts, 1)
                    pool.memset(eps_c[:, :], EPS).then_inc(consts, 1)
                    pool.wait_ge(consts, 3)
                    mask(ident[:, :], [[-1, P]], 0, 1, ALU.not_equal, 1.0)
            pool.dma_start(wf_raw[:, :, :], w_f.rearrange("(k p) n -> p k n", p=P)).then_inc(wf_landed, 16)
            pool.dma_start(bf[:, :], b_f.rearrange("(o n) -> o n", o=1).broadcast_to([P, H])).then_inc(wf_landed, 16)

            pool.wait_ge(conv_rows_done, 2)
            pool.dma_start(conv_prompt[0, 0], conv_rows[0:2, :]).then_inc(conv_stored, 16)
            pool.dma_start(conv_sample[0].rearrange("b t d -> (b t) d"), conv_rows[2:2 + 2 * NB, :])\
                .then_inc(conv_stored, 16)

            def ffn(layer, y_free):
                pool.wait_ge(rb_used, y_free)
                pool.memset(y[:, :, :], 0.0).then_inc(y_zero, 1)
                pool.wait_ge(acc_ready, NT * BLK0[f"pp{layer}"])
                for tb, (t0, n) in enumerate(TOKB):
                    src = p_prompt[layer, 0, t0:t0 + n, :] if tb < 8 else \
                        p_sample[layer].rearrange("b t d -> (b t) d")
                    pool.dma_start(p_nat[0:n, tb, :], src).then_inc(p_landed, 16)

            ffn(0, 9)

            pool.wait_ge(f_step, 1)
            pool.dma_start(logf_prompt[0].rearrange("(b p) h -> p b h", p=P), lf[:, 0:8, :])\
                .then_inc(f_stored, 16)
            pool.dma_start(logf_sample.rearrange("b t h -> (b t) h"), lf[P - NS:P, 8, :]).then_inc(f_stored, 16)

            def store_rows(tr0, prompt, sample):
                for tb, (t0, n) in enumerate(TOKB):
                    pool.wait_ge(tr_act, tr0 + tb + 1)
                    pool.wait_ge(tr_dve, tr0 + tb + 1)
                    dst = prompt[t0:t0 + n, :] if tb < 8 else sample
                    r = ROWS0[tr0] + tb
                    pool.dma_start(dst, rows_out[r % 2][0:n, :]).then_inc(rows_stored[r % 2], 16)

            pool.wait_ge(acc_free, ACCS + NT * (BLK0["k"] + 8))
            pool.dma_start(kT_dram.rearrange("(c p) t -> p c t", p=P), y[:, :, :]).then_inc(kT_stored, 16)
            store_rows(TR_K, k_prompt[0].rearrange("t h d -> t (h d)"), k_sample.rearrange("b t h d -> (b t) (h d)"))
            store_rows(TR_V, v_prompt[0].rearrange("t h d -> t (h d)"), v_sample.rearrange("b t h d -> (b t) (h d)"))
            for r in range(2):
                pool.wait_ge(rows_stored[r], 16 * NTB)
            pool.dma_start(v_keys[:, :, :], v_prompt[0].rearrange("(b p) h d -> p b (h d)", p=P))\
                .then_inc(v_back, 16)
            pool.wait_ge(acc_free, ACCS + NT * (BLK0["q"] + 8))
            pool.memset(causal[:, :], 0.0).then_inc(consts, 1)
            pool.wait_ge(consts, 5)
            mask(causal[:, :], [[-1, P]], 0, 1)
            pool.wait_ge(consts, 6)
            for k, t in enumerate((*kaug, *qaug)):
                if k:
                    pool.wait_ge(aug_one, k)
                pool.memset(t[DH:DH + 2, :], 1.0).then_inc(aug_one, 1)
            pool.wait_ge(f_step, 6)
            pool.dma_start(fsum_dram[0], fsum[:, 0:SEQ]).then_inc(fs_stored, 16)
            pool.dma_start(fsum_dram[1], nfsum[:, 0:SEQ]).then_inc(fs_stored, 16)
            pool.wait_ge(fs_stored, 32)
            pool.wait_ge(kT_stored, 16)
            pool.wait_ge(aug_one, 4)

            def load_aug(hp, hh):
                rows = kT_dram[ds(hp * P + DH * hh, DH), 0:SEQ]
                pool.dma_start(kaug[hh][0:DH, :], rows).then_inc(aug_landed[hh], 16)
                pool.dma_start(kaug[hh][DH:DH + 1, :], fsum_dram[1, ds(hp * 2 + hh, 1), :])\
                    .then_inc(aug_landed[hh], 16)
                pool.dma_start(qaug[hh][0:DH, :], y[DH * hh:DH * hh + DH, ds(hp, 1), 0:SEQ]
                               .rearrange("p o t -> p (o t)")).then_inc(aug_landed[hh], 16)
                pool.dma_start(qaug[hh][DH + 1:DH + 2, :], fsum_dram[0, ds(hp * 2 + hh, 1), :])\
                    .then_inc(aug_landed[hh], 16)

            for hh in range(2):
                load_aug(0, hh)
            with pool.Fori(1, H // 2) as hp:
                for hh in range(2):
                    pool.wait_ge(s_ready, hp * 16 + (8 * hh - 8))
                    load_aug(hp, hh)

            pool.wait_ge(pv_done, 2 + 8 * H)
            pool.memset(expand[:, :], 0.0).then_inc(consts, 1)
            pool.memset(qsel[:, :], 0.0).then_inc(consts, 1)
            pool.memset(wmask[:, :], 0.0).then_inc(consts, 1)
            pool.wait_ge(consts, 9)
            mask(expand[:, :], [[1, H], [0, NQ]], 0, -1, ALU.not_equal, 1.0)
            mask(qsel[:, :], [[0, H], [1, NQ]], 0, -1, ALU.not_equal, 1.0)
            mask(wmask[:, :], [[1, 120]], -56, 0)
            pool.wait_ge(consts, 12)
            mask(wmask[:, :], [[-1, 120]], 56, 1)
            pool.memset(qbd[:, :, :], 0.0).then_inc(qbd_zero, 1)
            pool.wait_ge(pt_ready, 26 * HP)
            pool.dma_start(v_new[:, :], v_sample.rearrange("b t h d -> (b t) (h d)")).then_inc(new_landed, 16)
            pool.dma_start(k_newT[:, :, :], kT_dram[:, SEQ:T].rearrange("(c p) t -> p c t", p=P))\
                .then_inc(new_landed, 16)
            pool.wait_ge(tab_landed, 16)
            v_pages = cache_v.rearrange("n t h d -> n t (h d)")
            with pool.Fori(0, NB) as b:
                pool.wait_ge(lfp_tr, b * 2 + 1)
                pool.sem_inc(passed, 1)
                for pg in range(NPG):
                    page = pool.value_load(ptab[0:1, ds(b * NPG + pg, 1)], min_val=0, max_val=POOL - 1)
                    pool.dma_start(lf_page[:, pg, :], cache_logf[ds(page, 1)].rearrange("o t h -> (o t) h"))\
                        .then_inc(lfpage_landed, 16)
                pool.wait_ge(spv_done, b + 1)
                pool.sem_inc(passed, 1)
                for pg in range(NPG):
                    page = pool.value_load(ptab[0:1, ds(b * NPG + pg, 1)], min_val=0, max_val=POOL - 1)
                    pool.dma_start(v_page[:, pg, :], v_pages[ds(page, 1)].rearrange("o t d -> (o t) d"))\
                        .then_inc(vpage_landed, 16)

            ffn(1, 21)
            store_rows(TR_Y, y_prompt[0], y_sample.rearrange("b t d -> (b t) d"))
            pool.wait_ge(rows_stored[0], 16 * ((3 * NTB + 1) // 2))
            pool.wait_ge(rows_stored[1], 16 * (3 * NTB // 2))
            pool.wait_ge(conv_stored, 32)
            pool.wait_ge(f_stored, 32)

        @block.scalar
        def _(act_e):
            A = nc.scalar.activation

            def hi(n2, slot, gain=None):
                act_e.wait_ge(raw_landed[slot], n2 * 16 + 16)
                act_e.wait_ge(slab_used, n2 * 2 + (slot + 1))
                if gain is None:
                    A(w_hi[slot][:, :], raw[slot][:, :], ACT.Copy).then_inc(hi_ready, 1)
                else:
                    for c in range(C):
                        ins = A(w_hi[slot][:, c * P:(c + 1) * P], raw[slot][:, c * P:(c + 1) * P], ACT.Copy,
                                scale=vecT[:, c, gain:gain + 1])
                    ins.then_inc(hi_ready, 1)

            def hi_run(n, count, gain=None):
                for j in range(n, n + count):
                    hi(j // 2, j % 2, gain)

            def squares(s, src, t):
                for t0, j in SQB[t]:
                    q = 3 * s + j
                    act_e.wait_ge(sq_used, q + 1)
                    A(sqb[q % 2][:, :, :], src[:, :, t0:t0 + P], ACT.Square).then_inc(sq_ready, 1)
                act_e.wait_ge(sq_used, 2 + 3 * (s + 1))
                if s:
                    act_e.wait_ge(rcol_ready, s)
                A(stdc[:, :], psum[:, 6, 0:3], ACT.Sqrt, bias=eps_c[:, :], scale=1.0 / D)\
                    .then_inc(std_ready, 1)

            def norm(name, seq, src, post_wait, xs0, raw_split=False):
                s0, pending, n_post, n_pre = STEP0[name], None, 0, 0
                for k, (kind, t) in enumerate(seq):
                    s = s0 + k
                    if kind == "post":
                        if k == 0:
                            act_e.wait_ge(acc_free, post_wait)
                        squares(s, src, t)
                    else:
                        if name in HR0:
                            act_e.wait_ge(h_ready, HR0[name] + t + 1)
                        squares(s, h, t)
                    if pending is not None:
                        pending()
                        pending = None
                    t0, n = TILES[t]
                    if kind == "pre":
                        def pending(s=s, t=t, t0=t0, n=n):
                            act_e.wait_ge(rb_used, s + 1)
                            A(xs_hi[:, :, t0:t0 + n], xn[t % 2][:, :, 0:n], ACT.Copy).then_inc(xs_hi_ready, 1)
                    elif raw_split:
                        def pending(t=t, t0=t0, n=n):
                            act_e.wait_ge(h_ready, HR0[name] + t + 1)
                            A(xs_hi[:, :, t0:t0 + n], h[:, :, t0:t0 + n], ACT.Copy).then_inc(xs_hi_ready, 1)
                if pending is not None:
                    pending()


            def take_in():
                for tb, (t0, n) in enumerate(TOKB):
                    act_e.wait_ge(tr_ready, 2 * (TR_X + tb) + 1)
                    bank = 2 * (tb % 3)
                    A(h[:, 0:4, t0:t0 + n], psum[:, bank, :].rearrange("p (c t) -> p c t", c=4)[:, :, 0:n], ACT.Copy)\
                        .then_inc(tr_act, 1)

            def rows(tr0, r0):
                for tb, (t0, n) in enumerate(TOKB):
                    g, r = tr0 + tb, r0 + tb
                    act_e.wait_ge(tr_ready, 2 * g + 1)
                    if r >= 2:
                        act_e.wait_ge(rows_stored[r % 2], 16 * (r // 2))
                    A(rows_out[r % 2][0:n, 0:512], psum[0:n, 2 * (g % 3), :], ACT.Copy).then_inc(tr_act, 1)

            take_in()
            act_e.wait_ge(vec_tr, 1)
            A(vecT[:, :, :].rearrange("p c n -> p (c n)"), psum[:, 6, 0:C * NVEC], ACT.Copy).then_inc(vec_done, 1)
            act_e.wait_ge(tr_dve, NTB)
            hi_run(0, 1)
            norm("n_in", PRE, h, 0, XS0["in"])

            with act_e.Fori(0, C // 2) as i:
                for u in range(2):
                    for j in range(3):
                        nxt = 3 * u + j + 1
                        hi(i * 3 + nxt // 2, nxt % 2)
                    act_e.wait_ge(conv_step, i * (2 * CONV_STEPS) + (u + 1) * CONV_STEPS)
                    m = i * 2 + u
                    A(mix_hi[:, ds(m, 1), :], zconv[:, ds(m, 1), :], ACT.Copy).then_inc(z_hi, 1)
            for j in range(2):
                act_e.wait_ge(conv_tr, j + 1)
                A(conv_rows[:, 512 * j:512 * j + 512], psum[0:2 + 2 * NB, 6 + j, :], ACT.Copy)\
                    .then_inc(conv_rows_done, 1)
            hi_run(SLAB0["out"] + 1, 8)
            norm("n_mix", PAIR, y_mix, ACCS + NT * (BLK0["out"] + 8), XS0["ffn0"])

            def ffn(layer):
                name = f"ffn{layer}"
                n0, b0 = SLAB0[name] // 2, BLK0[name]
                hr0 = layer * 22 * NT

                def gate_up(slab2, blk, chunk):
                    for j in range(2):
                        hi(slab2 + (2 * j + 1) // 2, 1)
                        for t, (t0, n) in enumerate(TILES):
                            act_e.wait_ge(acc_ready, blk * NT + (2 * j * NT + t + 1))
                            act_e.wait_ge(hid_ready, chunk * NT + (j * NT + t + 1))
                            A(act[:, t0:t0 + n], acc(2 * j, t), ACT.Sigmoid).then_inc(sig_ready, 1)
                        hi(slab2 + (2 * j + 2) // 2, 0)
                        for t, (t0, n) in enumerate(TILES):
                            act_e.wait_ge(act_ready, chunk * NT + (j * NT + t + 1))
                            A(hid_hi[gate_up.par][:, j, t0:t0 + n], act[:, t0:t0 + n], ACT.Copy)\
                                .then_inc(hid_hi_ready, 1)

                def down(slab2):
                    hi(slab2, 1)
                    hi(slab2 + 1, 0)

                c0 = layer * 22
                gate_up.par = 0
                gate_up(n0, b0, c0)
                with act_e.Fori(0, 5) as i:
                    gate_up.par = 1
                    gate_up(i * 6 + (n0 + 2), i * 24 + (b0 + 4), i * 4 + (c0 + 2))
                    down(i * 6 + (n0 + 4))
                    gate_up.par = 0
                    gate_up(i * 6 + (n0 + 5), i * 24 + (b0 + 16), i * 4 + (c0 + 4))
                    down(i * 6 + (n0 + 7))
                down(n0 + 32)

            def ple(layer):
                for tb, (t0, n) in enumerate(TOKB):
                    q = layer * NTB + tb
                    act_e.wait_ge(p_tr, q + 1)
                    A(pT_hi[:, :, t0:t0 + n], psum[:, tb % 6, 0:2 * P].rearrange("p (c t) -> p c t", c=2)[:, :, 0:n],
                      ACT.Copy).then_inc(p_hi_ready, 1)
                norm(f"n_ffn{layer}", POST, y, ACCS + NT * BLK0[f"pp{layer}"], XS0[f"pg{layer}"], raw_split=True)
                hi_run(SLAB0[f"pp{layer}"] + 1, 2)
                n0, b0 = SLAB0[f"pg{layer}"], BLK0[f"pg{layer}"]
                for m in range(C):
                    if n0 + m + 1 < SLABS:
                        nxt = n0 + m + 1
                        hi(nxt // 2, nxt % 2, ROW_KV if nxt == SLAB0["k"] else None)
                    for t, (t0, n) in enumerate(TILES):
                        q = (layer * C + m) * NT + t
                        act_e.wait_ge(acc_ready, NT * (b0 + m) + t + 1)
                        act_e.wait_ge(ple_mul, q + 1)
                        A(act[:, t0:t0 + n], acc(b0 + m, t), ACT.Sigmoid).then_inc(ple_sig, 1)

            act_e.wait_ge(conv_stored, 32)
            ffn(0)
            ple(0)

            act_e.wait_ge(ple_added, C * NT)
            norm("n_kv", PRE, h, 0, XS0["kvq"])
            act_e.wait_ge(wf_landed, 32)
            for c in range(C):
                ins = A(wf_hi[:, c, :], wf_raw[:, c, :], ACT.Copy, scale=vecT[:, c, ROW_KV:ROW_KV + 1])
            ins.then_inc(wf_hi_s, 1)
            hi_run(SLAB0["k"] + 1, 15, ROW_KV)
            hi_run(SLAB0["q"], 1, ROW_G + 4)
            act_e.wait_ge(f_z, 1)
            A(lf[:, :, :], lfz[:, :, :], ACT.Abs).then_inc(f_act, 1)
            act_e.wait_ge(f_act, 1)
            A(lf[:, :, :], lf[:, :, :], ACT.Exp, scale=-1.0).then_inc(f_act, 1)
            act_e.wait_ge(f_act, 2)
            A(lf[:, :, :], lf[:, :, :], ACT.Ln, bias=ones[:, :]).then_inc(f_act, 1)
            rows(TR_K, ROWS0[TR_K])
            rows(TR_V, ROWS0[TR_V])
            hi_run(SLAB0["q"] + 1, 7, ROW_G + 4)
            hi_run(SLAB0["o"], 1)
            act_e.wait_ge(acc_free, ACCS + NT * (BLK0["q"] + 8))
            for j, (c0, n, bank) in enumerate(((0, 512, 6), (512, 512, 7), (SEQ, NS, 0))):
                act_e.wait_ge(f_tr, j + 1)
                A(lfT[:, c0:c0 + n], psum[0:H, bank, (0 if j < 2 else P - NS):(n if j < 2 else P)], ACT.Copy)\
                    .then_inc(f_act, 1)

            act_e.sem_inc(exp_done, 4)
            act_e.sem_inc(pt_act, 1)

            def exps(hp, j):
                act_e.wait_ge(s_max, hp * NI + (j + 1))
                jj = j % NI
                if j >= 2:
                    act_e.wait_ge(pt_ready, gcount(hp, groups(j - 2)[-1][0] + 1))
                elif not (isinstance(hp, int) and hp == 0):
                    act_e.wait_ge(pt_ready, hp * 26 + (j - 3))
                A(prob[j % 2][:, 0:(ITEMS[jj][1] + 1) * P], s_view(j), ACT.Exp, bias=nmx[:, j % 4:j % 4 + 1],
                  accum_out=rsum[:, j % 4:j % 4 + 1]).then_inc(exp_done, 1)

            def take_probT(hp, j):
                for g, kb, nb in groups(j):
                    if g % 2 == 0:
                        act_e.wait_ge(pt_ready, gcount(hp, g + 1))
                        act_e.wait_ge(pv_done, hp * NI + (j + 1))
                        A(probT[j % 2][:, kb:kb + nb, :], psum[:, 5, 0:nb * P].rearrange("p (c t) -> p c t", c=nb),
                          ACT.Copy).then_inc(pt_act, 1)

            def take_o(hp, g_ready):
                act_e.wait_ge(pt_ready, g_ready)
                A(y[:, ds(hp, 1), 512:SEQ].rearrange("p o t -> p (o t)"), psum[:, 5, :], ACT.Copy).then_inc(pt_act, 1)

            def pair(hp, first, last):
                for j in range(NI):
                    if not (last and j == NI - 1):
                        exps(hp, j + 1)
                    take_probT(hp, j)
                    if j == 1 and not first:
                        take_o(hp - 1, gcount(hp, OT_AT + 2))

            exps(0, 0)
            pair(0, True, False)
            with act_e.Fori(1, HP - 1) as hp:
                pair(hp, False, False)
            pair(HP - 1, False, True)
            take_o(HP - 1, 26 * HP)

            act_e.sem_inc(kt_act, 1)
            act_e.sem_inc(spt_act, 1)
            with act_e.Fori(0, NB) as b:
                for pg in range(NPG):
                    act_e.wait_ge(kt_ready, b * 16 + (8 + 2 * pg + 1))
                    act_e.wait_ge(ss_ready, b * 2 + 2)
                    A(kT[pg // 4][:, 0:4, (pg % 4) * P:(pg % 4 + 1) * P],
                      psum[:, 4, :].rearrange("p (c t) -> p c t", c=4), ACT.Copy).then_inc(kt_act, 1)
                act_e.wait_ge(ss_max, b + 1)
                act_e.wait_ge(spv_done, b + 1)
                A(sprob[:, 0:NK], psum[:, 0:2, :].rearrange("p a b -> p (a b)"), ACT.Exp,
                  bias=sstat[:, 2:3], accum_out=sstat[:, 3:4]).then_inc(ss_exp, 1)
                A(sprob[:, NK:NK + NS], psum[:, 2, 0:NS], ACT.Exp,
                  bias=sstat[:, 2:3], accum_out=sstat[:, 4:5]).then_inc(ss_exp, 1)
                for g in (0, 2):
                    act_e.wait_ge(spt_ready, b * 3 + (g + 1))
                    nb = 4 if g == 0 else 1
                    if g == 0:
                        A(sprobT[:, 0:4, :], psum[:, 4, :].rearrange("p (c t) -> p c t", c=4), ACT.Copy)\
                            .then_inc(spt_act, 1)
                    else:
                        A(sprobT[0:NS, 8, :], psum[0:NS, 4, 0:P], ACT.Copy).then_inc(spt_act, 1)

            act_e.wait_ge(so_taken, 2 + 2 * NB - 1)
            for t, (t0, n) in enumerate(TILES):
                A(xs_hi[:, :, t0:t0 + n], y[:, :, t0:t0 + n], ACT.Copy).then_inc(xs_hi_ready, 1)
            hi_run(SLAB0["o"] + 1, 8)
            norm("n_att", PAIR, y, ACCS + NT * (BLK0["o"] + 8), XS0["ffn1"])
            ffn(1)
            ple(1)
            act_e.wait_ge(ple_added, 2 * C * NT)
            rows(TR_Y, ROWS0[TR_Y])

        @block.vector
        def _(dve):
            V = nc.vector

            def copy(out, in_):
                return V.tensor_scalar(out, in_, 1.0, None, ALU.mult)

            def lo(n2, slot, gain=None):
                dve.wait_ge(hi_ready, n2 * 2 + (slot + 1))
                if gain is None:
                    V.tensor_tensor(w_lo[slot][:, :], raw[slot][:, :], w_hi[slot][:, :].bitcast(F32), ALU.subtract)\
                        .then_inc(lo_ready, 1)
                else:
                    for c in range(C):
                        part = slice(c * P, (c + 1) * P)
                        ins = V.scalar_tensor_tensor(w_lo[slot][:, part], raw[slot][:, part],
                                                     vecT[:, c, gain:gain + 1], w_hi[slot][:, part].bitcast(F32),
                                                     ALU.mult, ALU.subtract)
                    ins.then_inc(lo_ready, 1)

            def lo_run(n, count, gain=None):
                for j in range(n, n + count):
                    lo(j // 2, j % 2, gain)

            def tile_ready(blk, t, last=False):
                dve.wait_ge(acc_ready, blk * NT + (t + 1))
                if last:
                    dve.sem_inc(slab_used, 1)

            def norm(name, seq, ysrc, post_row, pre_row, xs0, raw_split=False):
                s0, pending = STEP0[name], None
                for k, (kind, t) in enumerate(seq):
                    s = s0 + k
                    t0, n = TILES[t]
                    dve.wait_ge(std_ready, s + 1)
                    V.reciprocal(rcol[:, :], stdc[:, :]).then_inc(rcol_ready, 1)
                    if kind == "pre" and t == 2:
                        dve.wait_ge(xs_ready, xs0 + 1)
                    dve.wait_ge(rb_ready, s + 1)
                    rb = psum[:, 7, 0:n]
                    for c in range(C):
                        if kind == "post":
                            ins = V.scalar_tensor_tensor(ysrc[:, c, t0:t0 + n], ysrc[:, c, t0:t0 + n],
                                                         vecT[:, c, post_row:post_row + 1], rb, ALU.mult, ALU.mult)
                        elif pre_row is not None:
                            ins = V.scalar_tensor_tensor(xn[t % 2][:, c, 0:n], h[:, c, t0:t0 + n],
                                                         vecT[:, c, pre_row:pre_row + 1], rb, ALU.mult, ALU.mult)
                        else:
                            ins = V.tensor_tensor(xn[t % 2][:, c, 0:n], h[:, c, t0:t0 + n], rb, ALU.mult)
                    ins.then_inc(rb_used, 1)
                    if kind == "post":
                        dve.wait_ge(rb_used, s + 1)
                        V.tensor_tensor(h[:, :, t0:t0 + n], h[:, :, t0:t0 + n], ysrc[:, :, t0:t0 + n], ALU.add)\
                            .then_inc(h_ready, 1)
                    if pending is not None:
                        pending()
                        pending = None
                    if kind == "pre" or raw_split:
                        src = xn[t % 2][:, :, 0:n] if kind == "pre" else h[:, :, t0:t0 + n]

                        def pending(t=t, t0=t0, n=n, src=src):
                            dve.wait_ge(xs_hi_ready, xs0 + t + 1)
                            V.tensor_tensor(xs_lo[:, :, t0:t0 + n], src, xs_hi[:, :, t0:t0 + n].bitcast(F32),
                                            ALU.subtract).then_inc(xs_ready, 1)
                if pending is not None:
                    pending()

            dve.sem_inc(acc_free, ACCS)
            dve.sem_inc(lo_ready, RAWS)
            dve.sem_inc(slab_used, HLS)
            dve.sem_inc(hid_ready, NT)
            dve.sem_inc(ple_mul, NT)
            for tb, (t0, n) in enumerate(TOKB):
                dve.wait_ge(tr_ready, 2 * (TR_X + tb) + 2)
                bank = 2 * (tb % 3) + 1
                V.tensor_copy(h[:, 4:8, t0:t0 + n], psum[:, bank, :].rearrange("p (c t) -> p c t", c=4)[:, :, 0:n])\
                    .then_inc(tr_dve, 1)

            def rows(tr0, r0):
                for tb, (t0, n) in enumerate(TOKB):
                    g, r = tr0 + tb, r0 + tb
                    dve.wait_ge(tr_ready, 2 * g + 2)
                    if r >= 2:
                        dve.wait_ge(rows_stored[r % 2], 16 * (r // 2))
                    V.tensor_copy(rows_out[r % 2][0:n, 512:D], psum[0:n, 2 * (g % 3) + 1, :]).then_inc(tr_dve, 1)

            dve.wait_ge(vec_done, 1)
            lo_run(0, 1)
            dve.wait_ge(tr_act, NTB)
            dve.wait_ge(tr_dve, NTB)
            norm("n_in", PRE, None, None, ROW_G + 0, XS0["in"])

            V.memset(cup[:, 0:2], 0.0).then_inc(conv_step, 1)
            with dve.Fori(0, C // 2) as i:
                for u in range(2):
                    m = i * 2 + u
                    mm = ds(m, 1)
                    base = i * (2 * CONV_STEPS) + u * CONV_STEPS + 1
                    done = [0]

                    def step(ins):
                        ins.then_inc(conv_step, 1)
                        done[0] += 1

                    def after(k):
                        dve.wait_ge(conv_step, base + k)

                    def f(t):
                        return t.rearrange("p o t -> p (o t)")

                    blk = i * 6 + 3 * u
                    for part, dst in enumerate((bgate, zconv)):
                        nxt = 3 * u + part + 1
                        lo(i * 3 + nxt // 2, nxt % 2)
                        for t, (t0, n) in enumerate(TILES):
                            tile_ready(blk + part, t, t == NT - 1)
                            copy(f(dst[:, mm, t0:t0 + n]), acc(3 * u + part, t)).then_inc(acc_free, 1)
                    nxt = 3 * u + 3
                    lo(i * 3 + nxt // 2, nxt % 2)
                    dve.wait_ge(conv_step, base)
                    dve.wait_ge(acc_free, blk * NT + (ACCS + 2 * NT))
                    for t, (t0, n) in enumerate(TILES):
                        tile_ready(blk + 2, t, t == NT - 1)
                        np_ = min(t0 + n, SEQ) - t0
                        ins = V.tensor_tensor(cup[:, 2 + t0:2 + t0 + np_], f(zconv[:, mm, t0:t0 + np_]),
                                              acc(3 * u + 2, t)[:, 0:np_], ALU.mult)
                        if np_ < n:
                            step(ins)
                            ins = V.tensor_tensor(cup_s[:, :, 2:], f(zconv[:, mm, SEQ:T]).rearrange("p (b t) -> p b t", b=NB),
                                                  acc(3 * u + 2, t)[:, np_:n].rearrange("p (b t) -> p b t", b=NB), ALU.mult)
                        ins.then_inc(acc_free, 1)
                    step(copy(cup_s[:, :, 0:2], f(vecT[:, mm, ROW_STATE:ROW_STATE + 2 * NB])
                                       .rearrange("p (b t) -> p b t", b=NB)))
                    after(2)
                    dve.wait_ge(acc_free, blk * NT + (ACCS + 3 * NT))
                    step(copy(f(convT[:, mm, 0:2]), cup[:, SEQ:SEQ + 2]))
                    step(copy(f(convT[:, mm, 2:]).rearrange("p (b t) -> p b t", b=NB),
                                       cup_s[:, :, NQ:NQ + 2]))
                    zp = f(zconv[:, mm, 0:SEQ])
                    zs = f(zconv[:, mm, SEQ:T]).rearrange("p (b t) -> p b t", b=NB)
                    for k in range(3):
                        wk = vecT[:, mm, ROW_CONV + k:ROW_CONV + k + 1].rearrange("p a b -> p (a b)")
                        if k == 0:
                            step(V.tensor_scalar(zp, cup[:, 0:SEQ], wk, None, ALU.mult))
                            step(V.tensor_scalar(zs, cup_s[:, :, 0:NQ], wk, None, ALU.mult))
                        else:
                            after(4 + 2 * k)
                            step(V.scalar_tensor_tensor(zp, cup[:, k:k + SEQ], wk, zp, ALU.mult, ALU.add))
                            step(V.scalar_tensor_tensor(zs, cup_s[:, :, k:k + NQ], wk, zs, ALU.mult, ALU.add))
                    after(10)
                    step(V.tensor_tensor(f(zconv[:, mm, 0:544]), f(zconv[:, mm, 0:544]), f(bgate[:, mm, 0:544]), ALU.mult))
                    step(V.tensor_tensor(f(zconv[:, mm, 544:T]), f(zconv[:, mm, 544:T]), f(bgate[:, mm, 544:T]), ALU.mult))
                    assert done[0] == 12
                    dve.sem_inc(conv_step, CONV_STEPS - 12 - 1) if CONV_STEPS > 13 else None
                    after(CONV_STEPS - 1)
                    dve.sem_inc(conv_step, 1)
                    dve.wait_ge(z_hi, i * 2 + (u + 1))
                    V.tensor_tensor(f(mix_lo[:, mm, :]), f(zconv[:, mm, :]), f(mix_hi[:, mm, :]).bitcast(F32), ALU.subtract)\
                        .then_inc(mix_ready, 1)

            def plain(name, dst, gain_next, last_gain=None, scale=None, last=True, gain=None):
                n0, b0 = SLAB0[name], BLK0[name]
                for m in range(C):
                    if m < C - 1:
                        lo_run(n0 + m + 1, 1, gain)
                    elif gain_next != "none":
                        lo_run(n0 + m + 1, 1, gain_next)
                    for t, (t0, n) in enumerate(TILES):
                        tile_ready(b0 + m, t, t == NT - 1)
                        if scale is None:
                            V.tensor_copy(dst[:, m, t0:t0 + n], acc(b0 + m, t)).then_inc(acc_free, 1)
                        else:
                            V.tensor_scalar(dst[:, m, t0:t0 + n], acc(b0 + m, t), scale, None, ALU.mult)\
                                .then_inc(acc_free, 1)

            plain("out", y_mix, None)
            dve.wait_ge(acc_free, ACCS + NT * (BLK0["out"] + 8))
            norm("n_mix", PAIR, y_mix, ROW_G + 1, ROW_G + 2, XS0["ffn0"])

            def ffn(layer):
                name = f"ffn{layer}"
                n0, b0, c0 = SLAB0[name] // 2, BLK0[name], layer * 22

                def gate_up(slab2, blk, chunk, par):
                    for j in range(2):
                        lo(slab2 + (2 * j + 1) // 2, 1)
                        for t, (t0, n) in enumerate(TILES):
                            tile_ready(blk + 2 * j, t, t == NT - 1)
                            dve.wait_ge(sig_ready, chunk * NT + (j * NT + t + 1))
                            V.tensor_tensor(act[:, t0:t0 + n], act[:, t0:t0 + n], acc(2 * j, t), ALU.mult)\
                                .then_inc(acc_free, 1)
                        lo(slab2 + (2 * j + 2) // 2, 0)
                        dve.wait_ge(acc_free, blk * NT + (ACCS + (2 * j + 1) * NT))
                        for t in range(NT + 1):
                            if t < NT:
                                t0, n = TILES[t]
                                tile_ready(blk + 2 * j + 1, t, t == NT - 1)
                                V.tensor_tensor(act[:, t0:t0 + n], act[:, t0:t0 + n], acc(2 * j + 1, t), ALU.mult)\
                                    .then_inc(act_ready, 1)
                                dve.wait_ge(act_ready, chunk * NT + (j * NT + t + 1))
                                dve.sem_inc(acc_free, 1)
                            if t > 0:
                                t0, n = TILES[t - 1]
                                dve.wait_ge(hid_hi_ready, chunk * NT + (j * NT + t))
                                V.tensor_tensor(hid_lo[par][:, j, t0:t0 + n], act[:, t0:t0 + n],
                                                hid_hi[par][:, j, t0:t0 + n].bitcast(F32), ALU.subtract)\
                                    .then_inc(hid_ready, 1)

                def down(slab2, blk, gain=None, split_next=True):
                    for s in range(2):
                        if s == 0:
                            lo(slab2, 1)
                        elif split_next:
                            lo(slab2 + 1, 0, gain)
                        if s == 0:
                            dve.wait_ge(acc_free, blk * NT + ACCS)
                        for m in range(4):
                            for t, (t0, n) in enumerate(TILES):
                                tile_ready(blk + 4 * s + m, t, m == 3 and t == NT - 1)
                                yy = y[:, 4 * s + m, t0:t0 + n]
                                V.tensor_tensor(yy, yy, acc(m, t), ALU.add).then_inc(acc_free, 1)

                gate_up(n0, b0, c0, 0)
                dve.wait_ge(y_zero, layer + 1)
                with dve.Fori(0, 5) as i:
                    gate_up(i * 6 + (n0 + 2), i * 24 + (b0 + 4), i * 4 + (c0 + 2), 1)
                    down(i * 6 + (n0 + 4), i * 24 + (b0 + 8))
                    gate_up(i * 6 + (n0 + 5), i * 24 + (b0 + 16), i * 4 + (c0 + 4), 0)
                    down(i * 6 + (n0 + 7), i * 24 + (b0 + 20))
                down(n0 + 32, b0 + 124)

            def ple(layer):
                for tb, (t0, n) in enumerate(TOKB):
                    dve.wait_ge(p_hi_ready, layer * NTB + tb + 1)
                    V.tensor_tensor(pT_lo[:, :, t0:t0 + n],
                                    psum[:, tb % 6, 0:2 * P].rearrange("p (c t) -> p c t", c=2)[:, :, 0:n],
                                    pT_hi[:, :, t0:t0 + n].bitcast(F32), ALU.subtract).then_inc(p_ready, 1)
                dve.wait_ge(acc_free, ACCS + NT * BLK0[f"pp{layer}"])
                norm(f"n_ffn{layer}", POST, y, ROW_G + 4 * layer + 3, None, XS0[f"pg{layer}"], raw_split=True)
                n0, b0 = SLAB0[f"pp{layer}"], BLK0[f"pp{layer}"]
                for m in range(C):
                    if m % 4 == 0:
                        lo_run(n0 + m // 4 + 1, 1)
                    for t, (t0, n) in enumerate(TILES):
                        tile_ready(b0 + m, t, m % 4 == 3 and t == NT - 1)
                        V.tensor_copy(y[:, m, t0:t0 + n], acc(m, t)).then_inc(acc_free, 1)
                dve.wait_ge(acc_free, ACCS + NT * (b0 + C))
                n0, b0 = SLAB0[f"pg{layer}"], BLK0[f"pg{layer}"]
                for m in range(C):
                    if n0 + m + 1 < SLABS:
                        lo_run(n0 + m + 1, 1, ROW_KV if n0 + m + 1 == SLAB0["k"] else None)
                    for t, (t0, n) in enumerate(TILES):
                        q = (layer * C + m) * NT + t
                        tile_ready(b0 + m, t, t == NT - 1)
                        dve.wait_ge(ple_sig, q + 1)
                        dve.sem_inc(acc_free, 1)
                        V.tensor_tensor(y[:, m, t0:t0 + n], act[:, t0:t0 + n], y[:, m, t0:t0 + n], ALU.mult)\
                            .then_inc(ple_mul, 1)
                        dve.wait_ge(ple_mul, NT + q + 1)
                        V.tensor_tensor(h[:, m, t0:t0 + n], h[:, m, t0:t0 + n], y[:, m, t0:t0 + n], ALU.add)\
                            .then_inc(ple_added, 1)

            ffn(0)
            ple(0)
            dve.wait_ge(ple_added, C * NT)
            norm("n_kv", PRE, None, None, None, XS0["kvq"])
            dve.wait_ge(wf_hi_s, 1)
            for c in range(C):
                ins = V.scalar_tensor_tensor(wf_lo[:, c, :], wf_raw[:, c, :], vecT[:, c, ROW_KV:ROW_KV + 1],
                                             wf_hi[:, c, :].bitcast(F32), ALU.mult, ALU.subtract)
            ins.then_inc(wf_lo_s, 1)
            plain("k", y, ROW_KV, gain=ROW_KV)
            plain("v", vT, ROW_G + 4, gain=ROW_KV)
            dve.wait_ge(f_acc, 1)
            V.tensor_tensor(lfz[:, :, :], psum[:, 6, 0:NTB * H].rearrange("p (b n) -> p b n", b=NTB),
                            bf[:, :].unsqueeze(1).broadcast_to([P, NTB, H]), ALU.add).then_inc(f_z, 1)
            dve.wait_ge(f_act, 3)
            V.scalar_tensor_tensor(lf[:, :, :], lfz[:, :, :], 0.0, lf[:, :, :], ALU.min, ALU.subtract)\
                .then_inc(f_step, 1)
            rows(TR_K, ROWS0[TR_K])
            rows(TR_V, ROWS0[TR_V])
            dve.wait_ge(kT_stored, 16)
            plain("q", y, None, scale=SCALE, gain=ROW_G + 4)
            V.memset(segm[:, :], 1.0).then_inc(f_step, 1)
            V.memset(one16[:, :], 1.0).then_inc(f_step, 1)
            dve.wait_ge(f_step, 3)
            V.memset(segm[:, :].rearrange("p (b t) -> p b t", b=NB)[:, :, 0:1], 0.0).then_inc(f_step, 1)
            dve.wait_ge(f_act, 6)
            dve.wait_ge(f_step, 4)
            V.tensor_tensor_scan(fsum[:, 0:SEQ], one16[:, :].broadcast_to([H, SEQ]), lfT[:, 0:SEQ], 0.0,
                                 ALU.mult, ALU.add).then_inc(f_step, 1)
            dve.wait_ge(f_step, 5)
            V.tensor_scalar(nfsum[:, 0:SEQ], fsum[:, 0:SEQ], -1.0, None, ALU.mult).then_inc(f_step, 1)
            V.tensor_tensor_scan(fsum[:, SEQ:T], segm[:, :], lfT[:, SEQ:T], 0.0, ALU.mult, ALU.add)\
                .then_inc(f_step, 1)
            dve.wait_ge(v_back, 16)
            dve.wait_ge(f_step, 7)
            V.tensor_scalar(nfnew[:, :], fsum[:, SEQ:T], -1.0, None, ALU.mult).then_inc(f_step, 1)

            dve.sem_inc(pt_dve, 1)
            dve.sem_inc(o_taken, 1)

            def maxes(hp, j):
                dve.wait_ge(s_ready, hp * NI + (j + 1))
                V.reduce_max(nmx[:, j % 4:j % 4 + 1], s_view(j), AX_X, negate=True).then_inc(s_max, 1)

            def take_probT(hp, j):
                for g, kb, nb in groups(j):
                    if g % 2:
                        dve.wait_ge(pt_ready, gcount(hp, g + 1))
                        dve.wait_ge(pv_done, hp * NI + (j + 1))
                        V.tensor_copy(probT[j % 2][:, kb:kb + nb, :],
                                      psum[:, 6, 0:nb * P].rearrange("p (c t) -> p c t", c=nb)).then_inc(pt_dve, 1)

            def normed(hp, j):
                it = hp * NI
                hh, qb = ITEMS[j]
                dve.wait_ge(exp_done, it + (j + 5))
                V.reciprocal(rinv[:, j % 2:j % 2 + 1], rsum[:, j % 4:j % 4 + 1]).then_inc(rinv_s, 1)
                dve.wait_ge(rinv_s, it + (j + 1))
                dve.wait_ge(pv_done, it + (j + 3))
                V.tensor_scalar(o_pair[:, qb, DH * hh:DH * hh + DH], psum[:, 7, 0:DH], rinv[:, j % 2:j % 2 + 1],
                                None, ALU.mult).then_inc(o_taken, 1)

            def take_o(hp, g_ready):
                dve.wait_ge(pt_ready, g_ready)
                V.tensor_scalar(y[:, ds(hp, 1), 0:512].rearrange("p o t -> p (o t)"), psum[:, 6, :], 1.0, None,
                                ALU.mult).then_inc(pt_dve, 1)

            def pair(hp, first, last):
                for j in range(NI):
                    if not (last and j >= NI - 2):
                        maxes(hp, j + 2)
                    take_probT(hp, j)
                    if j == 1 and not first:
                        take_o(hp - 1, gcount(hp, OT_AT + 1))
                        dve.wait_ge(pt_ready, gcount(hp, OT_AT + 2))
                    if j > 0:
                        normed(hp, j - 1)
                    elif not first:
                        normed(hp - 1, NI - 1)

            maxes(0, 0)
            maxes(0, 1)
            pair(0, True, False)
            with dve.Fori(1, HP - 1) as hp:
                pair(hp, False, False)
            pair(HP - 1, False, True)
            normed(HP - 1, NI - 1)
            take_o(HP - 1, 26 * HP - 1)

            dve.sem_inc(kt_dve, 1)
            dve.sem_inc(spt_dve, 1)
            dve.sem_inc(fb_ready, 1)
            dve.sem_inc(so_taken, 1)
            dve.wait_ge(qbd_zero, 1)
            dve.wait_ge(pt_act, 1 + 13 * HP)
            with dve.Fori(0, NB) as b:
                cols = ds(b * NQ + SEQ, NQ)
                dve.wait_ge(ss_ready, b * 2 + 2)
                copy(qbd[0:DH, :, 0:NQ], y[0:DH, :, cols]).then_inc(sp_step, 1)
                copy(qbd[DH:P, :, NQ:2 * NQ], y[DH:P, :, cols]).then_inc(qbd_ready, 1)
                dve.wait_ge(lfp_tr, b * 2 + 3)
                V.tensor_tensor_scan(fb[:, :], one16[:, :].broadcast_to([H, NK]),
                                     psum[0:H, 6:8, :].rearrange("p a b -> p (a b)"), 0.0,
                                     ALU.mult, ALU.add).then_inc(fb_step, 1)
                dve.wait_ge(fb_step, b * 3 + 1)
                V.tensor_copy(sstat[0:H, 7:8], fb[:, NK - 1:NK]).then_inc(fb_step, 1)
                dve.wait_ge(fb_step, b * 3 + 2)
                V.tensor_scalar(fb[:, :], fb[:, :], sstat[0:H, 7:8], -1.0, ALU.subtract, ALU.mult).then_inc(fb_step, 1)
                dve.wait_ge(fb_step, b * 3 + 3)
                dve.sem_inc(fb_ready, 1)
                for pg in range(NPG):
                    dve.wait_ge(kt_ready, b * 16 + (8 + 2 * pg + 2))
                    V.tensor_copy(kT[pg // 4][:, 4:8, (pg % 4) * P:(pg % 4 + 1) * P],
                                  psum[:, 5, :].rearrange("p (c t) -> p c t", c=4)).then_inc(kt_dve, 1)
                dve.wait_ge(ss_ready, b * 2 + 4)
                V.reduce_max(sstat[:, 0:1], psum[:, 0:2, :].rearrange("p a b -> p (a b)"), AX_X, negate=True)\
                    .then_inc(sp_step, 1)
                V.reduce_max(sstat[:, 1:2], psum[:, 2, 0:NS], AX_X, negate=True).then_inc(sp_step, 1)
                dve.wait_ge(sp_step, b * 7 + 3)
                V.tensor_tensor(sstat[:, 2:3], sstat[:, 0:1], sstat[:, 1:2], ALU.min).then_inc(ss_max, 1)
                dve.wait_ge(ss_exp, b * 2 + 2)
                V.tensor_tensor(sstat[:, 5:6], sstat[:, 3:4], sstat[:, 4:5], ALU.add).then_inc(sp_step, 1)
                dve.wait_ge(sp_step, b * 7 + 4)
                V.reciprocal(sstat[:, 6:7], sstat[:, 5:6]).then_inc(sp_step, 1)
                dve.wait_ge(sp_step, b * 7 + 5)
                V.tensor_scalar(sprob[:, :], sprob[:, :], sstat[:, 6:7], None, ALU.mult).then_inc(sp_step, 1)
                dve.wait_ge(sp_step, b * 7 + 6)
                dve.sem_inc(sp_step, 1)
                dve.sem_inc(sp_ready, 1)
                dve.wait_ge(spt_ready, b * 3 + 2)
                V.tensor_copy(sprobT[:, 4:8, :], psum[:, 5, :].rearrange("p (c t) -> p c t", c=4)).then_inc(spt_dve, 1)
                dve.wait_ge(spv_done, b + 2)
                po = psum[:, 3, 0:P].rearrange("p (c n) -> p c n", c=C)
                copy(y[0:DH, :, cols], po[0:DH, :, 0:NQ]).then_inc(so_taken, 1)
                copy(y[DH:P, :, cols], po[DH:P, :, NQ:2 * NQ]).then_inc(so_taken, 1)

            for t, (t0, n) in enumerate(TILES):
                dve.wait_ge(xs_hi_ready, XS0["o"] + t + 1)
                if t == 0:
                    dve.wait_ge(so_taken, 1 + 2 * NB)
                V.tensor_tensor(xs_lo[:, :, t0:t0 + n], y[:, :, t0:t0 + n], xs_hi[:, :, t0:t0 + n].bitcast(F32),
                                ALU.subtract).then_inc(xs_ready, 1)
            plain("o", y, None)
            dve.wait_ge(acc_free, ACCS + NT * (BLK0["o"] + 8))
            norm("n_att", PAIR, y, ROW_G + 5, ROW_G + 6, XS0["ffn1"])
            ffn(1)
            ple(1)
            dve.wait_ge(ple_added, 2 * C * NT)
            rows(TR_Y, ROWS0[TR_Y])

        @block.tensor
        def _(pe):
            M = nc.tensor.matmul

            def three(out, wh, wl, xh, xl, first, last):
                M(out, wh, xh, start=first, stop=False)
                M(out, wh, xl, start=False, stop=False)
                return M(out, wl, xh, start=False, stop=last)

            def slab(n, slot):
                pe.wait_ge(lo_ready, n + (RAWS + 1))

            def block8(blk, par, slot, xh, xl, xs0=None):
                for t, (t0, n) in enumerate(TILES):
                    pe.wait_ge(acc_free, blk * NT + (t + 1))
                    if xs0 is not None:
                        pe.wait_ge(xs_ready, xs0 + t + 1)
                    for c in range(C):
                        k = slice(c * P, (c + 1) * P)
                        ins = three(acc(par, t), w_hi[slot][:, k], w_lo[slot][:, k],
                                    xh[:, c, t0:t0 + n], xl[:, c, t0:t0 + n], c == 0, c == C - 1)
                    ins.then_inc(acc_ready, 1)

            def transposes_in(tr0, src_of):
                for tb, (t0, n) in enumerate(TOKB):
                    g = tr0 + tb
                    if g >= 3:
                        pe.wait_ge(tr_act, g - 2)
                        pe.wait_ge(tr_dve, g - 2)
                    for half in range(2):
                        for c in range(4):
                            ins = src_of(tb, t0, n, half, c, 2 * (g % 3) + half)
                        ins.then_inc(tr_ready, 1)

            def norm(name, seq):
                s0 = STEP0[name]
                for k in range(len(seq)):
                    s = s0 + k
                    if s:
                        pe.wait_ge(std_ready, s)
                    for j in range(3):
                        q = 3 * s + j
                        pe.wait_ge(sq_ready, q + 1)
                        for c in range(C):
                            ins = M(psum[:, 6, j:j + 1], sqb[q % 2][:, c, :], ones[:, :], start=c == 0, stop=c == C - 1)
                        ins.then_inc(sq_used, 1)
                    pe.wait_ge(rcol_ready, s + 1)
                    if s:
                        pe.wait_ge(rb_used, s)
                    t = seq[k][1]
                    for t0, j in SQB[t]:
                        o = t0 - TILES[t][0]
                        ins = M(psum[:, 7, o:o + P], rcol[:, j:j + 1].broadcast_to([P, P]), ident[:, :],
                                start=True, stop=True)
                    ins.then_inc(rb_ready, 1)

            pe.sem_inc(sq_used, 2)
            pe.wait_ge(consts, 4)
            def x_in(tb, t0, n, half, c, bank):
                src = x_nat[:, tb, :] if tb < 8 else xs_nat[:, :]
                if half == 0 and c == 0:
                    pe.wait_ge(x_landed[tb], 16)
                f0 = (4 * half + c) * P
                return nc.tensor.transpose(psum[:, bank, c * P:c * P + n], src[:, f0:f0 + P], ident[0:n, 0:n])
            transposes_in(TR_X, x_in)
            pe.wait_ge(vec_landed, 64)
            for c in range(C):
                ins = nc.tensor.transpose(psum[:, 6, c * NVEC:(c + 1) * NVEC], vec_nat[:, c * P:(c + 1) * P],
                                          ident[0:NVEC, 0:NVEC])
            ins.then_inc(vec_tr, 1)
            pe.wait_ge(vec_done, 1)
            pe.wait_ge(tr_act, NTB)
            pe.wait_ge(tr_dve, NTB)
            norm("n_in", PRE)

            with pe.Fori(0, C // 2) as i:
                for u in range(6):
                    slab(i * 6 + u, u % 2)
                    block8(i * 6 + u, u, u % 2, xs_hi, xs_lo, XS0["in"])
            pe.wait_ge(mix_ready, C)
            for c in range(C):
                ins = nc.tensor.transpose(psum[0:2 + 2 * NB, 6 + c // 4, (c % 4) * P:(c % 4 + 1) * P],
                                          convT[:, c, :], ident[:, :])
                if c % 4 == 3:
                    ins.then_inc(conv_tr, 1)

            def plain(name, xh, xl, xs0=None):
                for m in range(C):
                    slab(SLAB0[name] + m, m % 2)
                    block8(BLK0[name] + m, m, m % 2, xh, xl, xs0)

            plain("out", mix_hi, mix_lo)
            pe.wait_ge(conv_rows_done, 2)
            norm("n_mix", PAIR)

            def ffn(layer):
                name = f"ffn{layer}"
                n0, b0, c0 = SLAB0[name], BLK0[name], layer * 22

                def gate_up(n, blk):
                    for u in range(4):
                        slab(n + u, u % 2)
                        block8(blk + u, u, u % 2, xs_hi, xs_lo, XS0[name])

                def down(n, blk, chunks, par):
                    pe.wait_ge(hid_ready, chunks * NT + NT)
                    for s in range(2):
                        slab(n + s, s)
                        for m in range(4):
                            for t, (t0, nn) in enumerate(TILES):
                                pe.wait_ge(acc_free, blk * NT + ((4 * s + m) * NT + t + 1))
                                for c in range(2):
                                    k = slice(c * 512 + m * P, c * 512 + (m + 1) * P)
                                    ins = three(acc(m, t), w_hi[s][:, k], w_lo[s][:, k],
                                                hid_hi[par][:, c, t0:t0 + nn], hid_lo[par][:, c, t0:t0 + nn],
                                                c == 0, c == 1)
                                ins.then_inc(acc_ready, 1)

                gate_up(n0, b0)
                with pe.Fori(0, 5) as i:
                    gate_up(i * 12 + (n0 + 4), i * 24 + (b0 + 4))
                    down(i * 12 + (n0 + 8), i * 24 + (b0 + 8), i * 4 + (c0 + 2), 0)
                    gate_up(i * 12 + (n0 + 10), i * 24 + (b0 + 16))
                    down(i * 12 + (n0 + 14), i * 24 + (b0 + 20), i * 4 + (c0 + 4), 1)
                down(n0 + 64, b0 + 124, c0 + 22, 0)

            def ple(layer):
                pe.wait_ge(p_landed, 16 * NTB * (layer + 1))
                pe.wait_ge(acc_free, ACCS + NT * BLK0[f"pp{layer}"])
                for tb, (t0, n) in enumerate(TOKB):
                    if tb >= 6:
                        pe.wait_ge(p_ready, layer * NTB + tb - 5)
                    for c in range(2):
                        ins = nc.tensor.transpose(psum[:, tb % 6, c * P:c * P + n], p_nat[0:n, tb, c * P:(c + 1) * P],
                                                  ident[0:n, 0:n])
                    ins.then_inc(p_tr, 1)
                norm(f"n_ffn{layer}", POST)
                pe.wait_ge(p_ready, (layer + 1) * NTB)
                n0, b0 = SLAB0[f"pp{layer}"], BLK0[f"pp{layer}"]
                for m in range(C):
                    if m % 4 == 0:
                        slab(n0 + m // 4, m // 4)
                    for t, (t0, n) in enumerate(TILES):
                        pe.wait_ge(acc_free, NT * (b0 + m) + t + 1)
                        for c in range(2):
                            k = slice(c * 512 + (m % 4) * P, c * 512 + (m % 4 + 1) * P)
                            ins = three(acc(m, t), w_hi[m // 4][:, k], w_lo[m // 4][:, k],
                                        pT_hi[:, c, t0:t0 + n], pT_lo[:, c, t0:t0 + n], c == 0, c == 1)
                        ins.then_inc(acc_ready, 1)
                plain(f"pg{layer}", xs_hi, xs_lo, XS0[f"pg{layer}"])

            ffn(0)
            ple(0)
            norm("n_kv", PRE)
            plain("k", xs_hi, xs_lo, XS0["kvq"])
            plain("v", xs_hi, xs_lo)
            pe.wait_ge(wf_lo_s, 1)
            for tb in range(8):
                t0 = tb * P
                for c in range(C):
                    ins = three(psum[:, 6, tb * H:(tb + 1) * H], xs_hi[:, c, t0:t0 + P], xs_lo[:, c, t0:t0 + P],
                                wf_hi[:, c, :], wf_lo[:, c, :], c == 0, c == C - 1)
            for c in range(C):
                ins = three(psum[:, 6, 8 * H:9 * H], xs_hi[:, c, T - P:T], xs_lo[:, c, T - P:T],
                            wf_hi[:, c, :], wf_lo[:, c, :], c == 0, c == C - 1)
            ins.then_inc(f_acc, 1)

            def out_of(src):
                def go(tb, t0, n, half, c, bank):
                    return nc.tensor.transpose(psum[0:n, bank, c * P:(c + 1) * P], src[:, 4 * half + c, t0:t0 + n],
                                               ident[:, :])
                return go
            pe.wait_ge(acc_free, ACCS + NT * (BLK0["v"] + 8))
            transposes_in(TR_K, out_of(y))
            transposes_in(TR_V, out_of(vT))
            pe.wait_ge(tr_act, TR_Y)
            pe.wait_ge(tr_dve, TR_Y)
            plain("q", xs_hi, xs_lo)
            pe.wait_ge(f_step, 1)
            for tb in range(8):
                ins = nc.tensor.transpose(psum[0:H, 6 + tb // 4, (tb % 4) * P:(tb % 4 + 1) * P], lf[:, tb, :], ident[:, :])
                if tb % 4 == 3:
                    ins.then_inc(f_tr, 1)
            pe.wait_ge(acc_free, ACCS + NT * (BLK0["q"] + 8))
            nc.tensor.transpose(psum[0:H, 0, 0:P], lf[:, 8, :], ident[:, :]).then_inc(f_tr, 1)

            pe.sem_inc(pv_done, 2)
            pe.wait_ge(f_act, 6)
            pe.wait_ge(consts, 6)
            pe.wait_ge(v_back, 16)

            def scores(hp, j):
                (hh, qb), b = ITEMS[j % NI], s_banks(j)
                if j % 8 == 0:
                    pe.wait_ge(aug_landed[hh], hp * 64 + 64 * (1 + j // NI))
                pe.wait_ge(exp_done, hp * NI + (j + 3 if j % 2 else j + 1))
                q = qaug[hh][:, qb * P:(qb + 1) * P]
                for part in range((qb + 4) // 4):
                    k0 = 512 * part
                    k1 = min(k0 + 512, (qb + 1) * P)
                    diag = k1 == (qb + 1) * P
                    M(psum[:, b + part, 0:k1 - k0], q, kaug[hh][:, k0:k1], start=True, stop=not diag)
                    if diag:
                        M(psum[:, b + part, k1 - k0 - P:k1 - k0], ident[:, :], causal[:, :], start=False,
                          stop=True).then_inc(s_ready, 1)

            def transpose_probs(hp, j):
                pe.wait_ge(exp_done, hp * NI + (j + 5))
                for g, kb, nb in groups(j):
                    pe.wait_ge((pt_act, pt_dve)[g % 2], ghalf(hp, g - g % 2) + 1)
                    for c in range(nb):
                        ins = nc.tensor.transpose(psum[:, 5 + g % 2, c * P:(c + 1) * P],
                                                  prob[j % 2][:, (kb + c) * P:(kb + c + 1) * P], ident[:, :])
                    ins.then_inc(pt_ready, 1)

            def outputs(hp, j):
                hh, qb = ITEMS[j]
                for g, kb, nb in groups(j):
                    pe.wait_ge((pt_act, pt_dve)[g % 2], ghalf(hp, g - g % 2) + 2)
                pe.wait_ge(o_taken, hp * NI + (j + 1))
                for c in range(qb + 1):
                    ins = M(psum[:, 7, 0:DH], probT[j % 2][:, c, :],
                            v_keys[:, c, ds(hp * P + DH * hh, DH)], start=c == 0, stop=c == qb)
                ins.then_inc(pv_done, 1)

            def transpose_o(hp, dve0, act0):
                pe.wait_ge(o_taken, hp * NI + (NI + 1))
                for r in range(2):
                    pe.wait_ge((pt_dve, pt_act)[r], (dve0, act0)[r] + 1)
                    for c in range(4):
                        ins = nc.tensor.transpose(psum[:, 6 - r, c * P:(c + 1) * P], o_pair[:, 4 * r + c, :], ident[:, :])
                    ins.then_inc(pt_ready, 1)

            def pair(hp, first, last):
                for j in range(NI):
                    if not (last and j >= NI - 2):
                        scores(hp, j + 2)
                    transpose_probs(hp, j)
                    if j == 1 and not first:
                        transpose_o(hp - 1, hp * 13, hp * 13 + 1)
                    if j > 0:
                        outputs(hp, j - 1)
                    elif not first:
                        outputs(hp - 1, NI - 1)

            scores(0, 0)
            scores(0, 1)
            pair(0, True, False)
            with pe.Fori(1, HP - 1) as hp:
                pair(hp, False, False)
            pair(HP - 1, False, True)
            outputs(HP - 1, NI - 1)
            transpose_o(HP - 1, 13 * HP - 1, 13 * HP - 1)

            pe.sem_inc(kt_ready, 8)
            pe.sem_inc(lfp_tr, 1)
            pe.sem_inc(ss_ready, 2)
            pe.sem_inc(spv_done, 1)
            pe.wait_ge(pt_act, 1 + 13 * HP)
            pe.wait_ge(pt_dve, 1 + 13 * HP)
            pe.wait_ge(consts, 13)
            pe.wait_ge(new_landed, 32)
            pe.wait_ge(f_step, 8)
            with pe.Fori(0, NB) as b:
                pe.wait_ge(lfpage_landed, b * (16 * NPG) + 16 * NPG)
                for r in range(2):
                    pe.wait_ge(fb_ready, b + 1)
                    for c in range(4):
                        ins = nc.tensor.transpose(psum[0:H, 6 + r, c * P:(c + 1) * P], lf_page[:, 4 * r + c, :], ident[:, :])
                    ins.then_inc(lfp_tr, 1)
                pe.wait_ge(qbd_ready, b + 1)
                for pg in range(NPG):
                    pe.wait_ge(kpage_landed[pg % 4], b * 32 + 16 * (pg // 4 + 1))
                    for half in range(2):
                        pe.wait_ge((kt_act, kt_dve)[half], b * NPG + (pg + 1))
                        if pg == 0:
                            pe.wait_ge((spt_act, spt_dve)[half], b * (2 - half) + 1)
                        for c in range(4):
                            f0 = (4 * half + c) * P
                            ins = nc.tensor.transpose(psum[:, 4 + half, c * P:(c + 1) * P], kpage[pg % 4][:, f0:f0 + P],
                                                      ident[:, :])
                        ins.then_inc(kt_ready, 1)
                    if pg % 4 == 3:
                        half = pg // 4
                        pe.wait_ge(kt_act, b * NPG + (pg + 2))
                        pe.wait_ge(kt_dve, b * NPG + (pg + 2))
                        pe.wait_ge(fb_ready, b + 2)
                        if half == 0:
                            pe.wait_ge(so_taken, b * 2 + 1)
                        for c in range(C):
                            M(psum[:, half, :], qbd_w[:, c, :], kT[half][:, c, :], start=c == 0, stop=False)
                        ins = M(psum[:, half, :], expand[:, :], fb[:, 512 * half:512 * half + 512], start=False, stop=True)
                        if half == 0:
                            ins.then_inc(ss_ready, 1)
                for c in range(C):
                    M(psum[:, 2, 0:NS], qbd_w[:, c, :], k_newT[:, c, :], start=c == 0, stop=False)
                M(psum[:, 2, 0:NS], expand[:, :], nfnew[:, :], start=False, stop=False)
                M(psum[:, 2, 0:NS], qsel[:, :], wmask[:, ds(b * (-NQ) + 56, NS)], start=False, stop=True)\
                    .then_inc(ss_ready, 1)
                pe.wait_ge(sp_ready, b + 1)
                for g in range(3):
                    if g == 2:
                        pe.wait_ge(spt_act, b * 2 + 2)
                        pe.sem_inc(passed, 1)
                    for c in range(4 * g, min(4 * g + 4, 9)):
                        n = P if c < 8 else NS
                        ins = nc.tensor.transpose(psum[0:n, 4 + g % 2, (c % 4) * P:(c % 4 + 1) * P],
                                                  sprob[:, c * P:c * P + n], ident[:, :])
                    ins.then_inc(spt_ready, 1)
                pe.wait_ge(spt_act, b * 2 + 3)
                pe.wait_ge(spt_dve, b + 2)
                pe.wait_ge(vpage_landed, b * (16 * NPG) + 16 * NPG)
                for c in range(C):
                    o = psum[:, 3, 16 * c:16 * c + 16]
                    for pg in range(NPG):
                        M(o, v_page[:, pg, c * P:(c + 1) * P], sprobT[:, pg, 16 * c:16 * c + 16], start=pg == 0, stop=False)
                    ins = M(o, v_new[:, c * P:(c + 1) * P], sprobT[0:NS, 8, 16 * c:16 * c + 16], start=False, stop=True)
                ins.then_inc(spv_done, 1)

            plain("o", xs_hi, xs_lo, XS0["o"])
            norm("n_att", PAIR)
            ffn(1)
            ple(1)
            pe.wait_ge(ple_added, 2 * C * NT)
            pe.wait_ge(acc_free, ACCS + NT * BLKS)
            transposes_in(TR_Y, out_of(h))


_INS = ['x_prompt', 'x_sample', 'state_conv', 'cache_k', 'cache_v', 'cache_logf', 'page_table', 'p_prompt',
        'p_sample', 'norm_g', 'w_in', 'w_conv', 'w_out', 'g_kv', 'w_k', 'w_v', 'w_f', 'b_f', 'w_q', 'w_o',
        'w_gate', 'w_up', 'w_down', 'w_ple', 'w_ple_gate']
_OUTS = [(1, SEQ, D), (NB, NQ, D), (1, 1, 2, D), (1, SEQ, H, DH), (1, SEQ, H, DH), (1, SEQ, H), (1, NB, 2, D),
         (NB, NQ, H, DH), (NB, NQ, H, DH), (NB, NQ, H)]


def kernel(**inputs):
    import numpy as _np
    import concourse.bacc as _bacc
    from concourse import mybir as _mybir
    from concourse.bass_utils import run_bass_kernel_spmd as _run

    nc = _bacc.Bacc("TRN2", target_bir_lowering=False, num_devices=1)
    arrays, ins, outs = {}, [], []
    for name in _INS:
        a = _np.ascontiguousarray(inputs[name])
        arrays[f"in_{name}"] = a
        ins.append(nc.dram_tensor(f"in_{name}", a.shape, _mybir.dt.from_np(a.dtype), kind="ExternalInput").ap())
    for i, shape in enumerate(_OUTS):
        outs.append(nc.dram_tensor(f"out_{i}", shape, F32, kind="ExternalOutput").ap())
    trunk(nc, ins, outs)
    r = _run(nc, [arrays], core_ids=[0])
    return tuple(r.results[0][f"out_{i}"] for i in range(len(_OUTS)))
```

```python
from contextlib import ExitStack

import concourse.bass as bass
from concourse import mybir

F32 = mybir.dt.float32
F32R = mybir.dt.float32r
I32 = mybir.dt.int32
ALU = mybir.AluOpType
ACT = mybir.ActivationFunctionType
AX_X = mybir.AxisListType.X
ds = bass.ds

P = 128
D = 1024
C = D // P
SEQ = 1024
NB, NQ = 8, 8
NS = NB * NQ
T = SEQ + NS
H, DH = 16, 64
D_FF = 2816
PLE = 256
PAGE, NPG, POOL = 128, 8, 80
EPS = 1e-6
SCALE = DH ** -0.5
MASKED = -1e30

TILES = [(0, 384), (384, 384), (768, T - 768)]
NT = len(TILES)
TOKB = [(128 * i, 128) for i in range(8)] + [(SEQ, NS)]
NTB = len(TOKB)
SQB = [[(0, 0), (128, 1), (256, 2)], [(384, 0), (512, 1), (640, 2)],
       [(768, 0), (896, 1), (T - 128, 2)]]

STAGES = [("in", 24, 24), ("out", 8, 8), ("ffn0", 66, 132), ("pp0", 2, 8), ("pg0", 8, 8),
          ("k", 8, 8), ("v", 8, 8), ("q", 8, 8), ("o", 8, 8), ("ffn1", 66, 132), ("pp1", 2, 8),
          ("pg1", 8, 8)]
SLAB0, BLK0 = {}, {}
_s = _b = 0
for _name, _ns, _nb in STAGES:
    SLAB0[_name], BLK0[_name] = _s, _b
    _s, _b = _s + _ns, _b + _nb
SLABS, BLKS = _s, _b
RAWS = 2
HLS = 2
ACCS = 2 * NT

PAIR = [("post", 0), ("post", 1), ("pre", 0), ("post", 2), ("pre", 1), ("pre", 2)]
PRE = [("pre", 0), ("pre", 1), ("pre", 2)]
POST = [("post", 0), ("post", 1), ("post", 2)]
STEP0 = {"n_in": 0, "n_mix": 3, "n_ffn0": 9, "n_kv": 12, "n_att": 15, "n_ffn1": 21}
XS0 = {"in": 0, "ffn0": 3, "pg0": 6, "kvq": 9, "o": 12, "ffn1": 15, "pg1": 18}
HR0 = {"n_mix": 0, "n_ffn0": 3, "n_att": 6, "n_ffn1": 9}
ROW_G, ROW_KV, ROW_CONV, ROW_STATE, NVEC = 0, 8, 9, 12, 28

REG = C * T * 4
B0 = 16640
A_H, A_XH, A_XL, A_Y, A_G = (B0 + i * REG for i in range(5))
A_RAW = B0 + 5 * REG
A_WH = A_RAW + RAWS * 4096
A_WL = A_WH + HLS * 4096
A_STG = A_WL + HLS * 4096
A_MISC = A_STG + 8192


def trunk(nc, ins, outs):
    (x_prompt, x_sample, state_conv, cache_k, cache_v, cache_logf, page_table, p_prompt, p_sample,
     norm_g, w_in, w_conv, w_out, g_kv, w_k, w_v, w_f, b_f, w_q, w_o, w_gate, w_up, w_down, w_ple,
     w_ple_gate) = ins
    (y_prompt, y_sample, conv_prompt, k_prompt, v_prompt, logf_prompt, conv_sample, k_sample,
     v_sample, logf_sample) = outs

    kT_dram = nc.dram_tensor("kT_scratch", [D, T], F32).ap()
    fsum_dram = nc.dram_tensor("fsum_scratch", [2, H, SEQ], F32).ap()

    def sb(name, shape, dt, off):
        return nc.alloc_sbuf_tensor_at(name, shape, dt, offset=off)

    h = sb("h", [P, C, T], F32, A_H)
    xs_hi = sb("xs_hi", [P, C, T], F32R, A_XH)
    xs_lo = sb("xs_lo", [P, C, T], F32R, A_XL)
    y_mix = sb("y_mix", [P, C, T], F32, A_XH)
    y = sb("y", [P, C, T], F32, A_Y)
    vT = sb("vT", [P, C, T], F32, A_G)
    raw = [sb(f"raw{i}", [P, 1024], F32, A_RAW + 4096 * i) for i in range(RAWS)]
    w_hi = [sb(f"w_hi{i}", [P, 1024], F32R, A_WH + 4096 * i) for i in range(HLS)]
    w_lo = [sb(f"w_lo{i}", [P, 1024], F32R, A_WL + 4096 * i) for i in range(HLS)]
    bgate = sb("bgate", [P, C, T], F32, A_Y)
    mix_hi = sb("mix_hi", [P, C, T], F32R, A_Y)
    zconv = sb("zconv", [P, C, T], F32, A_G)
    mix_lo = sb("mix_lo", [P, C, T], F32R, A_G)
    NPAD = SEQ + 2
    cup = sb("cup", [P, NPAD + NB * (NQ + 2)], F32, A_STG)
    cup_s = cup[:, NPAD:].rearrange("p (b t) -> p b t", b=NB)
    x_nat = sb("x_nat", [P, 8, D], F32, A_Y)
    xs_nat = sb("xs_nat", [NS, D], F32, A_STG)
    vec_nat = sb("vec_nat", [NVEC, D], F32, A_STG + 4096)
    sqb = [sb(f"sqb{i}", [P, C, P], F32, A_G + 4096 * i) for i in range(2)]
    xn = [sb(f"xn{i}", [P, C, 384], F32, A_G + 8192 + 12288 * i) for i in range(2)]
    p_nat = sb("p_nat", [P, NTB, PLE], F32, A_G + 8192)
    pT_hi = sb("pT_hi", [P, 2, T], F32R, A_G + 8192 + 9216)
    pT_lo = sb("pT_lo", [P, 2, T], F32R, A_G + 8192 + 9216 + 8704)
    hid_hi = [sb(f"hid_hi{i}", [P, 2, T], F32R, A_G + 17408 * i) for i in range(2)]
    hid_lo = [sb(f"hid_lo{i}", [P, 2, T], F32R, A_G + 17408 * i + 8704) for i in range(2)]
    act = sb("act", [P, T], F32, A_STG)
    rows_out = [sb(f"rows_out{i}", [P, D], F32, A_STG + 4096 * i) for i in range(2)]

    off = A_MISC
    def misc(name, shape, dt=F32):
        nonlocal off
        n = 4
        for s in shape[1:]:
            n *= s
        t = sb(name, shape, dt, off)
        off += (n + 31) // 32 * 32
        assert off <= 229344
        return t
    vecT = misc("vecT", [P, C, NVEC])
    ident = misc("ident", [P, P])
    ones = misc("ones", [P, 1])
    eps_c = misc("eps_c", [P, 1])
    stdc = misc("stdc", [P, 3])
    rcol = misc("rcol", [P, 3])
    convT = misc("convT", [P, C, 2 + 2 * NB])
    wf_raw = misc("wf_raw", [P, C, H])
    wf_hi = misc("wf_hi", [P, C, H], F32R)
    wf_lo = misc("wf_lo", [P, C, H], F32R)
    lfz = misc("lfz", [P, NTB, H])
    lf = misc("lf", [P, NTB, H])
    bf = misc("bf", [P, H])
    ptab = misc("ptab", [1, NB * NPG], I32)
    segm = misc("segm", [H, NS])
    one16 = misc("one16", [H, 1])
    fsum_new = misc("fsum_new", [H, NS])
    conv_rows = sb("conv_rows", [2 + 2 * NB, D], F32, A_STG)

    kaug = [sb(f"kaug{i}", [66, SEQ], F32, A_XH + 4096 * i) for i in range(2)]
    qaug = [sb(f"qaug{i}", [66, SEQ], F32, A_XH + 8192 + 4096 * i) for i in range(2)]
    prob = [sb(f"prob{i}", [P, SEQ], F32, A_XH + 16384 + 4096 * i) for i in range(2)]
    probT = [sb(f"probT{i}", [P, 8, P], F32, A_XH + 24576 + 4096 * i) for i in range(2)]
    o_pair = sb("o_pair", [P, 8, P], F32, A_XH + 32768)
    lfT = sb("lfT", [H, T], F32, A_XH + 36864)
    fsum = sb("fsum", [H, SEQ], F32, A_XH + 41216)
    nfsum = sb("nfsum", [H, SEQ], F32, A_XH + 45568)
    causal = sb("causal", [P, P], F32, A_XH + 49920)
    nmx = sb("nmx", [P, 8], F32, A_XH + 50432)
    rsum = sb("rsum", [P, 8], F32, A_XH + 50464)
    rinv = sb("rinv", [P, 8], F32, A_XH + 50496)
    v_keys = sb("v_keys", [P, 8, D], F32, A_G)
    NK = NPG * PAGE
    sprob = sb("sprob", [P, NK + NS], F32, A_XH)
    o_rows = sb("o_rows", [P, D], F32, A_XH)
    sprobT = sb("sprobT", [P, NPG + 1, P], F32, A_XH + 4352)
    cum = sb("cum", [H, NK], F32, A_XH + 8960)
    v_new = sb("v_new", [NS, D], F32, A_XH + 13056)
    kT = [sb(f"kT{i}", [P, C, 512], F32, A_XH + 17152 + 16384 * i) for i in range(2)]
    sstat = sb("sstat", [P, 8], F32, A_XH + 49920)
    kpage = [sb(f"kpage{i}", [P, D], F32, A_XH + 50560 + 4096 * i) for i in range(4)]
    k_newT = sb("k_newT", [P, C, NS], F32, A_XH + 66944)
    lf_page = sb("lf_page", [P, NPG, H], F32, A_XH + 68992)
    lf_pageT = sb("lf_pageT", [H, NK], F32, A_WH + 4096)
    v_page = sb("v_page", [P, NPG, D], F32, A_G)
    qdiag = [sb(f"qdiag{i}", [P, C, P + 16], F32, A_STG + 512 - 4608 * i) for i in range(2)]
    qbd = [q[:, :, :].rearrange("p c n -> p (c n)")[:, 0:D] for q in qdiag]
    E_off = A_G + 32768
    nexpand = sb("nexpand", [H, P], F32, E_off)
    qsel = sb("qsel", [NQ, P], F32, E_off + 512)
    wmask = sb("wmask", [NQ, 120], F32, E_off + 1024)
    cum_new = [sb(f"cum_new{i}", [H, NS], F32, E_off + 1504 + 256 * i) for i in range(2)]

    with ExitStack() as ctx:
        psum = ctx.enter_context(nc.psum_tensor("psum", [P, 8, 512], F32))

        def sem(name):
            return ctx.enter_context(nc.semaphore(name))

        def acc(b, t):
            return psum[:, 3 * (b % 2) + t, 0:TILES[t][1]]

        raw_landed = [sem(f"raw_landed{i}") for i in range(RAWS)]
        hi_ready = sem("hi_ready")
        lo_ready = sem("lo_ready")
        slab_used = sem("slab_used")
        acc_ready = sem("acc_ready")
        acc_free = sem("acc_free")
        consts = sem("consts")
        vec_landed = sem("vec_landed")
        x_landed = [sem(f"x_landed{i}") for i in range(NTB)]
        vec_tr, vec_done = sem("vec_tr"), sem("vec_done")
        tr_ready = sem("tr_ready")
        tr_act, tr_dve = sem("tr_act"), sem("tr_dve")
        rows_stored = [sem(f"rows_stored{i}") for i in range(2)]
        sq_ready, sq_used = sem("sq_ready"), sem("sq_used")
        std_ready, rcol_ready = sem("std_ready"), sem("rcol_ready")
        rb_ready, rb_used = sem("rb_ready"), sem("rb_used")
        h_ready = sem("h_ready")
        xs_hi_ready, xs_ready = sem("xs_hi_ready"), sem("xs_ready")
        conv_step = sem("conv_step")
        z_hi = sem("z_hi")
        mix_ready = sem("mix_ready")
        conv_tr, conv_rows_done, conv_stored = sem("conv_tr"), sem("conv_rows_done"), sem("conv_stored")
        y_zero = sem("y_zero")
        sig_ready = sem("sig_ready")
        act_ready, hid_hi_ready, hid_ready = sem("act_ready"), sem("hid_hi_ready"), sem("hid_ready")
        p_landed = sem("p_landed")
        p_tr, p_hi_ready, p_ready = sem("p_tr"), sem("p_hi_ready"), sem("p_ready")
        ple_mul, ple_sig = sem("ple_mul"), sem("ple_sig")
        ple_added = sem("ple_added")
        kT_stored = sem("kT_stored")
        wf_landed, wf_hi_s, wf_lo_s = sem("wf_landed"), sem("wf_hi_s"), sem("wf_lo_s")
        f_acc, f_z = sem("f_acc"), sem("f_z")
        f_act, f_step = sem("f_act"), sem("f_step")
        f_stored = sem("f_stored")
        f_tr = sem("f_tr")
        fs_stored = sem("fs_stored")
        v_back = sem("v_back")
        aug_one = sem("aug_one")
        aug_landed = [sem(f"aug_landed{i}") for i in range(2)]
        s_ready, s_max, exp_done = sem("s_ready"), sem("s_max"), sem("exp_done")
        pt_ready, pt_act, pt_dve = sem("pt_ready"), sem("pt_act"), sem("pt_dve")
        pv_done, rinv_s, o_taken = sem("pv_done"), sem("rinv_s"), sem("o_taken")
        tab_landed = sem("tab_landed")
        new_landed = sem("new_landed")
        kpage_landed = [sem(f"kpage_landed{i}") for i in range(4)]
        vpage_landed = [sem(f"vpage_landed{i}") for i in range(2)]
        lfpage_landed = sem("lfpage_landed")
        qbd_zero, qbd_ready = sem("qbd_zero"), sem("qbd_ready")
        kpage_used = sem("kpage_used")
        st_ready, st_act, st_dve = sem("st_ready"), sem("st_act"), sem("st_dve")
        cum_ready, fb_ready = sem("cum_ready"), sem("fb_ready")
        ss_ready, ss_max, ss_exp = sem("ss_ready"), sem("ss_max"), sem("ss_exp")
        sp_step = sem("sp_step")
        spv_done, so_rows = sem("spv_done"), sem("so_rows")
        so_tr, so_taken = sem("so_tr"), sem("so_taken")
        passed = sem("passed")
        block = ctx.enter_context(nc.Block())

        TR_X, TR_K, TR_V, TR_Y = 0, NTB, 2 * NTB, 3 * NTB
        ROWS0 = {TR_K: 0, TR_V: NTB, TR_Y: 2 * NTB}
        ITEMS = [(hh, qb) for hh in range(2) for qb in (7, 0, 6, 1, 5, 2, 4, 3)]
        NI, HP = len(ITEMS), H // 2
        OT_AT = 3

        def s_banks(j):
            return 4 if j % 2 else 2 * (j // 2 % 2)

        def s_view(j):
            nk = (ITEMS[j % NI][1] + 1) * P
            b = s_banks(j)
            return psum[:, b, 0:nk] if j % 2 else psum[:, b:b + 2, :].rearrange("p a b -> p (a b)")[:, 0:nk]

        def groups(j):
            g = 3 * (j // 2) + 2 * (j % 2)
            g += 2 if g >= OT_AT else 0
            nb = ITEMS[j][1] + 1
            return [(g + q, 4 * q, min(4, nb - 4 * q)) for q in range((nb + 3) // 4)]

        def gcount(hp, g):
            if isinstance(hp, int) and hp == 0:
                return g if g <= OT_AT else g - 2
            return hp * 26 + (g - 2)

        def ghalf(hp, g):
            if isinstance(hp, int) and hp == 0:
                return (g if g < OT_AT else g - 2) // 2
            return hp * 13 + (g // 2 - 1)

        def st_before(b):
            if isinstance(b, int) and b == 0:
                return 13, 7, 6
            return b * 21 + 10, b * 11 + 5, b * 10 + 5

        def st_mid(b, first):
            n, na, nv = st_before(b)
            return (n + 8, na + 4, nv + 4) if first else (n + 11, na + 6, nv + 5)

        CONV_STEPS = 14

        @block.sync
        def _(sp):
            def cols(w, c0, n=P, k=C):
                return w[:, ds(c0, n)].rearrange("(k p) n -> p k n", p=P)

            def load(n, slot, src, k, width):
                if isinstance(n, int) and n < RAWS:
                    pass
                else:
                    sp.wait_ge(lo_ready, n + 1)
                sp.dma_start(raw[slot][:, :].rearrange("p (k n) -> p k n", k=k), src)\
                    .then_inc(raw_landed[slot], 16)

            def plain(name, w, skip=0, take=C):
                for m in range(skip, take):
                    load(SLAB0[name] + m, m % 2, cols(w, m * P), C, P)

            w_in0 = w_in[0]
            for u, part in enumerate((0, 1, 2, 0, 1, 2)):
                load(u, u % 2, cols(w_in0, part * D + (u // 3) * P), C, P)
            with sp.Fori(1, C // 2) as i:
                for u, part in enumerate((0, 1, 2, 0, 1, 2)):
                    load(i * 6 + u, u % 2, cols(w_in0, i * (2 * P) + (part * D + (u // 3) * P)), C, P)
            plain("out", w_out[0])

            def ffn(name, layer):
                wg, wu, wd = w_gate[layer], w_up[layer], w_down[layer]

                def gate_up(g, n):
                    for u in range(4):
                        src = (wg, wu)[u % 2]
                        load(n + u, u % 2, cols(src, g * (2 * P) + (u // 2) * P), C, P)

                def down(g, n):
                    rows = wd[ds(g * (2 * P), 2 * P), :].rearrange("(k p) n -> p k n", p=P)
                    for u in range(2):
                        load(n + u, u % 2, rows[:, :, u * 512:(u + 1) * 512], 2, 512)

                n0 = SLAB0[name]
                gate_up(0, n0)
                with sp.Fori(0, 5) as i:
                    gate_up(i * 2 + 1, i * 12 + (n0 + 4))
                    down(i * 2, i * 12 + (n0 + 8))
                    gate_up(i * 2 + 2, i * 12 + (n0 + 10))
                    down(i * 2 + 1, i * 12 + (n0 + 14))
                down(10, n0 + 64)

            def ple(layer):
                rows = w_ple[layer].rearrange("(k p) n -> p k n", p=P)
                for u in range(2):
                    load(SLAB0[f"pp{layer}"] + u, u, rows[:, :, u * 512:(u + 1) * 512], 2, 512)
                plain(f"pg{layer}", w_ple_gate[layer])

            ffn("ffn0", 0)
            ple(0)
            plain("k", w_k)
            plain("v", w_v)
            plain("q", w_q[0])
            plain("o", w_o[0], 0, 3)

            sp.dma_start(ptab[:, :], page_table.rearrange("(o b) n -> o (b n)", o=1)).then_inc(tab_landed, 16)
            sp.wait_ge(tab_landed, 16)
            sp.wait_ge(acc_free, ACCS + NT * (BLK0["q"] + 8))
            k_pages = cache_k.rearrange("n t h d -> n t (h d)")
            with sp.Fori(0, NB) as b:
                for pg in range(NPG):
                    sp.wait_ge(kpage_used, b * NPG + (pg + 1))
                    page = sp.value_load(ptab[0:1, ds(b * NPG + pg, 1)], min_val=0, max_val=POOL - 1)
                    sp.dma_start(kpage[pg % 4][:, :], k_pages[ds(page, 1)].rearrange("o t d -> (o t) d"))\
                        .then_inc(kpage_landed[pg % 4], 16)
            plain("o", w_o[0], 3)
            ffn("ffn1", 1)
            ple(1)

        @block.gpsimd
        def _(pool):
            def mask(t, pattern, base, cm, op=ALU.is_ge, fill=MASKED):
                pool.affine_select(out=t, in_=t, compare_op=op, fill=fill, base=base, pattern=pattern,
                                   channel_multiplier=cm).then_inc(consts, 1)

            for tb, (t0, n) in enumerate(TOKB):
                dst = x_nat[:, tb, :] if tb < 8 else xs_nat[:, :]
                src = x_prompt[0, t0:t0 + n, :] if tb < 8 else x_sample.rearrange("b t d -> (b t) d")
                if tb == 3:
                    for r0, n_, s in ((ROW_G, 8, norm_g.rearrange("l k d -> (l k) d")),
                                      (ROW_KV, 1, g_kv.rearrange("(o d) -> o d", o=1)),
                                      (ROW_CONV, 3, w_conv[0]),
                                      (ROW_STATE, 16, state_conv[0].rearrange("b t d -> (b t) d"))):
                        pool.dma_start(vec_nat[r0:r0 + n_, :], s).then_inc(vec_landed, 16)
                pool.dma_start(dst, src).then_inc(x_landed[tb], 16)
                if tb == 0:
                    pool.memset(ident[:, :], 0.0).then_inc(consts, 1)
                    pool.memset(ones[:, :], 1.0).then_inc(consts, 1)
                    pool.memset(eps_c[:, :], EPS).then_inc(consts, 1)
                    pool.wait_ge(consts, 3)
                    mask(ident[:, :], [[-1, P]], 0, 1, ALU.not_equal, 1.0)
            pool.dma_start(wf_raw[:, :, :], w_f.rearrange("(k p) n -> p k n", p=P)).then_inc(wf_landed, 16)
            pool.dma_start(bf[:, :], b_f.rearrange("(o n) -> o n", o=1).broadcast_to([P, H])).then_inc(wf_landed, 16)

            pool.wait_ge(conv_rows_done, 2)
            pool.dma_start(conv_prompt[0, 0], conv_rows[0:2, :]).then_inc(conv_stored, 16)
            pool.dma_start(conv_sample[0].rearrange("b t d -> (b t) d"), conv_rows[2:2 + 2 * NB, :])\
                .then_inc(conv_stored, 16)

            def ffn(layer, y_free):
                pool.wait_ge(rb_used, y_free)
                pool.memset(y[:, :, :], 0.0).then_inc(y_zero, 1)
                pool.wait_ge(acc_ready, NT * BLK0[f"pp{layer}"])
                for tb, (t0, n) in enumerate(TOKB):
                    src = p_prompt[layer, 0, t0:t0 + n, :] if tb < 8 else \
                        p_sample[layer].rearrange("b t d -> (b t) d")
                    pool.dma_start(p_nat[0:n, tb, :], src).then_inc(p_landed, 16)

            ffn(0, 9)

            pool.wait_ge(f_step, 1)
            pool.dma_start(logf_prompt[0].rearrange("(b p) h -> p b h", p=P), lf[:, 0:8, :])\
                .then_inc(f_stored, 16)
            pool.dma_start(logf_sample.rearrange("b t h -> (b t) h"), lf[P - NS:P, 8, :]).then_inc(f_stored, 16)

            def store_rows(tr0, prompt, sample):
                for tb, (t0, n) in enumerate(TOKB):
                    pool.wait_ge(tr_act, tr0 + tb + 1)
                    pool.wait_ge(tr_dve, tr0 + tb + 1)
                    dst = prompt[t0:t0 + n, :] if tb < 8 else sample
                    r = ROWS0[tr0] + tb
                    pool.dma_start(dst, rows_out[r % 2][0:n, :]).then_inc(rows_stored[r % 2], 16)

            pool.wait_ge(acc_free, ACCS + NT * (BLK0["k"] + 8))
            pool.dma_start(kT_dram.rearrange("(c p) t -> p c t", p=P), y[:, :, :]).then_inc(kT_stored, 16)
            store_rows(TR_K, k_prompt[0].rearrange("t h d -> t (h d)"), k_sample.rearrange("b t h d -> (b t) (h d)"))
            store_rows(TR_V, v_prompt[0].rearrange("t h d -> t (h d)"), v_sample.rearrange("b t h d -> (b t) (h d)"))
            for r in range(2):
                pool.wait_ge(rows_stored[r], 16 * NTB)
            pool.dma_start(v_keys[:, :, :], v_prompt[0].rearrange("(b p) h d -> p b (h d)", p=P))\
                .then_inc(v_back, 16)
            pool.wait_ge(acc_free, ACCS + NT * (BLK0["q"] + 8))
            pool.memset(causal[:, :], 0.0).then_inc(consts, 1)
            pool.wait_ge(consts, 5)
            mask(causal[:, :], [[-1, P]], 0, 1)
            pool.wait_ge(consts, 6)
            for k, t in enumerate((*kaug, *qaug)):
                if k:
                    pool.wait_ge(aug_one, k)
                pool.memset(t[DH:DH + 2, :], 1.0).then_inc(aug_one, 1)
            pool.wait_ge(f_step, 6)
            pool.dma_start(fsum_dram[0], fsum[:, 0:SEQ]).then_inc(fs_stored, 16)
            pool.dma_start(fsum_dram[1], nfsum[:, 0:SEQ]).then_inc(fs_stored, 16)
            pool.wait_ge(fs_stored, 32)
            pool.wait_ge(kT_stored, 16)
            pool.wait_ge(aug_one, 4)

            def load_aug(hp, hh):
                rows = kT_dram[ds(hp * P + DH * hh, DH), 0:SEQ]
                pool.dma_start(kaug[hh][0:DH, :], rows).then_inc(aug_landed[hh], 16)
                pool.dma_start(kaug[hh][DH:DH + 1, :], fsum_dram[1, ds(hp * 2 + hh, 1), :])\
                    .then_inc(aug_landed[hh], 16)
                pool.dma_start(qaug[hh][0:DH, :], y[DH * hh:DH * hh + DH, ds(hp, 1), 0:SEQ]
                               .rearrange("p o t -> p (o t)")).then_inc(aug_landed[hh], 16)
                pool.dma_start(qaug[hh][DH + 1:DH + 2, :], fsum_dram[0, ds(hp * 2 + hh, 1), :])\
                    .then_inc(aug_landed[hh], 16)

            for hh in range(2):
                load_aug(0, hh)

            v_pages = cache_v.rearrange("n t h d -> n t (h d)")

            def load_lf(b):
                for pg in range(NPG):
                    page = pool.value_load(ptab[0:1, ds(b * NPG + pg, 1)], min_val=0, max_val=POOL - 1)
                    pool.dma_start(lf_page[:, pg, :], cache_logf[ds(page, 1)].rearrange("o t h -> (o t) h"))\
                        .then_inc(lfpage_landed, 16)

            def load_v(b):
                for f in range(2):
                    pool.wait_ge(spv_done, b * 2 + (f + 1))
                    pool.sem_inc(passed, 1)
                    for pg in range(NPG):
                        page = pool.value_load(ptab[0:1, ds(b * NPG + pg, 1)], min_val=0, max_val=POOL - 1)
                        pool.dma_start(v_page[:, pg, 512 * f:512 * f + 512],
                                       v_pages[ds(page, 1), :, 512 * f:512 * f + 512].rearrange("o t d -> (o t) d"))\
                            .then_inc(vpage_landed[f], 16)

            pool.memset(nexpand[:, :], 0.0).then_inc(consts, 1)
            pool.memset(qsel[:, :], 0.0).then_inc(consts, 1)
            pool.memset(wmask[:, :], 0.0).then_inc(consts, 1)
            pool.wait_ge(consts, 9)
            mask(nexpand[:, :], [[1, H], [0, NQ]], 0, -1, ALU.not_equal, -1.0)
            mask(qsel[:, :], [[0, H], [1, NQ]], 0, -1, ALU.not_equal, 1.0)
            mask(wmask[:, :], [[1, 120]], -56, 0)
            pool.wait_ge(consts, 12)
            mask(wmask[:, :], [[-1, 120]], 56, 1)
            for i in range(2):
                pool.memset(qbd[i], 0.0).then_inc(qbd_zero, 1)
            pool.dma_start(k_newT[:, :, :], kT_dram[:, SEQ:T].rearrange("(c p) t -> p c t", p=P))\
                .then_inc(new_landed, 16)
            pool.wait_ge(tab_landed, 16)
            load_lf(0)
            with pool.Fori(1, H // 2) as hp:
                for hh in range(2):
                    pool.wait_ge(s_ready, hp * 16 + (8 * hh - 8))
                    load_aug(hp, hh)

            pool.wait_ge(pv_done, 2 + 8 * H)
            pool.wait_ge(pt_ready, 26 * HP)
            pool.dma_start(v_new[:, :], v_sample.rearrange("b t h d -> (b t) (h d)")).then_inc(new_landed, 16)
            with pool.Fori(0, NB - 1) as b:
                pool.wait_ge(cum_ready, b + 1)
                pool.sem_inc(passed, 1)
                load_lf(b + 1)
                load_v(b)
            load_v(NB - 1)

            ffn(1, 21)
            store_rows(TR_Y, y_prompt[0], y_sample.rearrange("b t d -> (b t) d"))
            pool.wait_ge(rows_stored[0], 16 * ((3 * NTB + 1) // 2))
            pool.wait_ge(rows_stored[1], 16 * (3 * NTB // 2))
            pool.wait_ge(conv_stored, 32)
            pool.wait_ge(f_stored, 32)

        @block.scalar
        def _(act_e):
            A = nc.scalar.activation

            def hi(n2, slot, gain=None):
                act_e.wait_ge(raw_landed[slot], n2 * 16 + 16)
                act_e.wait_ge(slab_used, n2 * 2 + (slot + 1))
                if gain is None:
                    A(w_hi[slot][:, :], raw[slot][:, :], ACT.Copy).then_inc(hi_ready, 1)
                else:
                    for c in range(C):
                        ins = A(w_hi[slot][:, c * P:(c + 1) * P], raw[slot][:, c * P:(c + 1) * P], ACT.Copy,
                                scale=vecT[:, c, gain:gain + 1])
                    ins.then_inc(hi_ready, 1)

            def hi_run(n, count, gain=None):
                for j in range(n, n + count):
                    hi(j // 2, j % 2, gain)

            def squares(s, src, t):
                for t0, j in SQB[t]:
                    q = 3 * s + j
                    act_e.wait_ge(sq_used, q + 1)
                    A(sqb[q % 2][:, :, :], src[:, :, t0:t0 + P], ACT.Square).then_inc(sq_ready, 1)
                act_e.wait_ge(sq_used, 2 + 3 * (s + 1))
                if s:
                    act_e.wait_ge(rcol_ready, s)
                A(stdc[:, :], psum[:, 6, 0:3], ACT.Sqrt, bias=eps_c[:, :], scale=1.0 / D)\
                    .then_inc(std_ready, 1)

            def norm(name, seq, src, post_wait, xs0, raw_split=False):
                s0, pending, n_post, n_pre = STEP0[name], None, 0, 0
                for k, (kind, t) in enumerate(seq):
                    s = s0 + k
                    if kind == "post":
                        if k == 0:
                            act_e.wait_ge(acc_free, post_wait)
                        squares(s, src, t)
                    else:
                        if name in HR0:
                            act_e.wait_ge(h_ready, HR0[name] + t + 1)
                        squares(s, h, t)
                    if pending is not None:
                        pending()
                        pending = None
                    t0, n = TILES[t]
                    if kind == "pre":
                        def pending(s=s, t=t, t0=t0, n=n):
                            act_e.wait_ge(rb_used, s + 1)
                            A(xs_hi[:, :, t0:t0 + n], xn[t % 2][:, :, 0:n], ACT.Copy).then_inc(xs_hi_ready, 1)
                    elif raw_split:
                        def pending(t=t, t0=t0, n=n):
                            act_e.wait_ge(h_ready, HR0[name] + t + 1)
                            A(xs_hi[:, :, t0:t0 + n], h[:, :, t0:t0 + n], ACT.Copy).then_inc(xs_hi_ready, 1)
                if pending is not None:
                    pending()


            def take_in():
                for tb, (t0, n) in enumerate(TOKB):
                    act_e.wait_ge(tr_ready, 2 * (TR_X + tb) + 1)
                    bank = 2 * (tb % 3)
                    A(h[:, 0:4, t0:t0 + n], psum[:, bank, :].rearrange("p (c t) -> p c t", c=4)[:, :, 0:n], ACT.Copy)\
                        .then_inc(tr_act, 1)

            def rows(tr0, r0):
                for tb, (t0, n) in enumerate(TOKB):
                    g, r = tr0 + tb, r0 + tb
                    act_e.wait_ge(tr_ready, 2 * g + 1)
                    if r >= 2:
                        act_e.wait_ge(rows_stored[r % 2], 16 * (r // 2))
                    A(rows_out[r % 2][0:n, 0:512], psum[0:n, 2 * (g % 3), :], ACT.Copy).then_inc(tr_act, 1)

            take_in()
            act_e.wait_ge(vec_tr, 1)
            A(vecT[:, :, :].rearrange("p c n -> p (c n)"), psum[:, 6, 0:C * NVEC], ACT.Copy).then_inc(vec_done, 1)
            act_e.wait_ge(tr_dve, NTB)
            hi_run(0, 1)
            norm("n_in", PRE, h, 0, XS0["in"])

            with act_e.Fori(0, C // 2) as i:
                for u in range(2):
                    for j in range(3):
                        nxt = 3 * u + j + 1
                        hi(i * 3 + nxt // 2, nxt % 2)
                    act_e.wait_ge(conv_step, i * (2 * CONV_STEPS) + (u + 1) * CONV_STEPS)
                    m = i * 2 + u
                    A(mix_hi[:, ds(m, 1), :], zconv[:, ds(m, 1), :], ACT.Copy).then_inc(z_hi, 1)
            for j in range(2):
                act_e.wait_ge(conv_tr, j + 1)
                A(conv_rows[:, 512 * j:512 * j + 512], psum[0:2 + 2 * NB, 6 + j, :], ACT.Copy)\
                    .then_inc(conv_rows_done, 1)
            hi_run(SLAB0["out"] + 1, 8)
            norm("n_mix", PAIR, y_mix, ACCS + NT * (BLK0["out"] + 8), XS0["ffn0"])

            def ffn(layer):
                name = f"ffn{layer}"
                n0, b0 = SLAB0[name] // 2, BLK0[name]
                hr0 = layer * 22 * NT

                def gate_up(slab2, blk, chunk):
                    for j in range(2):
                        hi(slab2 + (2 * j + 1) // 2, 1)
                        for t, (t0, n) in enumerate(TILES):
                            act_e.wait_ge(acc_ready, blk * NT + (2 * j * NT + t + 1))
                            act_e.wait_ge(hid_ready, chunk * NT + (j * NT + t + 1))
                            A(act[:, t0:t0 + n], acc(2 * j, t), ACT.Sigmoid).then_inc(sig_ready, 1)
                        hi(slab2 + (2 * j + 2) // 2, 0)
                        for t, (t0, n) in enumerate(TILES):
                            act_e.wait_ge(act_ready, chunk * NT + (j * NT + t + 1))
                            A(hid_hi[gate_up.par][:, j, t0:t0 + n], act[:, t0:t0 + n], ACT.Copy)\
                                .then_inc(hid_hi_ready, 1)

                def down(slab2):
                    hi(slab2, 1)
                    hi(slab2 + 1, 0)

                c0 = layer * 22
                gate_up.par = 0
                gate_up(n0, b0, c0)
                with act_e.Fori(0, 5) as i:
                    gate_up.par = 1
                    gate_up(i * 6 + (n0 + 2), i * 24 + (b0 + 4), i * 4 + (c0 + 2))
                    down(i * 6 + (n0 + 4))
                    gate_up.par = 0
                    gate_up(i * 6 + (n0 + 5), i * 24 + (b0 + 16), i * 4 + (c0 + 4))
                    down(i * 6 + (n0 + 7))
                down(n0 + 32)

            def ple(layer):
                for tb, (t0, n) in enumerate(TOKB):
                    q = layer * NTB + tb
                    act_e.wait_ge(p_tr, q + 1)
                    A(pT_hi[:, :, t0:t0 + n], psum[:, tb % 6, 0:2 * P].rearrange("p (c t) -> p c t", c=2)[:, :, 0:n],
                      ACT.Copy).then_inc(p_hi_ready, 1)
                norm(f"n_ffn{layer}", POST, y, ACCS + NT * BLK0[f"pp{layer}"], XS0[f"pg{layer}"], raw_split=True)
                hi_run(SLAB0[f"pp{layer}"] + 1, 2)
                n0, b0 = SLAB0[f"pg{layer}"], BLK0[f"pg{layer}"]
                for m in range(C):
                    if n0 + m + 1 < SLABS:
                        nxt = n0 + m + 1
                        hi(nxt // 2, nxt % 2, ROW_KV if nxt == SLAB0["k"] else None)
                    for t, (t0, n) in enumerate(TILES):
                        q = (layer * C + m) * NT + t
                        act_e.wait_ge(acc_ready, NT * (b0 + m) + t + 1)
                        act_e.wait_ge(ple_mul, q + 1)
                        A(act[:, t0:t0 + n], acc(b0 + m, t), ACT.Sigmoid).then_inc(ple_sig, 1)

            act_e.wait_ge(conv_stored, 32)
            ffn(0)
            ple(0)

            act_e.wait_ge(ple_added, C * NT)
            norm("n_kv", PRE, h, 0, XS0["kvq"])
            act_e.wait_ge(wf_landed, 32)
            for c in range(C):
                ins = A(wf_hi[:, c, :], wf_raw[:, c, :], ACT.Copy, scale=vecT[:, c, ROW_KV:ROW_KV + 1])
            ins.then_inc(wf_hi_s, 1)
            hi_run(SLAB0["k"] + 1, 15, ROW_KV)
            hi_run(SLAB0["q"], 1, ROW_G + 4)
            act_e.wait_ge(f_z, 1)
            A(lf[:, :, :], lfz[:, :, :], ACT.Abs).then_inc(f_act, 1)
            act_e.wait_ge(f_act, 1)
            A(lf[:, :, :], lf[:, :, :], ACT.Exp, scale=-1.0).then_inc(f_act, 1)
            act_e.wait_ge(f_act, 2)
            A(lf[:, :, :], lf[:, :, :], ACT.Ln, bias=ones[:, :]).then_inc(f_act, 1)
            rows(TR_K, ROWS0[TR_K])
            rows(TR_V, ROWS0[TR_V])
            hi_run(SLAB0["q"] + 1, 7, ROW_G + 4)
            hi_run(SLAB0["o"], 1)
            act_e.wait_ge(acc_free, ACCS + NT * (BLK0["q"] + 8))
            for j, (c0, n, bank) in enumerate(((0, 512, 6), (512, 512, 7), (SEQ, NS, 0))):
                act_e.wait_ge(f_tr, j + 1)
                A(lfT[:, c0:c0 + n], psum[0:H, bank, (0 if j < 2 else P - NS):(n if j < 2 else P)], ACT.Copy)\
                    .then_inc(f_act, 1)

            act_e.sem_inc(exp_done, 4)
            act_e.sem_inc(pt_act, 1)

            def exps(hp, j):
                act_e.wait_ge(s_max, hp * NI + (j + 1))
                jj = j % NI
                if j >= 2:
                    act_e.wait_ge(pt_ready, gcount(hp, groups(j - 2)[-1][0] + 1))
                elif not (isinstance(hp, int) and hp == 0):
                    act_e.wait_ge(pt_ready, hp * 26 + (j - 3))
                A(prob[j % 2][:, 0:(ITEMS[jj][1] + 1) * P], s_view(j), ACT.Exp, bias=nmx[:, j % 4:j % 4 + 1],
                  accum_out=rsum[:, j % 4:j % 4 + 1]).then_inc(exp_done, 1)

            def take_probT(hp, j):
                for g, kb, nb in groups(j):
                    if g % 2 == 0:
                        act_e.wait_ge(pt_ready, gcount(hp, g + 1))
                        act_e.wait_ge(pv_done, hp * NI + (j + 1))
                        A(probT[j % 2][:, kb:kb + nb, :], psum[:, 5, 0:nb * P].rearrange("p (c t) -> p c t", c=nb),
                          ACT.Copy).then_inc(pt_act, 1)

            def take_o(hp, g_ready):
                act_e.wait_ge(pt_ready, g_ready)
                A(y[:, ds(hp, 1), 512:SEQ].rearrange("p o t -> p (o t)"), psum[:, 5, :], ACT.Copy).then_inc(pt_act, 1)

            def pair(hp, first, last):
                for j in range(NI):
                    if not (last and j == NI - 1):
                        exps(hp, j + 1)
                    take_probT(hp, j)
                    if j == 1 and not first:
                        take_o(hp - 1, gcount(hp, OT_AT + 2))

            exps(0, 0)
            pair(0, True, False)
            with act_e.Fori(1, HP - 1) as hp:
                pair(hp, False, False)
            pair(HP - 1, False, True)
            take_o(HP - 1, 26 * HP)

            act_e.sem_inc(st_act, 1 + 2)
            act_e.sem_inc(ss_exp, 2)

            def page_half(pg, count):
                act_e.wait_ge(st_ready, count)
                A(kT[pg // 4][:, 0:4, (pg % 4) * P:(pg % 4 + 1) * P],
                  psum[:, 4, :].rearrange("p (c t) -> p c t", c=4), ACT.Copy).then_inc(st_act, 1)

            def sample_exps(b, par):
                act_e.wait_ge(ss_max, b + 1)
                A(sprob[:, 0:NK], psum[:, 2 * par:2 * par + 2, :].rearrange("p a b -> p (a b)"), ACT.Exp,
                  bias=sstat[:, 2:3], accum_out=sstat[:, 3:4]).then_inc(ss_exp, 1)
                A(sprob[:, NK:NK + NS], psum[:, 6, 0:NS], ACT.Exp,
                  bias=sstat[:, 2:3], accum_out=sstat[:, 4:5]).then_inc(ss_exp, 1)

            def sample_probT(b, count):
                act_e.wait_ge(spv_done, b * 2 + 2)
                act_e.wait_ge(st_ready, count + 1)
                A(sprobT[:, 0:4, :], psum[:, 4, :].rearrange("p (c t) -> p c t", c=4), ACT.Copy).then_inc(st_act, 1)
                act_e.wait_ge(st_ready, count + 3)
                A(sprobT[0:NS, 8, :], psum[0:NS, 4, 0:P], ACT.Copy).then_inc(st_act, 1)

            def out_rows(b):
                act_e.wait_ge(spv_done, b * 2 + 3)
                A(o_rows[:, 0:512], psum[:, 6, :], ACT.Copy, scale=sstat[:, 6:7]).then_inc(so_rows, 1)

            def out_back(b):
                act_e.wait_ge(so_tr, b * 2 + 2)
                cols = ds(b * NQ + SEQ, NQ)
                po = psum[:, 6, :].rearrange("p (c n) -> p c n", c=4)
                A(y[0:DH, 0:4, cols], po[0:DH, :, 0:NQ], ACT.Copy).then_inc(so_taken, 1)
                A(y[DH:P, 0:4, cols], po[DH:P, :, NQ:2 * NQ], ACT.Copy).then_inc(so_taken, 1)

            def next_in(b, count):
                act_e.wait_ge(st_ready, count + 1)
                if not (isinstance(b, int) and b == 0):
                    act_e.wait_ge(cum_ready, b)
                A(lf_pageT[:, 0:512], psum[0:H, 4, :], ACT.Copy).then_inc(st_act, 1)
                for pg in range(4):
                    page_half(pg, count + (3 + 2 * pg))
                    if pg == 0 and not (isinstance(b, int) and b < 2):
                        out_back(b - 2)

            def sequence(b, par, first, last):
                n0 = st_before(b)[0]
                for pg in range(4, 8):
                    page_half(pg, n0 + (2 * (pg - 4) + 1))
                    if pg == 5 and not first:
                        sample_exps(b - 1, 1 - par)
                if not first:
                    sample_probT(b - 1, n0 + 8)
                    out_rows(b - 1)
                if not last:
                    next_in(b + 1, st_mid(b, first)[0])

            next_in(0, 3)
            sequence(0, 0, True, False)
            with act_e.Fori(0, NB // 2 - 1) as i:
                sequence(i * 2 + 1, 1, False, False)
                sequence(i * 2 + 2, 0, False, False)
            sequence(NB - 1, 1, False, True)
            out_back(NB - 2)
            sample_exps(NB - 1, 1)
            sample_probT(NB - 1, 21 * NB)
            out_rows(NB - 1)
            out_back(NB - 1)

            act_e.wait_ge(so_taken, 4 * NB)
            for t, (t0, n) in enumerate(TILES):
                A(xs_hi[:, :, t0:t0 + n], y[:, :, t0:t0 + n], ACT.Copy).then_inc(xs_hi_ready, 1)
            hi_run(SLAB0["o"] + 1, 8)
            norm("n_att", PAIR, y, ACCS + NT * (BLK0["o"] + 8), XS0["ffn1"])
            ffn(1)
            ple(1)
            act_e.wait_ge(ple_added, 2 * C * NT)
            rows(TR_Y, ROWS0[TR_Y])

        @block.vector
        def _(dve):
            V = nc.vector

            def copy(out, in_):
                return V.tensor_scalar(out, in_, 1.0, None, ALU.mult)

            def lo(n2, slot, gain=None):
                dve.wait_ge(hi_ready, n2 * 2 + (slot + 1))
                if gain is None:
                    V.tensor_tensor(w_lo[slot][:, :], raw[slot][:, :], w_hi[slot][:, :].bitcast(F32), ALU.subtract)\
                        .then_inc(lo_ready, 1)
                else:
                    for c in range(C):
                        part = slice(c * P, (c + 1) * P)
                        ins = V.scalar_tensor_tensor(w_lo[slot][:, part], raw[slot][:, part],
                                                     vecT[:, c, gain:gain + 1], w_hi[slot][:, part].bitcast(F32),
                                                     ALU.mult, ALU.subtract)
                    ins.then_inc(lo_ready, 1)

            def lo_run(n, count, gain=None):
                for j in range(n, n + count):
                    lo(j // 2, j % 2, gain)

            def tile_ready(blk, t, last=False):
                dve.wait_ge(acc_ready, blk * NT + (t + 1))
                if last:
                    dve.sem_inc(slab_used, 1)

            def norm(name, seq, ysrc, post_row, pre_row, xs0, raw_split=False):
                s0, pending = STEP0[name], None
                for k, (kind, t) in enumerate(seq):
                    s = s0 + k
                    t0, n = TILES[t]
                    dve.wait_ge(std_ready, s + 1)
                    V.reciprocal(rcol[:, :], stdc[:, :]).then_inc(rcol_ready, 1)
                    if kind == "pre" and t == 2:
                        dve.wait_ge(xs_ready, xs0 + 1)
                    dve.wait_ge(rb_ready, s + 1)
                    rb = psum[:, 7, 0:n]
                    for c in range(C):
                        if kind == "post":
                            ins = V.scalar_tensor_tensor(ysrc[:, c, t0:t0 + n], ysrc[:, c, t0:t0 + n],
                                                         vecT[:, c, post_row:post_row + 1], rb, ALU.mult, ALU.mult)
                        elif pre_row is not None:
                            ins = V.scalar_tensor_tensor(xn[t % 2][:, c, 0:n], h[:, c, t0:t0 + n],
                                                         vecT[:, c, pre_row:pre_row + 1], rb, ALU.mult, ALU.mult)
                        else:
                            ins = V.tensor_tensor(xn[t % 2][:, c, 0:n], h[:, c, t0:t0 + n], rb, ALU.mult)
                    ins.then_inc(rb_used, 1)
                    if kind == "post":
                        dve.wait_ge(rb_used, s + 1)
                        V.tensor_tensor(h[:, :, t0:t0 + n], h[:, :, t0:t0 + n], ysrc[:, :, t0:t0 + n], ALU.add)\
                            .then_inc(h_ready, 1)
                    if pending is not None:
                        pending()
                        pending = None
                    if kind == "pre" or raw_split:
                        src = xn[t % 2][:, :, 0:n] if kind == "pre" else h[:, :, t0:t0 + n]

                        def pending(t=t, t0=t0, n=n, src=src):
                            dve.wait_ge(xs_hi_ready, xs0 + t + 1)
                            V.tensor_tensor(xs_lo[:, :, t0:t0 + n], src, xs_hi[:, :, t0:t0 + n].bitcast(F32),
                                            ALU.subtract).then_inc(xs_ready, 1)
                if pending is not None:
                    pending()

            dve.sem_inc(acc_free, ACCS)
            dve.sem_inc(lo_ready, RAWS)
            dve.sem_inc(slab_used, HLS)
            dve.sem_inc(hid_ready, NT)
            dve.sem_inc(ple_mul, NT)
            for tb, (t0, n) in enumerate(TOKB):
                dve.wait_ge(tr_ready, 2 * (TR_X + tb) + 2)
                bank = 2 * (tb % 3) + 1
                V.tensor_copy(h[:, 4:8, t0:t0 + n], psum[:, bank, :].rearrange("p (c t) -> p c t", c=4)[:, :, 0:n])\
                    .then_inc(tr_dve, 1)

            def rows(tr0, r0):
                for tb, (t0, n) in enumerate(TOKB):
                    g, r = tr0 + tb, r0 + tb
                    dve.wait_ge(tr_ready, 2 * g + 2)
                    if r >= 2:
                        dve.wait_ge(rows_stored[r % 2], 16 * (r // 2))
                    V.tensor_copy(rows_out[r % 2][0:n, 512:D], psum[0:n, 2 * (g % 3) + 1, :]).then_inc(tr_dve, 1)

            dve.wait_ge(vec_done, 1)
            lo_run(0, 1)
            dve.wait_ge(tr_act, NTB)
            dve.wait_ge(tr_dve, NTB)
            norm("n_in", PRE, None, None, ROW_G + 0, XS0["in"])

            V.memset(cup[:, 0:2], 0.0).then_inc(conv_step, 1)
            with dve.Fori(0, C // 2) as i:
                for u in range(2):
                    m = i * 2 + u
                    mm = ds(m, 1)
                    base = i * (2 * CONV_STEPS) + u * CONV_STEPS + 1
                    done = [0]

                    def step(ins):
                        ins.then_inc(conv_step, 1)
                        done[0] += 1

                    def after(k):
                        dve.wait_ge(conv_step, base + k)

                    def f(t):
                        return t.rearrange("p o t -> p (o t)")

                    blk = i * 6 + 3 * u
                    for part, dst in enumerate((bgate, zconv)):
                        nxt = 3 * u + part + 1
                        lo(i * 3 + nxt // 2, nxt % 2)
                        for t, (t0, n) in enumerate(TILES):
                            tile_ready(blk + part, t, t == NT - 1)
                            copy(f(dst[:, mm, t0:t0 + n]), acc(3 * u + part, t)).then_inc(acc_free, 1)
                    nxt = 3 * u + 3
                    lo(i * 3 + nxt // 2, nxt % 2)
                    dve.wait_ge(conv_step, base)
                    dve.wait_ge(acc_free, blk * NT + (ACCS + 2 * NT))
                    for t, (t0, n) in enumerate(TILES):
                        tile_ready(blk + 2, t, t == NT - 1)
                        np_ = min(t0 + n, SEQ) - t0
                        ins = V.tensor_tensor(cup[:, 2 + t0:2 + t0 + np_], f(zconv[:, mm, t0:t0 + np_]),
                                              acc(3 * u + 2, t)[:, 0:np_], ALU.mult)
                        if np_ < n:
                            step(ins)
                            ins = V.tensor_tensor(cup_s[:, :, 2:], f(zconv[:, mm, SEQ:T]).rearrange("p (b t) -> p b t", b=NB),
                                                  acc(3 * u + 2, t)[:, np_:n].rearrange("p (b t) -> p b t", b=NB), ALU.mult)
                        ins.then_inc(acc_free, 1)
                    step(copy(cup_s[:, :, 0:2], f(vecT[:, mm, ROW_STATE:ROW_STATE + 2 * NB])
                                       .rearrange("p (b t) -> p b t", b=NB)))
                    after(2)
                    dve.wait_ge(acc_free, blk * NT + (ACCS + 3 * NT))
                    step(copy(f(convT[:, mm, 0:2]), cup[:, SEQ:SEQ + 2]))
                    step(copy(f(convT[:, mm, 2:]).rearrange("p (b t) -> p b t", b=NB),
                                       cup_s[:, :, NQ:NQ + 2]))
                    zp = f(zconv[:, mm, 0:SEQ])
                    zs = f(zconv[:, mm, SEQ:T]).rearrange("p (b t) -> p b t", b=NB)
                    for k in range(3):
                        wk = vecT[:, mm, ROW_CONV + k:ROW_CONV + k + 1].rearrange("p a b -> p (a b)")
                        if k == 0:
                            step(V.tensor_scalar(zp, cup[:, 0:SEQ], wk, None, ALU.mult))
                            step(V.tensor_scalar(zs, cup_s[:, :, 0:NQ], wk, None, ALU.mult))
                        else:
                            after(4 + 2 * k)
                            step(V.scalar_tensor_tensor(zp, cup[:, k:k + SEQ], wk, zp, ALU.mult, ALU.add))
                            step(V.scalar_tensor_tensor(zs, cup_s[:, :, k:k + NQ], wk, zs, ALU.mult, ALU.add))
                    after(10)
                    step(V.tensor_tensor(f(zconv[:, mm, 0:544]), f(zconv[:, mm, 0:544]), f(bgate[:, mm, 0:544]), ALU.mult))
                    step(V.tensor_tensor(f(zconv[:, mm, 544:T]), f(zconv[:, mm, 544:T]), f(bgate[:, mm, 544:T]), ALU.mult))
                    assert done[0] == 12
                    dve.sem_inc(conv_step, CONV_STEPS - 12 - 1) if CONV_STEPS > 13 else None
                    after(CONV_STEPS - 1)
                    dve.sem_inc(conv_step, 1)
                    dve.wait_ge(z_hi, i * 2 + (u + 1))
                    V.tensor_tensor(f(mix_lo[:, mm, :]), f(zconv[:, mm, :]), f(mix_hi[:, mm, :]).bitcast(F32), ALU.subtract)\
                        .then_inc(mix_ready, 1)

            def plain(name, dst, gain_next, last_gain=None, scale=None, last=True, gain=None):
                n0, b0 = SLAB0[name], BLK0[name]
                for m in range(C):
                    if m < C - 1:
                        lo_run(n0 + m + 1, 1, gain)
                    elif gain_next != "none":
                        lo_run(n0 + m + 1, 1, gain_next)
                    for t, (t0, n) in enumerate(TILES):
                        tile_ready(b0 + m, t, t == NT - 1)
                        if scale is None:
                            V.tensor_copy(dst[:, m, t0:t0 + n], acc(b0 + m, t)).then_inc(acc_free, 1)
                        else:
                            V.tensor_scalar(dst[:, m, t0:t0 + n], acc(b0 + m, t), scale, None, ALU.mult)\
                                .then_inc(acc_free, 1)

            plain("out", y_mix, None)
            dve.wait_ge(acc_free, ACCS + NT * (BLK0["out"] + 8))
            norm("n_mix", PAIR, y_mix, ROW_G + 1, ROW_G + 2, XS0["ffn0"])

            def ffn(layer):
                name = f"ffn{layer}"
                n0, b0, c0 = SLAB0[name] // 2, BLK0[name], layer * 22

                def gate_up(slab2, blk, chunk, par):
                    for j in range(2):
                        lo(slab2 + (2 * j + 1) // 2, 1)
                        for t, (t0, n) in enumerate(TILES):
                            tile_ready(blk + 2 * j, t, t == NT - 1)
                            dve.wait_ge(sig_ready, chunk * NT + (j * NT + t + 1))
                            V.tensor_tensor(act[:, t0:t0 + n], act[:, t0:t0 + n], acc(2 * j, t), ALU.mult)\
                                .then_inc(acc_free, 1)
                        lo(slab2 + (2 * j + 2) // 2, 0)
                        dve.wait_ge(acc_free, blk * NT + (ACCS + (2 * j + 1) * NT))
                        for t in range(NT + 1):
                            if t < NT:
                                t0, n = TILES[t]
                                tile_ready(blk + 2 * j + 1, t, t == NT - 1)
                                V.tensor_tensor(act[:, t0:t0 + n], act[:, t0:t0 + n], acc(2 * j + 1, t), ALU.mult)\
                                    .then_inc(act_ready, 1)
                                dve.wait_ge(act_ready, chunk * NT + (j * NT + t + 1))
                                dve.sem_inc(acc_free, 1)
                            if t > 0:
                                t0, n = TILES[t - 1]
                                dve.wait_ge(hid_hi_ready, chunk * NT + (j * NT + t))
                                V.tensor_tensor(hid_lo[par][:, j, t0:t0 + n], act[:, t0:t0 + n],
                                                hid_hi[par][:, j, t0:t0 + n].bitcast(F32), ALU.subtract)\
                                    .then_inc(hid_ready, 1)

                def down(slab2, blk, gain=None, split_next=True):
                    for s in range(2):
                        if s == 0:
                            lo(slab2, 1)
                        elif split_next:
                            lo(slab2 + 1, 0, gain)
                        if s == 0:
                            dve.wait_ge(acc_free, blk * NT + ACCS)
                        for m in range(4):
                            for t, (t0, n) in enumerate(TILES):
                                tile_ready(blk + 4 * s + m, t, m == 3 and t == NT - 1)
                                yy = y[:, 4 * s + m, t0:t0 + n]
                                V.tensor_tensor(yy, yy, acc(m, t), ALU.add).then_inc(acc_free, 1)

                gate_up(n0, b0, c0, 0)
                dve.wait_ge(y_zero, layer + 1)
                with dve.Fori(0, 5) as i:
                    gate_up(i * 6 + (n0 + 2), i * 24 + (b0 + 4), i * 4 + (c0 + 2), 1)
                    down(i * 6 + (n0 + 4), i * 24 + (b0 + 8))
                    gate_up(i * 6 + (n0 + 5), i * 24 + (b0 + 16), i * 4 + (c0 + 4), 0)
                    down(i * 6 + (n0 + 7), i * 24 + (b0 + 20))
                down(n0 + 32, b0 + 124)

            def ple(layer):
                for tb, (t0, n) in enumerate(TOKB):
                    dve.wait_ge(p_hi_ready, layer * NTB + tb + 1)
                    V.tensor_tensor(pT_lo[:, :, t0:t0 + n],
                                    psum[:, tb % 6, 0:2 * P].rearrange("p (c t) -> p c t", c=2)[:, :, 0:n],
                                    pT_hi[:, :, t0:t0 + n].bitcast(F32), ALU.subtract).then_inc(p_ready, 1)
                dve.wait_ge(acc_free, ACCS + NT * BLK0[f"pp{layer}"])
                norm(f"n_ffn{layer}", POST, y, ROW_G + 4 * layer + 3, None, XS0[f"pg{layer}"], raw_split=True)
                n0, b0 = SLAB0[f"pp{layer}"], BLK0[f"pp{layer}"]
                for m in range(C):
                    if m % 4 == 0:
                        lo_run(n0 + m // 4 + 1, 1)
                    for t, (t0, n) in enumerate(TILES):
                        tile_ready(b0 + m, t, m % 4 == 3 and t == NT - 1)
                        V.tensor_copy(y[:, m, t0:t0 + n], acc(m, t)).then_inc(acc_free, 1)
                dve.wait_ge(acc_free, ACCS + NT * (b0 + C))
                n0, b0 = SLAB0[f"pg{layer}"], BLK0[f"pg{layer}"]
                for m in range(C):
                    if n0 + m + 1 < SLABS:
                        lo_run(n0 + m + 1, 1, ROW_KV if n0 + m + 1 == SLAB0["k"] else None)
                    for t, (t0, n) in enumerate(TILES):
                        q = (layer * C + m) * NT + t
                        tile_ready(b0 + m, t, t == NT - 1)
                        dve.wait_ge(ple_sig, q + 1)
                        dve.sem_inc(acc_free, 1)
                        V.tensor_tensor(y[:, m, t0:t0 + n], act[:, t0:t0 + n], y[:, m, t0:t0 + n], ALU.mult)\
                            .then_inc(ple_mul, 1)
                        dve.wait_ge(ple_mul, NT + q + 1)
                        V.tensor_tensor(h[:, m, t0:t0 + n], h[:, m, t0:t0 + n], y[:, m, t0:t0 + n], ALU.add)\
                            .then_inc(ple_added, 1)

            ffn(0)
            ple(0)
            dve.wait_ge(ple_added, C * NT)
            norm("n_kv", PRE, None, None, None, XS0["kvq"])
            dve.wait_ge(wf_hi_s, 1)
            for c in range(C):
                ins = V.scalar_tensor_tensor(wf_lo[:, c, :], wf_raw[:, c, :], vecT[:, c, ROW_KV:ROW_KV + 1],
                                             wf_hi[:, c, :].bitcast(F32), ALU.mult, ALU.subtract)
            ins.then_inc(wf_lo_s, 1)
            plain("k", y, ROW_KV, gain=ROW_KV)
            plain("v", vT, ROW_G + 4, gain=ROW_KV)
            dve.wait_ge(f_acc, 1)
            V.tensor_tensor(lfz[:, :, :], psum[:, 6, 0:NTB * H].rearrange("p (b n) -> p b n", b=NTB),
                            bf[:, :].unsqueeze(1).broadcast_to([P, NTB, H]), ALU.add).then_inc(f_z, 1)
            dve.wait_ge(f_act, 3)
            V.scalar_tensor_tensor(lf[:, :, :], lfz[:, :, :], 0.0, lf[:, :, :], ALU.min, ALU.subtract)\
                .then_inc(f_step, 1)
            rows(TR_K, ROWS0[TR_K])
            rows(TR_V, ROWS0[TR_V])
            dve.wait_ge(kT_stored, 16)
            plain("q", y, None, scale=SCALE, gain=ROW_G + 4)
            V.memset(segm[:, :], 1.0).then_inc(f_step, 1)
            V.memset(one16[:, :], 1.0).then_inc(f_step, 1)
            dve.wait_ge(f_step, 3)
            V.memset(segm[:, :].rearrange("p (b t) -> p b t", b=NB)[:, :, 0:1], 0.0).then_inc(f_step, 1)
            dve.wait_ge(f_act, 6)
            dve.wait_ge(f_step, 4)
            V.tensor_tensor_scan(fsum[:, 0:SEQ], one16[:, :].broadcast_to([H, SEQ]), lfT[:, 0:SEQ], 0.0,
                                 ALU.mult, ALU.add).then_inc(f_step, 1)
            dve.wait_ge(f_step, 5)
            V.tensor_scalar(nfsum[:, 0:SEQ], fsum[:, 0:SEQ], -1.0, None, ALU.mult).then_inc(f_step, 1)
            V.tensor_tensor_scan(fsum_new[:, :], segm[:, :], lfT[:, SEQ:T], 0.0, ALU.mult, ALU.add)\
                .then_inc(f_step, 1)
            dve.sem_inc(pt_dve, 1)
            dve.sem_inc(o_taken, 1)

            def maxes(hp, j):
                dve.wait_ge(s_ready, hp * NI + (j + 1))
                V.reduce_max(nmx[:, j % 4:j % 4 + 1], s_view(j), AX_X, negate=True).then_inc(s_max, 1)

            def take_probT(hp, j):
                for g, kb, nb in groups(j):
                    if g % 2:
                        dve.wait_ge(pt_ready, gcount(hp, g + 1))
                        dve.wait_ge(pv_done, hp * NI + (j + 1))
                        V.tensor_copy(probT[j % 2][:, kb:kb + nb, :],
                                      psum[:, 6, 0:nb * P].rearrange("p (c t) -> p c t", c=nb)).then_inc(pt_dve, 1)

            def normed(hp, j):
                it = hp * NI
                hh, qb = ITEMS[j]
                dve.wait_ge(exp_done, it + (j + 5))
                V.reciprocal(rinv[:, j % 2:j % 2 + 1], rsum[:, j % 4:j % 4 + 1]).then_inc(rinv_s, 1)
                dve.wait_ge(rinv_s, it + (j + 1))
                dve.wait_ge(pv_done, it + (j + 3))
                V.tensor_scalar(o_pair[:, qb, DH * hh:DH * hh + DH], psum[:, 7, 0:DH], rinv[:, j % 2:j % 2 + 1],
                                None, ALU.mult).then_inc(o_taken, 1)

            def take_o(hp, g_ready):
                dve.wait_ge(pt_ready, g_ready)
                V.tensor_scalar(y[:, ds(hp, 1), 0:512].rearrange("p o t -> p (o t)"), psum[:, 6, :], 1.0, None,
                                ALU.mult).then_inc(pt_dve, 1)

            def pair(hp, first, last):
                for j in range(NI):
                    if not (last and j >= NI - 2):
                        maxes(hp, j + 2)
                    take_probT(hp, j)
                    if j == 1 and not first:
                        take_o(hp - 1, gcount(hp, OT_AT + 1))
                        dve.wait_ge(pt_ready, gcount(hp, OT_AT + 2))
                    if j > 0:
                        normed(hp, j - 1)
                    elif not first:
                        normed(hp - 1, NI - 1)

            maxes(0, 0)
            maxes(0, 1)
            pair(0, True, False)
            with dve.Fori(1, HP - 1) as hp:
                pair(hp, False, False)
            pair(HP - 1, False, True)
            normed(HP - 1, NI - 1)
            take_o(HP - 1, 26 * HP - 1)

            dve.sem_inc(st_dve, 1 + 1)
            dve.sem_inc(kpage_used, 4)

            def page_half(pg, count):
                dve.wait_ge(st_ready, count)
                dve.sem_inc(kpage_used, 1)
                V.tensor_copy(kT[pg // 4][:, 4:8, (pg % 4) * P:(pg % 4 + 1) * P],
                              psum[:, 5, :].rearrange("p (c t) -> p c t", c=4)).then_inc(st_dve, 1)

            def queries(b, par):
                cols = ds(b * NQ + SEQ, NQ)
                copy(qdiag[par][0:DH, :, 0:NQ], y[0:DH, :, cols]).then_inc(qbd_ready, 1)
                copy(qdiag[par][DH:P, :, NQ:2 * NQ], y[DH:P, :, cols]).then_inc(qbd_ready, 1)

            def sample_max(b, par):
                dve.wait_ge(ss_ready, b + 1)
                V.reduce_max(sstat[:, 0:1], psum[:, 2 * par:2 * par + 2, :].rearrange("p a b -> p (a b)"), AX_X,
                             negate=True).then_inc(sp_step, 1)
                V.reduce_max(sstat[:, 1:2], psum[:, 6, 0:NS], AX_X, negate=True).then_inc(sp_step, 1)
                dve.wait_ge(sp_step, b * 4 + 2)
                V.tensor_tensor(sstat[:, 2:3], sstat[:, 0:1], sstat[:, 1:2], ALU.min).then_inc(ss_max, 1)

            def row_sums(b):
                dve.wait_ge(ss_exp, b * 2 + 4)
                V.tensor_tensor(sstat[:, 5:6], sstat[:, 3:4], sstat[:, 4:5], ALU.add).then_inc(sp_step, 1)
                dve.wait_ge(sp_step, b * 4 + 3)
                V.reciprocal(sstat[:, 6:7], sstat[:, 5:6]).then_inc(sp_step, 1)

            def sample_out(b, count):
                dve.wait_ge(spv_done, b * 2 + 2)
                dve.wait_ge(st_ready, count + 2)
                V.tensor_copy(sprobT[:, 4:8, :], psum[:, 5, :].rearrange("p (c t) -> p c t", c=4)).then_inc(st_dve, 1)
                dve.wait_ge(spv_done, b * 2 + 4)
                V.tensor_scalar(o_rows[:, 512:1024], psum[:, 7, :], sstat[:, 6:7], None, ALU.mult).then_inc(so_rows, 1)

            def out_back(b):
                dve.wait_ge(so_tr, b * 2 + 2)
                cols = ds(b * NQ + SEQ, NQ)
                po = psum[:, 7, :].rearrange("p (c n) -> p c n", c=4)
                copy(y[0:DH, 4:8, cols], po[0:DH, :, DH:DH + NQ]).then_inc(so_taken, 1)
                copy(y[DH:P, 4:8, cols], po[DH:P, :, DH + NQ:DH + 2 * NQ]).then_inc(so_taken, 1)

            def next_in(b, par, count, act_count, dve_count):
                dve.wait_ge(st_ready, count + 2)
                if not (isinstance(b, int) and b == 0):
                    dve.wait_ge(cum_ready, b)
                V.tensor_copy(lf_pageT[:, 512:1024], psum[0:H, 5, :]).then_inc(st_dve, 1)
                for pg in range(4):
                    page_half(pg, count + (4 + 2 * pg))
                    if pg == 0:
                        dve.wait_ge(st_act, act_count + 2)
                        dve.wait_ge(st_dve, dve_count + 2)
                        V.tensor_tensor_scan(cum[:, :], one16[:, :].broadcast_to([H, NK]), lf_pageT[:, :], 0.0,
                                             ALU.mult, ALU.add).then_inc(cum_ready, 1)
                    elif pg == 1:
                        dve.wait_ge(cum_ready, b + 1)
                        V.tensor_scalar(cum_new[par][:, :], fsum_new[:, :], cum[:, NK - 1:NK], None, ALU.add)\
                            .then_inc(fb_ready, 1)
                    if pg == 0 and not (isinstance(b, int) and b < 2):
                        out_back(b - 2)

            def sequence(b, par, first, last):
                n0 = st_before(b)[0]
                for pg in range(4, 8):
                    page_half(pg, n0 + (2 * (pg - 4) + 2))
                    if pg == 4 and not first:
                        sample_max(b - 1, 1 - par)
                    elif pg == 6 and not first:
                        row_sums(b - 1)
                if not last:
                    queries(b + 1, 1 - par)
                if not first:
                    sample_out(b - 1, n0 + 8)
                if not last:
                    next_in(b + 1, 1 - par, *st_mid(b, first))

            dve.wait_ge(qbd_zero, 2)
            queries(0, 0)
            next_in(0, 0, 3, 2, 1)
            sequence(0, 0, True, False)
            with dve.Fori(0, NB // 2 - 1) as i:
                sequence(i * 2 + 1, 1, False, False)
                sequence(i * 2 + 2, 0, False, False)
            sequence(NB - 1, 1, False, True)
            out_back(NB - 2)
            sample_max(NB - 1, 1)
            row_sums(NB - 1)
            sample_out(NB - 1, 21 * NB)
            out_back(NB - 1)

            for t, (t0, n) in enumerate(TILES):
                dve.wait_ge(xs_hi_ready, XS0["o"] + t + 1)
                if t == 0:
                    dve.wait_ge(so_taken, 4 * NB)
                V.tensor_tensor(xs_lo[:, :, t0:t0 + n], y[:, :, t0:t0 + n], xs_hi[:, :, t0:t0 + n].bitcast(F32),
                                ALU.subtract).then_inc(xs_ready, 1)
            plain("o", y, None)
            dve.wait_ge(acc_free, ACCS + NT * (BLK0["o"] + 8))
            norm("n_att", PAIR, y, ROW_G + 5, ROW_G + 6, XS0["ffn1"])
            ffn(1)
            ple(1)
            dve.wait_ge(ple_added, 2 * C * NT)
            rows(TR_Y, ROWS0[TR_Y])

        @block.tensor
        def _(pe):
            M = nc.tensor.matmul

            def three(out, wh, wl, xh, xl, first, last):
                M(out, wh, xh, start=first, stop=False)
                M(out, wh, xl, start=False, stop=False)
                return M(out, wl, xh, start=False, stop=last)

            def slab(n, slot):
                pe.wait_ge(lo_ready, n + (RAWS + 1))

            def block8(blk, par, slot, xh, xl, xs0=None):
                for t, (t0, n) in enumerate(TILES):
                    pe.wait_ge(acc_free, blk * NT + (t + 1))
                    if xs0 is not None:
                        pe.wait_ge(xs_ready, xs0 + t + 1)
                    for c in range(C):
                        k = slice(c * P, (c + 1) * P)
                        ins = three(acc(par, t), w_hi[slot][:, k], w_lo[slot][:, k],
                                    xh[:, c, t0:t0 + n], xl[:, c, t0:t0 + n], c == 0, c == C - 1)
                    ins.then_inc(acc_ready, 1)

            def transposes_in(tr0, src_of):
                for tb, (t0, n) in enumerate(TOKB):
                    g = tr0 + tb
                    if g >= 3:
                        pe.wait_ge(tr_act, g - 2)
                        pe.wait_ge(tr_dve, g - 2)
                    for half in range(2):
                        for c in range(4):
                            ins = src_of(tb, t0, n, half, c, 2 * (g % 3) + half)
                        ins.then_inc(tr_ready, 1)

            def norm(name, seq):
                s0 = STEP0[name]
                for k in range(len(seq)):
                    s = s0 + k
                    if s:
                        pe.wait_ge(std_ready, s)
                    for j in range(3):
                        q = 3 * s + j
                        pe.wait_ge(sq_ready, q + 1)
                        for c in range(C):
                            ins = M(psum[:, 6, j:j + 1], sqb[q % 2][:, c, :], ones[:, :], start=c == 0, stop=c == C - 1)
                        ins.then_inc(sq_used, 1)
                    pe.wait_ge(rcol_ready, s + 1)
                    if s:
                        pe.wait_ge(rb_used, s)
                    t = seq[k][1]
                    for t0, j in SQB[t]:
                        o = t0 - TILES[t][0]
                        ins = M(psum[:, 7, o:o + P], rcol[:, j:j + 1].broadcast_to([P, P]), ident[:, :],
                                start=True, stop=True)
                    ins.then_inc(rb_ready, 1)

            pe.sem_inc(sq_used, 2)
            pe.wait_ge(consts, 4)
            def x_in(tb, t0, n, half, c, bank):
                src = x_nat[:, tb, :] if tb < 8 else xs_nat[:, :]
                if half == 0 and c == 0:
                    pe.wait_ge(x_landed[tb], 16)
                f0 = (4 * half + c) * P
                return nc.tensor.transpose(psum[:, bank, c * P:c * P + n], src[:, f0:f0 + P], ident[0:n, 0:n])
            transposes_in(TR_X, x_in)
            pe.wait_ge(vec_landed, 64)
            for c in range(C):
                ins = nc.tensor.transpose(psum[:, 6, c * NVEC:(c + 1) * NVEC], vec_nat[:, c * P:(c + 1) * P],
                                          ident[0:NVEC, 0:NVEC])
            ins.then_inc(vec_tr, 1)
            pe.wait_ge(vec_done, 1)
            pe.wait_ge(tr_act, NTB)
            pe.wait_ge(tr_dve, NTB)
            norm("n_in", PRE)

            with pe.Fori(0, C // 2) as i:
                for u in range(6):
                    slab(i * 6 + u, u % 2)
                    block8(i * 6 + u, u, u % 2, xs_hi, xs_lo, XS0["in"])
            pe.wait_ge(mix_ready, C)
            for c in range(C):
                ins = nc.tensor.transpose(psum[0:2 + 2 * NB, 6 + c // 4, (c % 4) * P:(c % 4 + 1) * P],
                                          convT[:, c, :], ident[:, :])
                if c % 4 == 3:
                    ins.then_inc(conv_tr, 1)

            def plain(name, xh, xl, xs0=None):
                for m in range(C):
                    slab(SLAB0[name] + m, m % 2)
                    block8(BLK0[name] + m, m, m % 2, xh, xl, xs0)

            plain("out", mix_hi, mix_lo)
            pe.wait_ge(conv_rows_done, 2)
            norm("n_mix", PAIR)

            def ffn(layer):
                name = f"ffn{layer}"
                n0, b0, c0 = SLAB0[name], BLK0[name], layer * 22

                def gate_up(n, blk):
                    for u in range(4):
                        slab(n + u, u % 2)
                        block8(blk + u, u, u % 2, xs_hi, xs_lo, XS0[name])

                def down(n, blk, chunks, par):
                    pe.wait_ge(hid_ready, chunks * NT + NT)
                    for s in range(2):
                        slab(n + s, s)
                        for m in range(4):
                            for t, (t0, nn) in enumerate(TILES):
                                pe.wait_ge(acc_free, blk * NT + ((4 * s + m) * NT + t + 1))
                                for c in range(2):
                                    k = slice(c * 512 + m * P, c * 512 + (m + 1) * P)
                                    ins = three(acc(m, t), w_hi[s][:, k], w_lo[s][:, k],
                                                hid_hi[par][:, c, t0:t0 + nn], hid_lo[par][:, c, t0:t0 + nn],
                                                c == 0, c == 1)
                                ins.then_inc(acc_ready, 1)

                gate_up(n0, b0)
                with pe.Fori(0, 5) as i:
                    gate_up(i * 12 + (n0 + 4), i * 24 + (b0 + 4))
                    down(i * 12 + (n0 + 8), i * 24 + (b0 + 8), i * 4 + (c0 + 2), 0)
                    gate_up(i * 12 + (n0 + 10), i * 24 + (b0 + 16))
                    down(i * 12 + (n0 + 14), i * 24 + (b0 + 20), i * 4 + (c0 + 4), 1)
                down(n0 + 64, b0 + 124, c0 + 22, 0)

            def ple(layer):
                pe.wait_ge(p_landed, 16 * NTB * (layer + 1))
                pe.wait_ge(acc_free, ACCS + NT * BLK0[f"pp{layer}"])
                for tb, (t0, n) in enumerate(TOKB):
                    if tb >= 6:
                        pe.wait_ge(p_ready, layer * NTB + tb - 5)
                    for c in range(2):
                        ins = nc.tensor.transpose(psum[:, tb % 6, c * P:c * P + n], p_nat[0:n, tb, c * P:(c + 1) * P],
                                                  ident[0:n, 0:n])
                    ins.then_inc(p_tr, 1)
                norm(f"n_ffn{layer}", POST)
                pe.wait_ge(p_ready, (layer + 1) * NTB)
                n0, b0 = SLAB0[f"pp{layer}"], BLK0[f"pp{layer}"]
                for m in range(C):
                    if m % 4 == 0:
                        slab(n0 + m // 4, m // 4)
                    for t, (t0, n) in enumerate(TILES):
                        pe.wait_ge(acc_free, NT * (b0 + m) + t + 1)
                        for c in range(2):
                            k = slice(c * 512 + (m % 4) * P, c * 512 + (m % 4 + 1) * P)
                            ins = three(acc(m, t), w_hi[m // 4][:, k], w_lo[m // 4][:, k],
                                        pT_hi[:, c, t0:t0 + n], pT_lo[:, c, t0:t0 + n], c == 0, c == 1)
                        ins.then_inc(acc_ready, 1)
                plain(f"pg{layer}", xs_hi, xs_lo, XS0[f"pg{layer}"])

            ffn(0)
            ple(0)
            norm("n_kv", PRE)
            plain("k", xs_hi, xs_lo, XS0["kvq"])
            plain("v", xs_hi, xs_lo)
            pe.wait_ge(wf_lo_s, 1)
            for tb in range(8):
                t0 = tb * P
                for c in range(C):
                    ins = three(psum[:, 6, tb * H:(tb + 1) * H], xs_hi[:, c, t0:t0 + P], xs_lo[:, c, t0:t0 + P],
                                wf_hi[:, c, :], wf_lo[:, c, :], c == 0, c == C - 1)
            for c in range(C):
                ins = three(psum[:, 6, 8 * H:9 * H], xs_hi[:, c, T - P:T], xs_lo[:, c, T - P:T],
                            wf_hi[:, c, :], wf_lo[:, c, :], c == 0, c == C - 1)
            ins.then_inc(f_acc, 1)

            def out_of(src):
                def go(tb, t0, n, half, c, bank):
                    return nc.tensor.transpose(psum[0:n, bank, c * P:(c + 1) * P], src[:, 4 * half + c, t0:t0 + n],
                                               ident[:, :])
                return go
            pe.wait_ge(acc_free, ACCS + NT * (BLK0["v"] + 8))
            transposes_in(TR_K, out_of(y))
            transposes_in(TR_V, out_of(vT))
            pe.wait_ge(tr_act, TR_Y)
            pe.wait_ge(tr_dve, TR_Y)
            plain("q", xs_hi, xs_lo)
            pe.wait_ge(f_step, 1)
            for tb in range(8):
                ins = nc.tensor.transpose(psum[0:H, 6 + tb // 4, (tb % 4) * P:(tb % 4 + 1) * P], lf[:, tb, :], ident[:, :])
                if tb % 4 == 3:
                    ins.then_inc(f_tr, 1)
            pe.wait_ge(acc_free, ACCS + NT * (BLK0["q"] + 8))
            nc.tensor.transpose(psum[0:H, 0, 0:P], lf[:, 8, :], ident[:, :]).then_inc(f_tr, 1)

            pe.sem_inc(pv_done, 2)
            pe.wait_ge(f_act, 6)
            pe.wait_ge(consts, 6)
            pe.wait_ge(v_back, 16)

            def scores(hp, j):
                (hh, qb), b = ITEMS[j % NI], s_banks(j)
                if j % 8 == 0:
                    pe.wait_ge(aug_landed[hh], hp * 64 + 64 * (1 + j // NI))
                pe.wait_ge(exp_done, hp * NI + (j + 3 if j % 2 else j + 1))
                q = qaug[hh][:, qb * P:(qb + 1) * P]
                for part in range((qb + 4) // 4):
                    k0 = 512 * part
                    k1 = min(k0 + 512, (qb + 1) * P)
                    diag = k1 == (qb + 1) * P
                    M(psum[:, b + part, 0:k1 - k0], q, kaug[hh][:, k0:k1], start=True, stop=not diag)
                    if diag:
                        M(psum[:, b + part, k1 - k0 - P:k1 - k0], ident[:, :], causal[:, :], start=False,
                          stop=True).then_inc(s_ready, 1)

            def transpose_probs(hp, j):
                pe.wait_ge(exp_done, hp * NI + (j + 5))
                for g, kb, nb in groups(j):
                    pe.wait_ge((pt_act, pt_dve)[g % 2], ghalf(hp, g - g % 2) + 1)
                    for c in range(nb):
                        ins = nc.tensor.transpose(psum[:, 5 + g % 2, c * P:(c + 1) * P],
                                                  prob[j % 2][:, (kb + c) * P:(kb + c + 1) * P], ident[:, :])
                    ins.then_inc(pt_ready, 1)

            def outputs(hp, j):
                hh, qb = ITEMS[j]
                for g, kb, nb in groups(j):
                    pe.wait_ge((pt_act, pt_dve)[g % 2], ghalf(hp, g - g % 2) + 2)
                pe.wait_ge(o_taken, hp * NI + (j + 1))
                for c in range(qb + 1):
                    ins = M(psum[:, 7, 0:DH], probT[j % 2][:, c, :],
                            v_keys[:, c, ds(hp * P + DH * hh, DH)], start=c == 0, stop=c == qb)
                ins.then_inc(pv_done, 1)

            def transpose_o(hp, dve0, act0):
                pe.wait_ge(o_taken, hp * NI + (NI + 1))
                for r in range(2):
                    pe.wait_ge((pt_dve, pt_act)[r], (dve0, act0)[r] + 1)
                    for c in range(4):
                        ins = nc.tensor.transpose(psum[:, 6 - r, c * P:(c + 1) * P], o_pair[:, 4 * r + c, :], ident[:, :])
                    ins.then_inc(pt_ready, 1)

            def pair(hp, first, last):
                for j in range(NI):
                    if not (last and j >= NI - 2):
                        scores(hp, j + 2)
                    transpose_probs(hp, j)
                    if j == 1 and not first:
                        transpose_o(hp - 1, hp * 13, hp * 13 + 1)
                    if j > 0:
                        outputs(hp, j - 1)
                    elif not first:
                        outputs(hp - 1, NI - 1)

            scores(0, 0)
            scores(0, 1)
            pair(0, True, False)
            with pe.Fori(1, HP - 1) as hp:
                pair(hp, False, False)
            pair(HP - 1, False, True)
            outputs(HP - 1, NI - 1)
            transpose_o(HP - 1, 13 * HP - 1, 13 * HP - 1)

            pe.sem_inc(st_ready, 3)
            pe.sem_inc(spv_done, 2)
            pe.wait_ge(pt_act, 1 + 13 * HP)
            pe.wait_ge(pt_dve, 1 + 13 * HP)
            pe.wait_ge(consts, 13)
            pe.wait_ge(new_landed, 32)

            def page(b, pg, na, nv):
                pe.wait_ge(kpage_landed[pg % 4], b * 32 + 16 * (pg // 4 + 1))
                for half in range(2):
                    pe.wait_ge((st_act, st_dve)[half], (na, nv)[half] + 1)
                    for c in range(4):
                        f0 = (4 * half + c) * P
                        ins = nc.tensor.transpose(psum[:, 4 + half, c * P:(c + 1) * P], kpage[pg % 4][:, f0:f0 + P],
                                                  ident[:, :])
                    ins.then_inc(st_ready, 1)

            def forget_values(b, na, nv):
                pe.wait_ge(lfpage_landed, b * (16 * NPG) + 16 * NPG)
                for r in range(2):
                    pe.wait_ge((st_act, st_dve)[r], (na, nv)[r] + 1)
                    for c in range(4):
                        ins = nc.tensor.transpose(psum[0:H, 4 + r, c * P:(c + 1) * P], lf_page[:, 4 * r + c, :],
                                                  ident[:, :])
                    ins.then_inc(st_ready, 1)

            def q_of(par, c):
                return qbd[par][:, c * P:(c + 1) * P]

            def sample_probs(b, na, nv):
                pe.wait_ge(ss_exp, b * 2 + 4)
                for g in range(3):
                    pe.wait_ge((st_act, st_dve, st_act)[g], (na, nv, na + 1)[g] + 1)
                    if g == 2:
                        pe.sem_inc(passed, 1)
                    for c in range(4 * g, min(4 * g + 4, 9)):
                        n = P if c < 8 else NS
                        ins = nc.tensor.transpose(psum[0:n, 4 + g % 2, (c % 4) * P:(c % 4 + 1) * P],
                                                  sprob[:, c * P:c * P + n], ident[:, :])
                    ins.then_inc(st_ready, 1)

            def sample_pv(b, na, nv):
                pe.wait_ge(st_act, na + 3)
                pe.wait_ge(st_dve, nv + 2)
                for f in range(2):
                    pe.wait_ge(vpage_landed[f], b * (16 * NPG) + 16 * NPG)
                    fs = slice(512 * f, 512 * f + 512)
                    for pg in range(NPG):
                        M(psum[:, 6 + f, :], sprobT[:, pg, :], v_page[:, pg, fs], start=pg == 0, stop=False)
                    M(psum[:, 6 + f, :], sprobT[0:NS, 8, :], v_new[:, fs], start=False, stop=True).then_inc(spv_done, 1)

            def out_back(b):
                for f in range(2):
                    pe.wait_ge(so_rows, b * 2 + 2)
                    for c in range(4):
                        f0 = (4 * f + c) * P
                        ins = nc.tensor.transpose(psum[:, 6 + f, 112 * c:112 * c + P], o_rows[:, f0:f0 + P], ident[:, :])
                    ins.then_inc(so_tr, 1)

            def sequence(b, par, first, last):
                _, na, nv = st_before(b)
                for i in range(4):
                    page(b, 4 + i, na + i, nv + i)
                    if i == 0:
                        pe.wait_ge(qbd_ready, b * 2 + 2)
                        if not first:
                            pe.wait_ge(ss_exp, b * 2)
                        pe.wait_ge(st_act, na + 1)
                        pe.wait_ge(st_dve, nv + 1)
                    for c in (2 * i, 2 * i + 1):
                        M(psum[:, 2 * par, :], q_of(par, c), kT[0][:, c, :], start=c == 0, stop=False)
                pe.wait_ge(fb_ready, b + 1)
                M(psum[:, 2 * par, :], nexpand[:, :], cum[:, 0:512], start=False, stop=True)
                if not first:
                    sample_probs(b - 1, na + 4, nv + 4)
                    sample_pv(b - 1, na + 4, nv + 4)
                M(psum[:, 2 * par + 1, :], nexpand[:, :], cum[:, 512:1024], start=True, stop=False)
                _, ma, mv = st_mid(b, first)
                if not last:
                    forget_values(b + 1, ma, mv)
                for i in range(4):
                    if not last:
                        page(b + 1, i, ma + (1 + i), mv + (1 + i))
                    if i == 0:
                        pe.wait_ge(st_act, na + 5)
                        pe.wait_ge(st_dve, nv + 5)
                    if i == 1 and not first:
                        out_back(b - 1)
                    for c in (2 * i, 2 * i + 1):
                        M(psum[:, 2 * par + 1, :], q_of(par, c), kT[1][:, c, :], start=False, stop=c == C - 1)
                if not first:
                    pe.wait_ge(so_taken, b * 4)
                for c in range(C):
                    M(psum[:, 6, 0:NS], q_of(par, c), k_newT[:, c, :], start=c == 0, stop=False)
                M(psum[:, 6, 0:NS], nexpand[:, :], cum_new[par][:, :], start=False, stop=False)
                M(psum[:, 6, 0:NS], qsel[:, :], wmask[:, ds(b * (-NQ) + 56, NS)], start=False, stop=True)\
                    .then_inc(ss_ready, 1)

            forget_values(0, 2, 1)
            for i in range(4):
                page(0, i, 3 + i, 2 + i)
            sequence(0, 0, True, False)
            with pe.Fori(0, NB // 2 - 1) as i:
                sequence(i * 2 + 1, 1, False, False)
                sequence(i * 2 + 2, 0, False, False)
            sequence(NB - 1, 1, False, True)
            _, na, nv = st_mid(NB - 1, False)
            sample_probs(NB - 1, na, nv)
            sample_pv(NB - 1, na, nv)
            out_back(NB - 1)

            plain("o", xs_hi, xs_lo, XS0["o"])
            norm("n_att", PAIR)
            ffn(1)
            ple(1)
            pe.wait_ge(ple_added, 2 * C * NT)
            pe.wait_ge(acc_free, ACCS + NT * BLKS)
            transposes_in(TR_Y, out_of(h))


_INS = ['x_prompt', 'x_sample', 'state_conv', 'cache_k', 'cache_v', 'cache_logf', 'page_table', 'p_prompt',
        'p_sample', 'norm_g', 'w_in', 'w_conv', 'w_out', 'g_kv', 'w_k', 'w_v', 'w_f', 'b_f', 'w_q', 'w_o',
        'w_gate', 'w_up', 'w_down', 'w_ple', 'w_ple_gate']
_OUTS = [(1, SEQ, D), (NB, NQ, D), (1, 1, 2, D), (1, SEQ, H, DH), (1, SEQ, H, DH), (1, SEQ, H), (1, NB, 2, D),
         (NB, NQ, H, DH), (NB, NQ, H, DH), (NB, NQ, H)]


def kernel(**inputs):
    import numpy as _np
    import concourse.bacc as _bacc
    from concourse import mybir as _mybir
    from concourse.bass_utils import run_bass_kernel_spmd as _run

    nc = _bacc.Bacc("TRN2", target_bir_lowering=False, num_devices=1)
    arrays, ins, outs = {}, [], []
    for name in _INS:
        a = _np.ascontiguousarray(inputs[name])
        arrays[f"in_{name}"] = a
        ins.append(nc.dram_tensor(f"in_{name}", a.shape, _mybir.dt.from_np(a.dtype), kind="ExternalInput").ap())
    for i, shape in enumerate(_OUTS):
        outs.append(nc.dram_tensor(f"out_{i}", shape, F32, kind="ExternalOutput").ap())
    trunk(nc, ins, outs)
    r = _run(nc, [arrays], core_ids=[0])
    return tuple(r.results[0][f"out_{i}"] for i in range(len(_OUTS)))
```

```python
from contextlib import ExitStack

import concourse.bass as bass
from concourse import mybir

F32 = mybir.dt.float32
F32R = mybir.dt.float32r
I32 = mybir.dt.int32
ALU = mybir.AluOpType
ACT = mybir.ActivationFunctionType
AX_X = mybir.AxisListType.X
ds = bass.ds

P = 128
D = 1024
C = D // P
SEQ = 1024
NB, NQ = 8, 8
NS = NB * NQ
T = SEQ + NS
H, DH = 16, 64
D_FF = 2816
PLE = 256
PAGE, NPG, POOL = 128, 8, 80
EPS = 1e-6
SCALE = DH ** -0.5
MASKED = -1e30

TILES = [(0, 384), (384, 384), (768, T - 768)]
NT = len(TILES)
TOKB = [(128 * i, 128) for i in range(8)] + [(SEQ, NS)]
NTB = len(TOKB)

STAGES = [("in", 24, 24), ("out", 8, 8), ("ffn0", 66, 132), ("pp0", 2, 0), ("pg0", 8, 16),
          ("k", 8, 8), ("q", 8, 8), ("v", 8, 8), ("o", 8, 8), ("ffn1", 66, 132), ("pp1", 2, 0),
          ("pg1", 8, 16)]
SLAB0, BLK0 = {}, {}
_s = _b = 0
for _name, _ns, _nb in STAGES:
    SLAB0[_name], BLK0[_name] = _s, _b
    _s, _b = _s + _ns, _b + _nb
SLABS, BLKS = _s, _b
RAWS = 2
HLS = 2
ACCS = 2 * NT

PAIR = [("post", 0), ("post", 1), ("pre", 0), ("post", 2), ("pre", 1), ("pre", 2)]
PRE = [("pre", 0), ("pre", 1), ("pre", 2)]
POST = [("post", 0), ("post", 1), ("post", 2)]
STEP0 = {"n_in": 0, "n_mix": 3, "n_ffn0": 9, "n_kv": 12, "n_att": 15, "n_ffn1": 21}
XS0 = {"in": 0, "ffn0": 3, "pg0": 6, "kvq": 9, "o": 12, "ffn1": 15, "pg1": 18}
SQ0 = {"n_in": 0, "n_mix": 12, "n_att": 24}
PQ = {"n_mix": 0, "n_ffn0": 1, "n_kv": 2, "n_att": 3, "n_ffn1": 4}
HR0 = {"n_mix": 0, "n_ffn0": 3, "n_att": 6, "n_ffn1": 9}
ROW_G, ROW_KV, ROW_CONV, ROW_STATE, NVEC = 0, 8, 9, 12, 28

REG = C * T * 4
B0 = 16640
A_H, A_XH, A_XL, A_Y, A_G = (B0 + i * REG for i in range(5))
A_RAW = B0 + 5 * REG
A_WH = A_RAW + RAWS * 4096
A_WL = A_WH + HLS * 4096
A_STG = A_WL + HLS * 4096
A_MISC = A_STG + 8192


def trunk(nc, ins, outs):
    (x_prompt, x_sample, state_conv, cache_k, cache_v, cache_logf, page_table, p_prompt, p_sample,
     norm_g, w_in, w_conv, w_out, g_kv, w_k, w_v, w_f, b_f, w_q, w_o, w_gate, w_up, w_down, w_ple,
     w_ple_gate) = ins
    (y_prompt, y_sample, conv_prompt, k_prompt, v_prompt, logf_prompt, conv_sample, k_sample,
     v_sample, logf_sample) = outs

    kT_dram = nc.dram_tensor("kT_scratch", [D, T], F32).ap()
    fsum_dram = nc.dram_tensor("fsum_scratch", [2, H, SEQ], F32R).ap()

    def sb(name, shape, dt, off):
        return nc.alloc_sbuf_tensor_at(name, shape, dt, offset=off)

    h = sb("h", [P, C, T], F32, A_H)
    xs_hi = sb("xs_hi", [P, C, T], F32R, A_XH)
    xs_lo = sb("xs_lo", [P, C, T], F32R, A_XL)
    y_mix = sb("y_mix", [P, C, T], F32, A_XH)
    y = sb("y", [P, C, T], F32, A_Y)
    vT = sb("vT", [P, C, T], F32, A_Y)
    qo = sb("qo", [P, C, T], F32, A_G)
    raw = [sb(f"raw{i}", [P, 1024], F32, A_RAW + 4096 * i) for i in range(RAWS)]
    w_hi = [sb(f"w_hi{i}", [P, 1024], F32R, A_WH + 4096 * i) for i in range(HLS)]
    w_lo = [sb(f"w_lo{i}", [P, 1024], F32R, A_WL + 4096 * i) for i in range(HLS)]
    bgate = sb("bgate", [P, C, T], F32, A_Y)
    mix_hi = sb("mix_hi", [P, C, T], F32R, A_Y)
    zconv = sb("zconv", [P, C, T], F32, A_G)
    mix_lo = sb("mix_lo", [P, C, T], F32R, A_G)
    NPAD = SEQ + 2
    cup = sb("cup", [P, NPAD + NB * (NQ + 2)], F32, A_STG)
    cup_s = cup[:, NPAD:].rearrange("p (b t) -> p b t", b=NB)
    x_nat = sb("x_nat", [P, 8, D], F32, A_Y)
    xs_nat = sb("xs_nat", [NS, D], F32, A_STG)
    vec_nat = sb("vec_nat", [NVEC, D], F32, A_STG + 4096)
    xn = [sb(f"xn{i}", [P, C, 384], F32, A_G + 12288 * i) for i in range(2)]
    sqp = [sb(f"sqp{i}", [P, 2, 384], F32, A_G + 24576 + 3072 * i) for i in range(2)]
    ssum = sb("ssum", [P, T], F32, A_STG)
    ssum_kv = sb("ssum_kv", [P, T], F32, A_Y)
    psq = [sb(f"psq{i}", [P, T], F32, A_XL + 4352 * i) for i in range(2)]
    psq_kv = [sb(f"psq_kv{i}", [P, T], F32, A_Y + 4352 * (1 + i)) for i in range(2)]
    psq_att = [sb(f"psq_att{i}", [P, T], F32, A_G + 17408 + 4352 * i) for i in range(2)]
    p_nat = sb("p_nat", [P, NTB, PLE], F32, A_G + 17408)
    pT_hi = sb("pT_hi", [P, 2, T], F32R, A_G)
    pT_lo = sb("pT_lo", [P, 2, T], F32R, A_G + 8704)
    wp_hi = sb("wp_hi", [P, 2, 1024], F32R, A_G + 17408)
    wp_lo = sb("wp_lo", [P, 2, 1024], F32R, A_G + 25600)
    hid_hi = [sb(f"hid_hi{i}", [P, 2, T], F32R, A_G + 17408 * i) for i in range(2)]
    hid_lo = [sb(f"hid_lo{i}", [P, 2, T], F32R, A_G + 17408 * i + 8704) for i in range(2)]
    act = sb("act", [P, T], F32, A_STG)
    rows_out = [sb(f"rows_out{i}", [P, D], F32, A_STG + 4096 * i) for i in range(2)]

    off = A_MISC
    def misc(name, shape, dt=F32):
        nonlocal off
        n = 4
        for s in shape[1:]:
            n *= s
        t = sb(name, shape, dt, off)
        off += (n + 31) // 32 * 32
        assert off <= 229344
        return t
    vecT = misc("vecT", [P, C, NVEC])
    ident = misc("ident", [P, P])
    ones = misc("ones", [P, 1])
    eps_c = misc("eps_c", [P, 1])
    convT = misc("convT", [P, C, 2 + 2 * NB])
    causal = sb("causal", [P, P], F32, off)
    causal_r = sb("causal_r", [P, P], F32R, off + 512)
    ident_r = sb("ident_r", [P, P], F32R, off + 1024)
    wf_raw = misc("wf_raw", [P, C, H])
    wf_hi = misc("wf_hi", [P, C, H], F32R)
    wf_lo = misc("wf_lo", [P, C, H], F32R)
    lf = misc("lf", [P, NTB, H])
    bf = misc("bf", [H, 1])
    ptab = misc("ptab", [1, NB * NPG], I32)
    segm = misc("segm", [H, NS])
    one16 = misc("one16", [H, 1])
    fsum_new = misc("fsum_new", [H, NS])
    conv_rows = sb("conv_rows", [2 + 2 * NB, D], F32, A_STG)

    fz = sb("fz", [H, T], F32, A_G + 6 * T * 4)
    flog = sb("flog", [H, T], F32, A_G + 7 * T * 4)

    k_raw = sb("k_raw", [P, SEQ], F32, A_RAW + 4096)
    q_raw = sb("q_raw", [P, SEQ], F32, A_WH + 4096)
    k_hh = [sb(f"k_hh{i}", [P, SEQ], F32R, A_XH + 16384 * i) for i in range(2)]
    k_low = [sb(f"k_low{i}", [DH + 4, SEQ], F32R, A_XH + 16384 * i + 4096) for i in range(2)]
    q_hl = [sb(f"q_hl{i}", [P, SEQ], F32R, A_XH + 16384 * i + 8192) for i in range(2)]
    q_high = [sb(f"q_high{i}", [DH + 4, SEQ], F32R, A_XH + 16384 * i + 12288) for i in range(2)]
    fsum = sb("fsum", [H, SEQ], F32, A_XH + 16384)
    fsum_hi = sb("fsum_hi", [H, SEQ], F32R, A_XH + 16384 + 8192)
    fsum_lo = sb("fsum_lo", [H, SEQ], F32R, A_XH + 16384 + 4096)
    prob = [sb(f"prob{i}", [P, SEQ], F32, A_Y + 4736 + 4096 * i) for i in range(2)]
    probT = [sb(f"probT{i}", [P, 8, P], F32, A_Y + 12928 + 4096 * i) for i in range(2)]
    v_keys = sb("v_keys", [P, 8, D], F32, A_XL)
    o_pair = sb("o_pair", [P, 8, P], F32, A_Y)
    nmx = sb("nmx", [P, 8], F32, A_Y + 4608)
    rsum = sb("rsum", [P, 8], F32, A_Y + 4640)
    rinv = sb("rinv", [P, 8], F32, A_Y + 4672)
    NK = NPG * PAGE
    kT = [sb(f"kT{i}", [P, C, 512], F32, A_XH + 16384 * i) for i in range(2)]
    v_page = sb("v_page", [P, NPG, D], F32, A_XL)
    sprob = sb("sprob", [P, NK + NS], F32, A_Y)
    o_rows = sb("o_rows", [P, D], F32, A_Y)
    sstat = sb("sstat", [P, 8], F32, A_Y + 4704)
    kpage = [sb(f"kpage{i}", [P, D], F32, A_Y + 4736 + 4096 * i) for i in range(4)]
    k_newT = sb("k_newT", [P, C, NS], F32, A_Y + 21120)
    lf_page = sb("lf_page", [P, NPG, H], F32, A_Y + 23168)
    nexpand = sb("nexpand", [H, P], F32, A_Y + 23680)
    qsel = sb("qsel", [NQ, P], F32, A_Y + 24192)
    wmask = sb("wmask", [NQ, 120], F32, A_Y + 24704)
    cum_new = [sb(f"cum_new{i}", [H, NS], F32, A_Y + 25184 + 256 * i) for i in range(2)]
    v_new = sb("v_new", [NS, D], F32, A_Y + 25696)
    sprobT = sb("sprobT", [P, NPG + 1, P], F32, A_Y + 29792)
    cum = sb("cum", [H, NK], F32, A_RAW + 4096)
    lf_pageT = sb("lf_pageT", [H, NK], F32, A_WH + 4096)
    qdiag = [sb(f"qdiag{i}", [P, C, P + 16], F32, A_STG + 512 - 4608 * i) for i in range(2)]
    qbd = [q[:, :, :].rearrange("p c n -> p (c n)")[:, 0:D] for q in qdiag]

    SSUM = {"n_mix": ssum, "n_ffn0": ssum, "n_kv": ssum_kv, "n_att": ssum, "n_ffn1": ssum}
    PSQ = {"n_mix": psq, "n_ffn0": psq, "n_kv": psq_kv, "n_att": psq_att, "n_ffn1": psq}

    with ExitStack() as ctx:
        psum = ctx.enter_context(nc.psum_tensor("psum", [P, 8, 512], F32))

        def sem(name):
            return ctx.enter_context(nc.semaphore(name))

        def acc(b, t):
            return psum[:, 3 * (b % 2) + t, 0:TILES[t][1]]

        raw_landed = [sem(f"raw_landed{i}") for i in range(RAWS)]
        hi_ready = sem("hi_ready")
        lo_ready = sem("lo_ready")
        slab_used = sem("slab_used")
        acc_ready = sem("acc_ready")
        acc_free = sem("acc_free")
        consts = sem("consts")
        vec_landed = sem("vec_landed")
        x_landed = [sem(f"x_landed{i}") for i in range(NTB)]
        vec_tr, vec_done = sem("vec_tr"), sem("vec_done")
        tr_ready = sem("tr_ready")
        tr_act, tr_dve = sem("tr_act"), sem("tr_dve")
        rows_stored = [sem(f"rows_stored{i}") for i in range(2)]
        psq_ready, psq_added = sem("psq_ready"), sem("psq_added")
        post_sum = sem("post_sum")
        sq_ready, sq_used = sem("sq_ready"), sem("sq_used")
        std_ready, rb_ready, rb_used = sem("std_ready"), sem("rb_ready"), sem("rb_used")
        h_ready = sem("h_ready")
        xs_hi_ready, xs_ready = sem("xs_hi_ready"), sem("xs_ready")
        conv_step = sem("conv_step")
        z_hi = sem("z_hi")
        mix_ready = sem("mix_ready")
        conv_tr, conv_rows_done, conv_stored = sem("conv_tr"), sem("conv_rows_done"), sem("conv_stored")
        y_zero = sem("y_zero")
        sig_ready = sem("sig_ready")
        act_ready, hid_hi_ready, hid_ready = sem("act_ready"), sem("hid_hi_ready"), sem("hid_ready")
        p_landed = sem("p_landed")
        p_tr, p_hi_ready, p_ready = sem("p_tr"), sem("p_hi_ready"), sem("p_ready")
        ple_mul, ple_sig = sem("ple_mul"), sem("ple_sig")
        ple_added = sem("ple_added")
        kT_stored = sem("kT_stored")
        wf_landed, wf_hi_s, wf_lo_s = sem("wf_landed"), sem("wf_hi_s"), sem("wf_lo_s")
        f_acc, f_z = sem("f_acc"), sem("f_z")
        f_act, f_step = sem("f_act"), sem("f_step")
        f_stored = sem("f_stored")
        f_tr = sem("f_tr")
        fs_stored = sem("fs_stored")
        v_stored = sem("v_stored")
        aug_one, mask_ready = sem("aug_one"), sem("mask_ready")
        head_landed = sem("head_landed")
        aug_landed = [sem(f"aug_landed{i}") for i in range(2)]
        split_act, split_dve = sem("split_act"), sem("split_dve")
        s_ready, s_max, exp_done = sem("s_ready"), sem("s_max"), sem("exp_done")
        pt_ready, pt_act, pt_dve = sem("pt_ready"), sem("pt_act"), sem("pt_dve")
        pv_done, rinv_s, o_taken = sem("pv_done"), sem("rinv_s"), sem("o_taken")
        tab_landed = sem("tab_landed")
        new_landed = sem("new_landed")
        kpage_landed = [sem(f"kpage_landed{i}") for i in range(4)]
        vpage_landed = [sem(f"vpage_landed{i}") for i in range(2)]
        lfpage_landed = sem("lfpage_landed")
        qbd_zero, qbd_ready = sem("qbd_zero"), sem("qbd_ready")
        kpage_used = sem("kpage_used")
        st_ready, st_act, st_dve = sem("st_ready"), sem("st_act"), sem("st_dve")
        cum_ready, fb_ready = sem("cum_ready"), sem("fb_ready")
        ss_ready, ss_max, ss_exp = sem("ss_ready"), sem("ss_max"), sem("ss_exp")
        sp_step = sem("sp_step")
        spv_done, so_rows = sem("spv_done"), sem("so_rows")
        so_tr, so_taken = sem("so_tr"), sem("so_taken")
        passed = sem("passed")
        block = ctx.enter_context(nc.Block())

        TR_X, TR_K, TR_V, TR_Y = 0, NTB, 2 * NTB, 3 * NTB
        ROWS0 = {TR_K: 0, TR_V: NTB - 8, TR_Y: NTB + 1}
        ITEMS = [(hh, qb) for hh in range(2) for qb in (7, 0, 6, 1, 5, 2, 4, 3)]
        NI, HP = len(ITEMS), H // 2
        OT_AT = 3

        def s_banks(j):
            return 4 if j % 2 else 2 * (j // 2 % 2)

        def s_view(j):
            nk = (ITEMS[j % NI][1] + 1) * P
            b = s_banks(j)
            return psum[:, b, 0:nk] if j % 2 else psum[:, b:b + 2, :].rearrange("p a b -> p (a b)")[:, 0:nk]

        def groups(j):
            g = 3 * (j // 2) + 2 * (j % 2)
            g += 2 if g >= OT_AT else 0
            nb = ITEMS[j][1] + 1
            return [(g + q, 4 * q, min(4, nb - 4 * q)) for q in range((nb + 3) // 4)]

        def gcount(hp, g):
            if isinstance(hp, int) and hp == 0:
                return g if g <= OT_AT else g - 2
            return hp * 26 + (g - 2)

        def ghalf(hp, g):
            if isinstance(hp, int) and hp == 0:
                return (g if g < OT_AT else g - 2) // 2
            return hp * 13 + (g // 2 - 1)

        def ready(blk, t, two=False, second=0):
            return blk * NT + (2 * t + second + 1 if two else second * NT + t + 1)

        def st_before(b):
            if isinstance(b, int) and b == 0:
                return 13, 7, 6
            return b * 21 + 10, b * 11 + 5, b * 10 + 5

        def st_mid(b, first):
            n, na, nv = st_before(b)
            return (n + 8, na + 4, nv + 4) if first else (n + 11, na + 6, nv + 5)

        CONV_STEPS = 14

        @block.sync
        def _(sp):
            def cols(w, c0, n=P, k=C):
                return w[:, ds(c0, n)].rearrange("(k p) n -> p k n", p=P)

            def load(n, slot, src, k, width):
                if isinstance(n, int) and n < RAWS:
                    pass
                else:
                    sp.wait_ge(lo_ready, n + 1)
                sp.dma_start(raw[slot][:, :].rearrange("p (k n) -> p k n", k=k), src)\
                    .then_inc(raw_landed[slot], 16)

            def plain(name, w, skip=0, take=C):
                for m in range(skip, take):
                    load(SLAB0[name] + m, m % 2, cols(w, m * P), C, P)

            w_in0 = w_in[0]
            for u, part in enumerate((0, 1, 2, 0, 1, 2)):
                load(u, u % 2, cols(w_in0, part * D + (u // 3) * P), C, P)
            with sp.Fori(1, C // 2) as i:
                for u, part in enumerate((0, 1, 2, 0, 1, 2)):
                    load(i * 6 + u, u % 2, cols(w_in0, i * (2 * P) + (part * D + (u // 3) * P)), C, P)
            plain("out", w_out[0])

            def ffn(name, layer):
                wg, wu, wd = w_gate[layer], w_up[layer], w_down[layer]

                def gate_up(g, n):
                    for u in range(4):
                        src = (wg, wu)[u % 2]
                        load(n + u, u % 2, cols(src, g * (2 * P) + (u // 2) * P), C, P)

                def down(g, n):
                    rows = wd[ds(g * (2 * P), 2 * P), :].rearrange("(k p) n -> p k n", p=P)
                    for u in range(2):
                        load(n + u, u % 2, rows[:, :, u * 512:(u + 1) * 512], 2, 512)

                n0 = SLAB0[name]
                gate_up(0, n0)
                with sp.Fori(0, 5) as i:
                    gate_up(i * 2 + 1, i * 12 + (n0 + 4))
                    down(i * 2, i * 12 + (n0 + 8))
                    gate_up(i * 2 + 2, i * 12 + (n0 + 10))
                    down(i * 2 + 1, i * 12 + (n0 + 14))
                down(10, n0 + 64)

            def ple(layer):
                rows = w_ple[layer].rearrange("(k p) n -> p k n", p=P)
                for u in range(2):
                    load(SLAB0[f"pp{layer}"] + u, u, rows[:, :, u * 512:(u + 1) * 512], 2, 512)
                plain(f"pg{layer}", w_ple_gate[layer])

            ffn("ffn0", 0)
            ple(0)
            plain("k", w_k)
            plain("q", w_q[0])
            plain("v", w_v)
            plain("o", w_o[0], 0, 1)

            sp.dma_start(ptab[:, :], page_table.rearrange("(o b) n -> o (b n)", o=1)).then_inc(tab_landed, 16)
            sp.wait_ge(tab_landed, 16)
            sp.wait_ge(pv_done, 2 + NI * HP)
            k_pages = cache_k.rearrange("n t h d -> n t (h d)")
            with sp.Fori(0, NB) as b:
                for pg in range(NPG):
                    sp.wait_ge(kpage_used, b * NPG + (pg + 1))
                    page = sp.value_load(ptab[0:1, ds(b * NPG + pg, 1)], min_val=0, max_val=POOL - 1)
                    sp.dma_start(kpage[pg % 4][:, :], k_pages[ds(page, 1)].rearrange("o t d -> (o t) d"))\
                        .then_inc(kpage_landed[pg % 4], 16)
            sp.wait_ge(so_taken, 4 * NB)
            plain("o", w_o[0], 1)
            ffn("ffn1", 1)
            ple(1)

        @block.gpsimd
        def _(pool):
            def mask(t, pattern, base, cm, op=ALU.is_ge, fill=MASKED):
                pool.affine_select(out=t, in_=t, compare_op=op, fill=fill, base=base, pattern=pattern,
                                   channel_multiplier=cm).then_inc(consts, 1)

            for tb, (t0, n) in enumerate(TOKB):
                dst = x_nat[:, tb, :] if tb < 8 else xs_nat[:, :]
                src = x_prompt[0, t0:t0 + n, :] if tb < 8 else x_sample.rearrange("b t d -> (b t) d")
                if tb == 3:
                    for r0, n_, s in ((ROW_G, 8, norm_g.rearrange("l k d -> (l k) d")),
                                      (ROW_KV, 1, g_kv.rearrange("(o d) -> o d", o=1)),
                                      (ROW_CONV, 3, w_conv[0]),
                                      (ROW_STATE, 16, state_conv[0].rearrange("b t d -> (b t) d"))):
                        pool.dma_start(vec_nat[r0:r0 + n_, :], s).then_inc(vec_landed, 16)
                pool.dma_start(dst, src).then_inc(x_landed[tb], 16)
                if tb == 0:
                    pool.memset(ident[:, :], 0.0).then_inc(consts, 1)
                    pool.memset(ones[:, :], 1.0).then_inc(consts, 1)
                    pool.memset(eps_c[:, :], EPS).then_inc(consts, 1)
                    pool.wait_ge(consts, 3)
                    mask(ident[:, :], [[-1, P]], 0, 1, ALU.not_equal, 1.0)
            pool.dma_start(wf_raw[:, :, :], w_f.rearrange("(k p) n -> p k n", p=P)).then_inc(wf_landed, 16)
            pool.dma_start(bf[:, :], b_f.rearrange("(n o) -> n o", o=1)).then_inc(wf_landed, 16)

            pool.wait_ge(conv_rows_done, 2)
            pool.dma_start(conv_prompt[0, 0], conv_rows[0:2, :]).then_inc(conv_stored, 16)
            pool.dma_start(conv_sample[0].rearrange("b t d -> (b t) d"), conv_rows[2:2 + 2 * NB, :])\
                .then_inc(conv_stored, 16)

            def ffn(layer, y_free):
                pool.wait_ge(rb_used, y_free)
                pool.memset(y[:, :, :], 0.0).then_inc(y_zero, 1)
                pool.wait_ge(acc_ready, NT * (BLK0[f"pp{layer}"] - C))
                for tb, (t0, n) in enumerate(TOKB):
                    src = p_prompt[layer, 0, t0:t0 + n, :] if tb < 8 else \
                        p_sample[layer].rearrange("b t d -> (b t) d")
                    pool.dma_start(p_nat[0:n, tb, :], src).then_inc(p_landed, 16)

            ffn(0, 9)


            def store_rows(tr0, prompt, sample):
                for tb, (t0, n) in enumerate(TOKB):
                    pool.wait_ge(tr_act, tr0 + tb + 1)
                    pool.wait_ge(tr_dve, tr0 + tb + 1)
                    dst = prompt[t0:t0 + n, :] if tb < 8 else sample
                    r = ROWS0[tr0] + tb
                    pool.dma_start(dst, rows_out[r % 2][0:n, :]).then_inc(rows_stored[r % 2], 16)

            pool.wait_ge(acc_free, ACCS + NT * (BLK0["k"] + 8))
            pool.dma_start(kT_dram.rearrange("(c p) t -> p c t", p=P), y[:, :, :]).then_inc(kT_stored, 16)
            pool.wait_ge(f_step, 2)
            pool.dma_start(logf_prompt[0].rearrange("(b p) h -> p b h", p=P), lf[:, 0:8, :])\
                .then_inc(f_stored, 16)
            pool.dma_start(logf_sample.rearrange("b t h -> (b t) h"), lf[P - NS:P, 8, :]).then_inc(f_stored, 16)
            store_rows(TR_K, k_prompt[0].rearrange("t h d -> t (h d)"), k_sample.rearrange("b t h d -> (b t) (h d)"))
            pool.wait_ge(wf_lo_s, 1)
            pool.memset(causal[:, :], 0.0).then_inc(consts, 1)
            pool.wait_ge(consts, 5)
            mask(causal[:, :], [[-1, P]], 0, 1)
            pool.wait_ge(f_step, 7)
            pool.dma_start(fsum_dram[0], fsum_hi[:, :]).then_inc(fs_stored, 16)
            pool.dma_start(fsum_dram[1], fsum_lo[:, :]).then_inc(fs_stored, 16)
            pool.wait_ge(kT_stored, 16)
            pool.wait_ge(aug_one, 5)

            def load_head(hp, hh):
                for half in range(2):
                    part = slice(DH * half, DH * half + DH)
                    pool.dma_start(k_raw[part, :], kT_dram[ds(hp * P + DH * hh, DH), 0:SEQ]).then_inc(head_landed, 16)
                    pool.dma_start(q_raw[part, :], qo[DH * hh:DH * hh + DH, ds(hp, 1), 0:SEQ]
                                   .rearrange("p o t -> p (o t)")).then_inc(head_landed, 16)

            def load_rows(hp, hh):
                for t, r in ((k_low, DH), (q_high, DH + 2)):
                    pool.dma_start(t[hh][r:r + 2, :], fsum_dram[:, ds(hp * 2 + hh, 1), :]
                                   .rearrange("a o t -> a (o t)")).then_inc(aug_landed[hh], 16)

            load_head(0, 0)
            pool.wait_ge(fs_stored, 32)
            load_rows(0, 0)
            load_rows(0, 1)
            pool.wait_ge(split_act, 3)
            pool.wait_ge(split_dve, 2)
            load_head(0, 1)

            for tb, (t0, n) in enumerate(TOKB):
                pool.wait_ge(tr_act, TR_V + tb + 1)
                pool.wait_ge(tr_dve, TR_V + tb + 1)
                if tb < 8:
                    pool.dma_start(v_prompt[0, t0:t0 + n].rearrange("t h d -> t (h d)"), v_keys[:, tb, :])\
                        .then_inc(v_stored, 16)
                else:
                    pool.dma_start(v_sample.rearrange("b t h d -> (b t) (h d)"), rows_out[NTB % 2][0:n, :])\
                        .then_inc(rows_stored[NTB % 2], 16)

            v_pages = cache_v.rearrange("n t h d -> n t (h d)")

            def load_lf(b):
                for pg in range(NPG):
                    page = pool.value_load(ptab[0:1, ds(b * NPG + pg, 1)], min_val=0, max_val=POOL - 1)
                    pool.dma_start(lf_page[:, pg, :], cache_logf[ds(page, 1)].rearrange("o t h -> (o t) h"))\
                        .then_inc(lfpage_landed, 16)

            def load_v(b):
                for f in range(2):
                    pool.wait_ge(spv_done, b * 2 + (f + 1))
                    pool.sem_inc(passed, 1)
                    for pg in range(NPG):
                        page = pool.value_load(ptab[0:1, ds(b * NPG + pg, 1)], min_val=0, max_val=POOL - 1)
                        pool.dma_start(v_page[:, pg, 512 * f:512 * f + 512],
                                       v_pages[ds(page, 1), :, 512 * f:512 * f + 512].rearrange("o t d -> (o t) d"))\
                            .then_inc(vpage_landed[f], 16)

            pool.memset(nexpand[:, :], 0.0).then_inc(consts, 1)
            pool.memset(qsel[:, :], 0.0).then_inc(consts, 1)
            pool.memset(wmask[:, :], 0.0).then_inc(consts, 1)
            pool.wait_ge(consts, 9)
            mask(nexpand[:, :], [[1, H], [0, NQ]], 0, -1, ALU.not_equal, -1.0)
            mask(qsel[:, :], [[0, H], [1, NQ]], 0, -1, ALU.not_equal, 1.0)
            mask(wmask[:, :], [[1, 120]], -56, 0)
            pool.wait_ge(consts, 12)
            mask(wmask[:, :], [[-1, 120]], 56, 1)
            for r in range(2):
                pool.wait_ge(rows_stored[r], 16 * 5)
            for i in range(2):
                pool.memset(qbd[i], 0.0).then_inc(qbd_zero, 1)
            pool.dma_start(k_newT[:, :, :], kT_dram[:, SEQ:T].rearrange("(c p) t -> p c t", p=P))\
                .then_inc(new_landed, 16)
            pool.dma_start(v_new[:, :], v_sample.rearrange("b t h d -> (b t) (h d)")).then_inc(new_landed, 16)
            pool.wait_ge(tab_landed, 16)
            load_lf(0)
            with pool.Fori(1, H // 2) as hp:
                for hh in range(2):
                    pool.wait_ge(split_act, hp * 6 + 3 * hh)
                    pool.wait_ge(split_dve, hp * 4 + 2 * hh)
                    load_head(hp, hh)
                    pool.wait_ge(s_ready, hp * 16 + (8 * hh - 8))
                    load_rows(hp, hh)

            pool.wait_ge(pv_done, 2 + 8 * H)
            pool.wait_ge(pt_ready, 26 * HP)
            pool.wait_ge(v_stored, 16 * 8)
            with pool.Fori(0, NB - 1) as b:
                pool.wait_ge(cum_ready, b + 1)
                pool.sem_inc(passed, 1)
                load_lf(b + 1)
                load_v(b)
            load_v(NB - 1)

            ffn(1, 21)
            store_rows(TR_Y, y_prompt[0], y_sample.rearrange("b t d -> (b t) d"))
            pool.wait_ge(rows_stored[0], 16 * (NTB + 1))
            pool.wait_ge(rows_stored[1], 16 * NTB)
            pool.wait_ge(conv_stored, 32)
            pool.wait_ge(f_stored, 32)

        @block.scalar
        def _(act_e):
            A = nc.scalar.activation

            def hi(n2, slot, gain=None):
                act_e.wait_ge(raw_landed[slot], n2 * 16 + 16)
                act_e.wait_ge(slab_used, n2 * 2 + (slot + 1))
                if gain is None:
                    A(w_hi[slot][:, :], raw[slot][:, :], ACT.Copy).then_inc(hi_ready, 1)
                else:
                    for c in range(C):
                        ins = A(w_hi[slot][:, c * P:(c + 1) * P], raw[slot][:, c * P:(c + 1) * P], ACT.Copy,
                                scale=vecT[:, c, gain:gain + 1])
                    ins.then_inc(hi_ready, 1)

            def hi_run(n, count, gain=None):
                for j in range(n, n + count):
                    hi(j // 2, j % 2, gain)

            def block_squares(name, src, m, done, count):
                act_e.wait_ge(done, count)
                p = PQ[name]
                if m >= 3:
                    act_e.wait_ge(psq_added, 7 * p + m - 2)
                dst = SSUM[name] if m == 0 else PSQ[name][m % 2]
                A(dst[:, :], src[:, m, :], ACT.Square).then_inc(psq_ready, 1)

            def norm(name, seq, xs0, raw_split=False):
                s0, pending = STEP0[name], None
                for k, (kind, t) in enumerate(seq):
                    s = s0 + k
                    t0, n = TILES[t]
                    if kind == "post" or name == "n_kv":
                        act_e.wait_ge(post_sum, 3 * PQ[name] + t + 1)
                    else:
                        if name in HR0:
                            act_e.wait_ge(h_ready, HR0[name] + t + 1)
                        for j in range(4):
                            q = SQ0[name] + 4 * t + j
                            act_e.wait_ge(sq_used, q + 1)
                            A(sqp[q % 2][:, :, 0:n], h[:, 2 * j:2 * j + 2, t0:t0 + n], ACT.Square)\
                                .then_inc(sq_ready, 1)
                        act_e.wait_ge(sq_used, 2 + SQ0[name] + 4 * t + 4)
                    A(psum[:, 6 + s % 2, 0:n], psum[:, 6 + s % 2, 0:n], ACT.Sqrt, bias=eps_c[:, :], scale=1.0 / D)\
                        .then_inc(std_ready, 1)
                    if pending is not None:
                        pending()
                        pending = None
                    if kind == "pre":
                        def pending(s=s, t=t, t0=t0, n=n):
                            act_e.wait_ge(rb_used, s + 1)
                            A(xs_hi[:, :, t0:t0 + n], xn[t % 2][:, :, 0:n], ACT.Copy).then_inc(xs_hi_ready, 1)
                    elif raw_split:
                        def pending(t=t, t0=t0, n=n):
                            act_e.wait_ge(h_ready, HR0[name] + t + 1)
                            A(xs_hi[:, :, t0:t0 + n], h[:, :, t0:t0 + n], ACT.Copy).then_inc(xs_hi_ready, 1)
                if pending is not None:
                    pending()


            def take_in():
                for tb, (t0, n) in enumerate(TOKB):
                    act_e.wait_ge(tr_ready, 2 * (TR_X + tb) + 1)
                    bank = 2 * (tb % 3)
                    A(h[:, 0:4, t0:t0 + n], psum[:, bank, :].rearrange("p (c t) -> p c t", c=4)[:, :, 0:n], ACT.Copy)\
                        .then_inc(tr_act, 1)

            def row(tr0, tb, bank=None):
                g, r, n = tr0 + tb, ROWS0[tr0] + tb, TOKB[tb][1]
                bank = 2 * (g % 3) if bank is None else bank
                act_e.wait_ge(tr_ready, 2 * g + 1)
                if tr0 == TR_V and tb < 8:
                    A(v_keys[:, tb, 0:512], psum[:, bank, :], ACT.Copy).then_inc(tr_act, 1)
                    return
                if r >= 2:
                    act_e.wait_ge(rows_stored[r % 2], 16 * (r // 2))
                A(rows_out[r % 2][0:n, 0:512], psum[0:n, bank, :], ACT.Copy).then_inc(tr_act, 1)

            take_in()
            act_e.wait_ge(vec_tr, 1)
            A(vecT[:, :, :].rearrange("p c n -> p (c n)"), psum[:, 6, 0:C * NVEC], ACT.Copy).then_inc(vec_done, 1)
            act_e.wait_ge(tr_dve, NTB)
            hi_run(0, 1)
            norm("n_in", PRE, XS0["in"])

            with act_e.Fori(0, C // 2) as i:
                for u in range(2):
                    for j in range(3):
                        nxt = 3 * u + j + 1
                        hi(i * 3 + nxt // 2, nxt % 2)
                    act_e.wait_ge(conv_step, i * (2 * CONV_STEPS) + (u + 1) * CONV_STEPS)
                    m = i * 2 + u
                    A(mix_hi[:, ds(m, 1), :], zconv[:, ds(m, 1), :], ACT.Copy).then_inc(z_hi, 1)
            hi_run(SLAB0["out"] + 1, 1)
            for j in range(2):
                act_e.wait_ge(conv_tr, j + 1)
                A(conv_rows[:, 512 * j:512 * j + 512], psum[0:2 + 2 * NB, 6 + j, :], ACT.Copy)\
                    .then_inc(conv_rows_done, 1)
            act_e.wait_ge(conv_stored, 32)
            for m in range(C):
                if m:
                    hi_run(SLAB0["out"] + 1 + m, 1)
                block_squares("n_mix", y_mix, m, acc_free, ACCS + NT * (BLK0["out"] + m + 1))
            hi_run(SLAB0["ffn0"] + 1, 1)
            norm("n_mix", PAIR, XS0["ffn0"])

            def ffn(layer):
                name = f"ffn{layer}"
                n0, b0 = SLAB0[name] // 2, BLK0[name]
                hr0 = layer * 22 * NT

                def gate_up(slab2, blk, chunk, first=False):
                    for j in range(2):
                        two = first and j == 0
                        if not two:
                            hi(slab2 + (2 * j + 1) // 2, 1)
                        for t, (t0, n) in enumerate(TILES):
                            act_e.wait_ge(acc_ready, ready(blk + 2 * j, t, two))
                            act_e.wait_ge(hid_ready, chunk * NT + (j * NT + t + 1))
                            A(act[:, t0:t0 + n], acc(2 * j, t), ACT.Sigmoid).then_inc(sig_ready, 1)
                        hi(slab2 + (2 * j + 2) // 2, 0)
                        for t, (t0, n) in enumerate(TILES):
                            act_e.wait_ge(act_ready, chunk * NT + (j * NT + t + 1))
                            A(hid_hi[gate_up.par][:, j, t0:t0 + n], act[:, t0:t0 + n], ACT.Copy)\
                                .then_inc(hid_hi_ready, 1)

                def down(slab2, squares=False):
                    hi(slab2, 1)
                    if not squares:
                        hi(slab2 + 1, 0)
                    else:
                        for m in range(C):
                            block_squares(f"n_ffn{layer}", y, m, acc_free, ACCS + NT * (b0 + 124 + m + 1))

                c0 = layer * 22
                gate_up.par = 0
                gate_up(n0, b0, c0, True)
                with act_e.Fori(0, 5) as i:
                    gate_up.par = 1
                    gate_up(i * 6 + (n0 + 2), i * 24 + (b0 + 4), i * 4 + (c0 + 2))
                    down(i * 6 + (n0 + 4))
                    gate_up.par = 0
                    gate_up(i * 6 + (n0 + 5), i * 24 + (b0 + 16), i * 4 + (c0 + 4))
                    down(i * 6 + (n0 + 7))
                down(n0 + 32, True)

            def ple(layer):
                for tb, (t0, n) in enumerate(TOKB):
                    q = layer * NTB + tb
                    act_e.wait_ge(p_tr, q + 1)
                    A(pT_hi[:, :, t0:t0 + n], psum[:, tb % 6, 0:2 * P].rearrange("p (c t) -> p c t", c=2)[:, :, 0:n],
                      ACT.Copy).then_inc(p_hi_ready, 1)
                for u in range(2):
                    n = SLAB0[f"pp{layer}"] + u
                    act_e.wait_ge(raw_landed[u], 16 * (n // 2 + 1))
                    A(wp_hi[:, u, :], raw[u][:, :], ACT.Copy).then_inc(hi_ready, 1)
                hi_run(SLAB0[f"pg{layer}"], 1)
                norm(f"n_ffn{layer}", POST, XS0[f"pg{layer}"], raw_split=True)
                n0, b0 = SLAB0[f"pg{layer}"], BLK0[f"pg{layer}"]
                for m in range(C):
                    if n0 + m + 1 < SLABS:
                        nxt = n0 + m + 1
                        hi(nxt // 2, nxt % 2, ROW_KV if nxt == SLAB0["k"] else None)
                    for t, (t0, n) in enumerate(TILES):
                        q = (layer * C + m) * NT + t
                        act_e.wait_ge(acc_ready, NT * (b0 + 2 * m + 1) + t + 1)
                        if q >= NT:
                            act_e.wait_ge(ple_added, q + 1 - NT)
                        A(act[:, t0:t0 + n], acc(b0 + 2 * m + 1, t), ACT.Sigmoid).then_inc(ple_sig, 1)
                    if layer == 0 and m:
                        block_squares("n_kv", h, m - 1, ple_added, NT * m)
                if layer == 0:
                    block_squares("n_kv", h, C - 1, ple_added, NT * C)

            ffn(0)
            ple(0)

            act_e.wait_ge(ple_added, C * NT)
            hi_run(SLAB0["k"] + 1, 1, ROW_KV)
            norm("n_kv", PRE, XS0["kvq"])
            act_e.wait_ge(wf_landed, 32)
            for c in range(C):
                ins = A(wf_hi[:, c, :], wf_raw[:, c, :], ACT.Copy, scale=vecT[:, c, ROW_KV:ROW_KV + 1])
            ins.then_inc(wf_hi_s, 1)
            hi_run(SLAB0["k"] + 2, 6, ROW_KV)
            hi_run(SLAB0["q"], 1, ROW_G + 4)
            act_e.wait_ge(f_z, NT)
            A(flog[:, :], fz[:, :], ACT.Abs).then_inc(f_act, 1)
            act_e.wait_ge(f_act, 1)
            A(flog[:, :], flog[:, :], ACT.Exp, scale=-1.0).then_inc(f_act, 1)
            act_e.wait_ge(f_act, 2)
            A(flog[:, :], flog[:, :], ACT.Ln, bias=ones[0:H, :]).then_inc(f_act, 1)
            for m in range(C):
                hi_run(SLAB0["q"] + m + 1, 1, ROW_G + 4 if m < C - 1 else ROW_KV)
                row(TR_K, m, 6)
            row(TR_K, 8, 6)
            hi_run(SLAB0["v"] + 1, 7, ROW_KV)
            hi_run(SLAB0["o"], 1)
            act_e.wait_ge(acc_free, ACCS + NT * (BLK0["v"] + 8))
            act_e.wait_ge(aug_one, 1)
            for hh in range(2):
                A(k_low[hh][DH:DH + 4, :], k_raw[DH:DH + 4, :], ACT.Copy).then_inc(aug_one, 1)
                A(q_high[hh][DH:DH + 4, :], k_raw[DH:DH + 4, :], ACT.Copy, scale=-1.0).then_inc(aug_one, 1)
            act_e.wait_ge(f_step, 6)
            A(fsum_hi[:, :], fsum[:, :], ACT.Copy).then_inc(f_act, 1)
            act_e.wait_ge(consts, 6)
            A(causal_r[:, :], causal[:, :], ACT.Copy).then_inc(mask_ready, 1)
            A(ident_r[:, :], ident[:, :], ACT.Copy).then_inc(mask_ready, 1)
            for tb in range(NTB):
                row(TR_V, tb)

            act_e.sem_inc(exp_done, 4)
            act_e.sem_inc(pt_act, 1)

            def split(hp, hh):
                g = hp * 2 + hh
                act_e.wait_ge(head_landed, g * 64 + 64)
                if not (isinstance(hp, int) and hp == 0):
                    act_e.wait_ge(s_ready, hp * 16 + (8 * hh - 8))
                else:
                    act_e.wait_ge(fs_stored, 32)
                A(k_hh[hh][:, :], k_raw[:, :], ACT.Copy).then_inc(split_act, 1)
                A(q_hl[hh][:, :], q_raw[:, :], ACT.Copy).then_inc(split_act, 1)
                A(q_high[hh][0:DH, :], q_raw[0:DH, :], ACT.Copy).then_inc(split_act, 1)

            def exps(hp, j):
                act_e.wait_ge(s_max, hp * NI + (j + 1))
                jj = j % NI
                if j >= 2:
                    act_e.wait_ge(pt_ready, gcount(hp, groups(j - 2)[-1][0] + 1))
                elif not (isinstance(hp, int) and hp == 0):
                    act_e.wait_ge(pt_ready, hp * 26 + (j - 3))
                A(prob[j % 2][:, 0:(ITEMS[jj][1] + 1) * P], s_view(j), ACT.Exp, bias=nmx[:, j % 4:j % 4 + 1],
                  accum_out=rsum[:, j % 4:j % 4 + 1]).then_inc(exp_done, 1)

            def take_probT(hp, j):
                for g, kb, nb in groups(j):
                    if g % 2 == 0:
                        act_e.wait_ge(pt_ready, gcount(hp, g + 1))
                        act_e.wait_ge(pv_done, hp * NI + (j + 1))
                        A(probT[j % 2][:, kb:kb + nb, :], psum[:, 5, 0:nb * P].rearrange("p (c t) -> p c t", c=nb),
                          ACT.Copy).then_inc(pt_act, 1)

            def take_o(hp, g_ready):
                act_e.wait_ge(pt_ready, g_ready)
                A(qo[:, ds(hp, 1), 512:SEQ].rearrange("p o t -> p (o t)"), psum[:, 5, :], ACT.Copy).then_inc(pt_act, 1)

            def pair(hp, first, last):
                for j in range(NI):
                    if not (last and j == NI - 1):
                        exps(hp, j + 1)
                    take_probT(hp, j)
                    if j == 2:
                        split(hp, 1)
                    elif j == 10 and not last:
                        split(hp + 1, 0)
                    if j == 1 and not first:
                        take_o(hp - 1, gcount(hp, OT_AT + 2))

            split(0, 0)
            exps(0, 0)
            pair(0, True, False)
            with act_e.Fori(1, HP - 1) as hp:
                pair(hp, False, False)
            pair(HP - 1, False, True)
            take_o(HP - 1, 26 * HP)

            act_e.sem_inc(st_act, 1 + 2)
            act_e.sem_inc(ss_exp, 2)

            def page_half(pg, count):
                act_e.wait_ge(st_ready, count)
                A(kT[pg // 4][:, 0:4, (pg % 4) * P:(pg % 4 + 1) * P],
                  psum[:, 4, :].rearrange("p (c t) -> p c t", c=4), ACT.Copy).then_inc(st_act, 1)

            def sample_exps(b, par):
                act_e.wait_ge(ss_max, b + 1)
                A(sprob[:, 0:NK], psum[:, 2 * par:2 * par + 2, :].rearrange("p a b -> p (a b)"), ACT.Exp,
                  bias=sstat[:, 2:3], accum_out=sstat[:, 3:4]).then_inc(ss_exp, 1)
                A(sprob[:, NK:NK + NS], psum[:, 6, 0:NS], ACT.Exp,
                  bias=sstat[:, 2:3], accum_out=sstat[:, 4:5]).then_inc(ss_exp, 1)

            def sample_probT(b, count):
                act_e.wait_ge(spv_done, b * 2 + 2)
                act_e.wait_ge(st_ready, count + 1)
                A(sprobT[:, 0:4, :], psum[:, 4, :].rearrange("p (c t) -> p c t", c=4), ACT.Copy).then_inc(st_act, 1)
                act_e.wait_ge(st_ready, count + 3)
                A(sprobT[0:NS, 8, :], psum[0:NS, 4, 0:P], ACT.Copy).then_inc(st_act, 1)

            def out_rows(b):
                act_e.wait_ge(spv_done, b * 2 + 3)
                A(o_rows[:, 0:512], psum[:, 6, :], ACT.Copy, scale=sstat[:, 6:7]).then_inc(so_rows, 1)

            def out_back(b):
                act_e.wait_ge(so_tr, b * 2 + 2)
                cols = ds(b * NQ + SEQ, NQ)
                po = psum[:, 6, :].rearrange("p (c n) -> p c n", c=4)
                A(qo[0:DH, 0:4, cols], po[0:DH, :, 0:NQ], ACT.Copy).then_inc(so_taken, 1)
                A(qo[DH:P, 0:4, cols], po[DH:P, :, NQ:2 * NQ], ACT.Copy).then_inc(so_taken, 1)

            def next_in(b, count):
                act_e.wait_ge(st_ready, count + 1)
                if not (isinstance(b, int) and b == 0):
                    act_e.wait_ge(cum_ready, b)
                A(lf_pageT[:, 0:512], psum[0:H, 4, :], ACT.Copy).then_inc(st_act, 1)
                for pg in range(4):
                    page_half(pg, count + (3 + 2 * pg))
                    if pg == 0 and not (isinstance(b, int) and b < 2):
                        out_back(b - 2)

            def sequence(b, par, first, last):
                n0 = st_before(b)[0]
                for pg in range(4, 8):
                    page_half(pg, n0 + (2 * (pg - 4) + 1))
                    if pg == 5 and not first:
                        sample_exps(b - 1, 1 - par)
                if not first:
                    sample_probT(b - 1, n0 + 8)
                    out_rows(b - 1)
                if not last:
                    next_in(b + 1, st_mid(b, first)[0])

            next_in(0, 3)
            sequence(0, 0, True, False)
            with act_e.Fori(0, NB // 2 - 1) as i:
                sequence(i * 2 + 1, 1, False, False)
                sequence(i * 2 + 2, 0, False, False)
            sequence(NB - 1, 1, False, True)
            out_back(NB - 2)
            sample_exps(NB - 1, 1)
            sample_probT(NB - 1, 21 * NB)
            out_rows(NB - 1)
            out_back(NB - 1)

            act_e.wait_ge(so_taken, 4 * NB)
            for t, (t0, n) in enumerate(TILES):
                A(xs_hi[:, :, t0:t0 + n], qo[:, :, t0:t0 + n], ACT.Copy).then_inc(xs_hi_ready, 1)
            for m in range(C):
                hi_run(SLAB0["o"] + 1 + m, 1)
                block_squares("n_att", y, m, acc_free, ACCS + NT * (BLK0["o"] + m + 1))
            hi_run(SLAB0["ffn1"] + 1, 1)
            norm("n_att", PAIR, XS0["ffn1"])
            ffn(1)
            ple(1)
            act_e.wait_ge(ple_added, 2 * C * NT)
            for tb in range(NTB):
                row(TR_Y, tb)

        @block.vector
        def _(dve):
            V = nc.vector

            def copy(out, in_):
                return V.tensor_scalar(out, in_, 1.0, None, ALU.mult)

            def lo(n2, slot, gain=None):
                dve.wait_ge(hi_ready, n2 * 2 + (slot + 1))
                if gain is None:
                    V.tensor_tensor(w_lo[slot][:, :], raw[slot][:, :], w_hi[slot][:, :].bitcast(F32), ALU.subtract)\
                        .then_inc(lo_ready, 1)
                else:
                    for c in range(C):
                        part = slice(c * P, (c + 1) * P)
                        ins = V.scalar_tensor_tensor(w_lo[slot][:, part], raw[slot][:, part],
                                                     vecT[:, c, gain:gain + 1], w_hi[slot][:, part].bitcast(F32),
                                                     ALU.mult, ALU.subtract)
                    ins.then_inc(lo_ready, 1)

            def lo_run(n, count, gain=None):
                for j in range(n, n + count):
                    lo(j // 2, j % 2, gain)

            def tile_ready(blk, t, last=False, two=False, second=0):
                dve.wait_ge(acc_ready, ready(blk, t, two, second))
                if last:
                    dve.sem_inc(slab_used, 1)

            def norm(name, seq, ysrc, post_row, pre_row, xs0, raw_split=False):
                s0, pending = STEP0[name], None
                for k, (kind, t) in enumerate(seq):
                    s = s0 + k
                    t0, n = TILES[t]
                    rb = psum[:, 6 + s % 2, 0:n]
                    dve.wait_ge(std_ready, s + 1)
                    V.reciprocal(rb, rb).then_inc(rb_ready, 1)
                    if kind == "pre" and t == 2:
                        dve.wait_ge(xs_ready, xs0 + 1)
                    dve.wait_ge(rb_ready, s + 1)
                    for c in range(C):
                        if kind == "post":
                            ins = V.scalar_tensor_tensor(ysrc[:, c, t0:t0 + n], ysrc[:, c, t0:t0 + n],
                                                         vecT[:, c, post_row:post_row + 1], rb, ALU.mult, ALU.mult)
                        elif pre_row is not None:
                            ins = V.scalar_tensor_tensor(xn[t % 2][:, c, 0:n], h[:, c, t0:t0 + n],
                                                         vecT[:, c, pre_row:pre_row + 1], rb, ALU.mult, ALU.mult)
                        else:
                            ins = V.tensor_tensor(xn[t % 2][:, c, 0:n], h[:, c, t0:t0 + n], rb, ALU.mult)
                    ins.then_inc(rb_used, 1)
                    if kind == "post":
                        dve.wait_ge(rb_used, s + 1)
                        V.tensor_tensor(h[:, :, t0:t0 + n], h[:, :, t0:t0 + n], ysrc[:, :, t0:t0 + n], ALU.add)\
                            .then_inc(h_ready, 1)
                    if pending is not None:
                        pending()
                        pending = None
                    if kind == "pre" or raw_split:
                        src = xn[t % 2][:, :, 0:n] if kind == "pre" else h[:, :, t0:t0 + n]

                        def pending(t=t, t0=t0, n=n, src=src):
                            dve.wait_ge(xs_hi_ready, xs0 + t + 1)
                            V.tensor_tensor(xs_lo[:, :, t0:t0 + n], src, xs_hi[:, :, t0:t0 + n].bitcast(F32),
                                            ALU.subtract).then_inc(xs_ready, 1)
                if pending is not None:
                    pending()

            def add_squares(name, m):
                p = PQ[name]
                dve.wait_ge(psq_ready, 8 * p + m + 1)
                if m >= 2:
                    dve.wait_ge(psq_added, 7 * p + m - 1)
                V.tensor_tensor(SSUM[name][:, :], SSUM[name][:, :], PSQ[name][m % 2][:, :], ALU.add)\
                    .then_inc(psq_added, 1)

            dve.sem_inc(acc_free, ACCS)
            dve.sem_inc(lo_ready, RAWS)
            dve.sem_inc(slab_used, HLS)
            dve.sem_inc(hid_ready, NT)
            for tb, (t0, n) in enumerate(TOKB):
                dve.wait_ge(tr_ready, 2 * (TR_X + tb) + 2)
                bank = 2 * (tb % 3) + 1
                V.tensor_copy(h[:, 4:8, t0:t0 + n], psum[:, bank, :].rearrange("p (c t) -> p c t", c=4)[:, :, 0:n])\
                    .then_inc(tr_dve, 1)

            def row(tr0, tb, bank=None):
                g, r, n = tr0 + tb, ROWS0[tr0] + tb, TOKB[tb][1]
                bank = 2 * (g % 3) + 1 if bank is None else bank
                dve.wait_ge(tr_ready, 2 * g + 2)
                if tr0 == TR_V and tb < 8:
                    V.tensor_copy(v_keys[:, tb, 512:D], psum[:, bank, :]).then_inc(tr_dve, 1)
                    return
                if r >= 2:
                    dve.wait_ge(rows_stored[r % 2], 16 * (r // 2))
                V.tensor_copy(rows_out[r % 2][0:n, 512:D], psum[0:n, bank, :]).then_inc(tr_dve, 1)

            dve.wait_ge(vec_done, 1)
            lo_run(0, 1)
            dve.wait_ge(tr_act, NTB)
            dve.wait_ge(tr_dve, NTB)
            norm("n_in", PRE, None, None, ROW_G + 0, XS0["in"])

            V.memset(cup[:, 0:2], 0.0).then_inc(conv_step, 1)
            with dve.Fori(0, C // 2) as i:
                for u in range(2):
                    m = i * 2 + u
                    mm = ds(m, 1)
                    base = i * (2 * CONV_STEPS) + u * CONV_STEPS + 1
                    done = [0]

                    def step(ins):
                        ins.then_inc(conv_step, 1)
                        done[0] += 1

                    def after(k):
                        dve.wait_ge(conv_step, base + k)

                    def f(t):
                        return t.rearrange("p o t -> p (o t)")

                    blk = i * 6 + 3 * u
                    for part, dst in enumerate((bgate, zconv)):
                        nxt = 3 * u + part + 1
                        lo(i * 3 + nxt // 2, nxt % 2)
                        for t, (t0, n) in enumerate(TILES):
                            tile_ready(blk + part, t, t == NT - 1)
                            copy(f(dst[:, mm, t0:t0 + n]), acc(3 * u + part, t)).then_inc(acc_free, 1)
                    nxt = 3 * u + 3
                    lo(i * 3 + nxt // 2, nxt % 2)
                    dve.wait_ge(conv_step, base)
                    dve.wait_ge(acc_free, blk * NT + (ACCS + 2 * NT))
                    for t, (t0, n) in enumerate(TILES):
                        tile_ready(blk + 2, t, t == NT - 1)
                        np_ = min(t0 + n, SEQ) - t0
                        ins = V.tensor_tensor(cup[:, 2 + t0:2 + t0 + np_], f(zconv[:, mm, t0:t0 + np_]),
                                              acc(3 * u + 2, t)[:, 0:np_], ALU.mult)
                        if np_ < n:
                            step(ins)
                            ins = V.tensor_tensor(cup_s[:, :, 2:], f(zconv[:, mm, SEQ:T]).rearrange("p (b t) -> p b t", b=NB),
                                                  acc(3 * u + 2, t)[:, np_:n].rearrange("p (b t) -> p b t", b=NB), ALU.mult)
                        ins.then_inc(acc_free, 1)
                    step(copy(cup_s[:, :, 0:2], f(vecT[:, mm, ROW_STATE:ROW_STATE + 2 * NB])
                                       .rearrange("p (b t) -> p b t", b=NB)))
                    after(2)
                    dve.wait_ge(acc_free, blk * NT + (ACCS + 3 * NT))
                    step(copy(f(convT[:, mm, 0:2]), cup[:, SEQ:SEQ + 2]))
                    step(copy(f(convT[:, mm, 2:]).rearrange("p (b t) -> p b t", b=NB),
                                       cup_s[:, :, NQ:NQ + 2]))
                    zp = f(zconv[:, mm, 0:SEQ])
                    zs = f(zconv[:, mm, SEQ:T]).rearrange("p (b t) -> p b t", b=NB)
                    for k in range(3):
                        wk = vecT[:, mm, ROW_CONV + k:ROW_CONV + k + 1].rearrange("p a b -> p (a b)")
                        if k == 0:
                            step(V.tensor_scalar(zp, cup[:, 0:SEQ], wk, None, ALU.mult))
                            step(V.tensor_scalar(zs, cup_s[:, :, 0:NQ], wk, None, ALU.mult))
                        else:
                            after(4 + 2 * k)
                            step(V.scalar_tensor_tensor(zp, cup[:, k:k + SEQ], wk, zp, ALU.mult, ALU.add))
                            step(V.scalar_tensor_tensor(zs, cup_s[:, :, k:k + NQ], wk, zs, ALU.mult, ALU.add))
                    after(10)
                    step(V.tensor_tensor(f(zconv[:, mm, 0:544]), f(zconv[:, mm, 0:544]), f(bgate[:, mm, 0:544]), ALU.mult))
                    step(V.tensor_tensor(f(zconv[:, mm, 544:T]), f(zconv[:, mm, 544:T]), f(bgate[:, mm, 544:T]), ALU.mult))
                    assert done[0] == 12
                    dve.sem_inc(conv_step, 1)
                    after(CONV_STEPS - 1)
                    dve.sem_inc(conv_step, 1)
                    dve.wait_ge(z_hi, i * 2 + (u + 1))
                    V.tensor_tensor(f(mix_lo[:, mm, :]), f(zconv[:, mm, :]), f(mix_hi[:, mm, :]).bitcast(F32), ALU.subtract)\
                        .then_inc(mix_ready, 1)

            def plain(name, dst, gain_next, scale=None, gain=None, squares=None, after=None, two=False):
                n0, b0 = SLAB0[name], BLK0[name]
                for m in range(C):
                    if two and m == 0:
                        pass
                    elif m < C - 1:
                        lo_run(n0 + m + 1, 1, gain)
                    elif gain_next != "none":
                        lo_run(n0 + m + 1, 1, gain_next)
                    for t, (t0, n) in enumerate(TILES):
                        tile_ready(b0 if two and m < 2 else b0 + m, t, t == NT - 1, two and m < 2,
                                   1 if two and m == 1 else 0)
                        if scale is None:
                            V.tensor_copy(dst[:, m, t0:t0 + n], acc(b0 + m, t)).then_inc(acc_free, 1)
                        else:
                            V.tensor_scalar(dst[:, m, t0:t0 + n], acc(b0 + m, t), scale, None, ALU.mult)\
                                .then_inc(acc_free, 1)
                    if squares and m > 1:
                        add_squares(squares, m - 1)
                    if after:
                        after(m)
                if squares:
                    add_squares(squares, C - 1)

            plain("out", y_mix, None, squares="n_mix")
            dve.wait_ge(acc_free, ACCS + NT * (BLK0["out"] + 8))
            lo_run(SLAB0["ffn0"] + 1, 1)
            norm("n_mix", PAIR, y_mix, ROW_G + 1, ROW_G + 2, XS0["ffn0"])

            def ffn(layer):
                name = f"ffn{layer}"
                n0, b0, c0 = SLAB0[name] // 2, BLK0[name], layer * 22

                def gate_up(slab2, blk, chunk, par, first=False):
                    for j in range(2):
                        two = first and j == 0
                        if not two:
                            lo(slab2 + (2 * j + 1) // 2, 1)
                        for t, (t0, n) in enumerate(TILES):
                            tile_ready(blk + 2 * j, t, t == NT - 1, two)
                            dve.wait_ge(sig_ready, chunk * NT + (j * NT + t + 1))
                            V.tensor_tensor(act[:, t0:t0 + n], act[:, t0:t0 + n], acc(2 * j, t), ALU.mult)\
                                .then_inc(acc_free, 1)
                        lo(slab2 + (2 * j + 2) // 2, 0)
                        dve.wait_ge(acc_free, blk * NT + (ACCS + (2 * j + 1) * NT))
                        for t in range(NT + 1):
                            if t < NT:
                                t0, n = TILES[t]
                                tile_ready(blk + 2 * j, t, t == NT - 1, two, 1)
                                V.tensor_tensor(act[:, t0:t0 + n], act[:, t0:t0 + n], acc(2 * j + 1, t), ALU.mult)\
                                    .then_inc(act_ready, 1)
                                dve.wait_ge(act_ready, chunk * NT + (j * NT + t + 1))
                                dve.sem_inc(acc_free, 1)
                            if t > 0:
                                t0, n = TILES[t - 1]
                                dve.wait_ge(hid_hi_ready, chunk * NT + (j * NT + t))
                                V.tensor_tensor(hid_lo[par][:, j, t0:t0 + n], act[:, t0:t0 + n],
                                                hid_hi[par][:, j, t0:t0 + n].bitcast(F32), ALU.subtract)\
                                    .then_inc(hid_ready, 1)

                def down(slab2, blk, squares=None):
                    for s in range(2):
                        if s == 0:
                            lo(slab2, 1)
                        elif not squares:
                            lo(slab2 + 1, 0)
                        if s == 0:
                            dve.wait_ge(acc_free, blk * NT + ACCS)
                        for m in range(4):
                            for t, (t0, n) in enumerate(TILES):
                                tile_ready(blk + 4 * s + m, t, m == 3 and t == NT - 1)
                                yy = y[:, 4 * s + m, t0:t0 + n]
                                V.tensor_tensor(yy, yy, acc(m, t), ALU.add).then_inc(acc_free, 1)
                            if squares and 4 * s + m > 1:
                                add_squares(squares, 4 * s + m - 1)
                    if squares:
                        add_squares(squares, C - 1)

                gate_up(n0, b0, c0, 0, True)
                dve.wait_ge(y_zero, layer + 1)
                with dve.Fori(0, 5) as i:
                    gate_up(i * 6 + (n0 + 2), i * 24 + (b0 + 4), i * 4 + (c0 + 2), 1)
                    down(i * 6 + (n0 + 4), i * 24 + (b0 + 8))
                    gate_up(i * 6 + (n0 + 5), i * 24 + (b0 + 16), i * 4 + (c0 + 4), 0)
                    down(i * 6 + (n0 + 7), i * 24 + (b0 + 20))
                down(n0 + 32, b0 + 124, f"n_ffn{layer}")

            def ple(layer):
                for tb, (t0, n) in enumerate(TOKB):
                    dve.wait_ge(p_hi_ready, layer * NTB + tb + 1)
                    V.tensor_tensor(pT_lo[:, :, t0:t0 + n],
                                    psum[:, tb % 6, 0:2 * P].rearrange("p (c t) -> p c t", c=2)[:, :, 0:n],
                                    pT_hi[:, :, t0:t0 + n].bitcast(F32), ALU.subtract).then_inc(p_ready, 1)
                for u in range(2):
                    dve.wait_ge(hi_ready, SLAB0[f"pp{layer}"] + u + 1)
                    V.tensor_tensor(wp_lo[:, u, :], raw[u][:, :], wp_hi[:, u, :].bitcast(F32), ALU.subtract)\
                        .then_inc(lo_ready, 1)
                    dve.sem_inc(slab_used, 1)
                lo_run(SLAB0[f"pg{layer}"], 1)
                dve.wait_ge(acc_free, ACCS + NT * BLK0[f"pg{layer}"])
                norm(f"n_ffn{layer}", POST, y, ROW_G + 4 * layer + 3, None, XS0[f"pg{layer}"], raw_split=True)
                n0, b0 = SLAB0[f"pg{layer}"], BLK0[f"pg{layer}"]
                for m in range(C):
                    if n0 + m + 1 < SLABS:
                        lo_run(n0 + m + 1, 1, ROW_KV if n0 + m + 1 == SLAB0["k"] else None)
                    for t, (t0, n) in enumerate(TILES):
                        q = (layer * C + m) * NT + t
                        tile_ready(b0 + 2 * m, t)
                        tile_ready(b0 + 2 * m + 1, t, t == NT - 1)
                        dve.wait_ge(ple_sig, q + 1)
                        V.tensor_tensor(act[:, t0:t0 + n], act[:, t0:t0 + n], acc(b0 + 2 * m, t), ALU.mult)\
                            .then_inc(ple_mul, 1)
                        dve.wait_ge(ple_mul, q + 1)
                        dve.sem_inc(acc_free, 2)
                        V.tensor_tensor(h[:, m, t0:t0 + n], h[:, m, t0:t0 + n], act[:, t0:t0 + n], ALU.add)\
                            .then_inc(ple_added, 1)
                    if layer == 0 and m > 1:
                        add_squares("n_kv", m - 1)
                if layer == 0:
                    add_squares("n_kv", C - 1)

            ffn(0)
            ple(0)
            dve.wait_ge(ple_added, C * NT)
            lo_run(SLAB0["k"] + 1, 1, ROW_KV)
            norm("n_kv", PRE, None, None, None, XS0["kvq"])
            dve.wait_ge(wf_hi_s, 1)
            for c in range(C):
                ins = V.scalar_tensor_tensor(wf_lo[:, c, :], wf_raw[:, c, :], vecT[:, c, ROW_KV:ROW_KV + 1],
                                             wf_hi[:, c, :].bitcast(F32), ALU.mult, ALU.subtract)
            ins.then_inc(wf_lo_s, 1)
            plain("k", y, ROW_G + 4, gain=ROW_KV, two=True)
            for t, (t0, n) in enumerate(TILES):
                dve.wait_ge(f_acc, t + 1)
                V.tensor_scalar(fz[:, t0:t0 + n], psum[0:H, 6 + t % 2, 0:n], bf[:, 0:1], None, ALU.add).then_inc(f_z, 1)
            dve.wait_ge(f_act, 3)
            V.scalar_tensor_tensor(flog[:, :], fz[:, :], 0.0, flog[:, :], ALU.min, ALU.subtract)\
                .then_inc(f_step, 1)

            def key_row(m):
                if m == 0:
                    dve.wait_ge(f_tr, 1)
                    V.tensor_copy(lf[:, :, :], psum[:, 6, 0:NTB * H].rearrange("p (b n) -> p b n", b=NTB))\
                        .then_inc(f_step, 1)
                row(TR_K, m, 7)

            plain("q", qo, ROW_KV, scale=SCALE, gain=ROW_G + 4, after=key_row)
            row(TR_K, 8, 7)
            V.memset(segm[:, :], 1.0).then_inc(f_step, 1)
            V.memset(one16[:, :], 1.0).then_inc(f_step, 1)
            dve.wait_ge(f_step, 4)
            V.memset(segm[:, :].rearrange("p (b t) -> p b t", b=NB)[:, :, 0:1], 0.0).then_inc(f_step, 1)
            dve.wait_ge(kT_stored, 16)
            plain("v", vT, None, gain=ROW_KV)
            dve.wait_ge(f_tr, 3)
            dve.wait_ge(f_step, 5)
            V.tensor_tensor_scan(fsum[:, :], one16[:, :].broadcast_to([H, SEQ]),
                                 psum[0:H, 6:8, :].rearrange("p a b -> p (a b)"), 0.0,
                                 ALU.mult, ALU.add).then_inc(f_step, 1)
            dve.wait_ge(f_step, 6)
            V.memset(k_raw[DH:DH + 4, :], 1.0).then_inc(aug_one, 1)
            dve.wait_ge(f_act, 4)
            V.tensor_tensor(fsum_lo[:, :], fsum[:, :], fsum_hi[:, :].bitcast(F32), ALU.subtract)\
                .then_inc(f_step, 1)
            dve.wait_ge(f_tr, 4)
            V.tensor_tensor_scan(fsum_new[:, :], segm[:, :], psum[0:H, 5, P - NS:P], 0.0, ALU.mult, ALU.add)\
                .then_inc(f_step, 1)
            for tb in range(NTB):
                row(TR_V, tb)

            dve.sem_inc(pt_dve, 1)
            dve.sem_inc(o_taken, 1)

            def split(hp, hh):
                g = hp * 2 + hh
                dve.wait_ge(split_act, g * 3 + 1)
                V.tensor_tensor(k_low[hh][0:DH, :], k_raw[0:DH, :], k_hh[hh][0:DH, :].bitcast(F32), ALU.subtract)\
                    .then_inc(split_dve, 1)
                dve.wait_ge(split_act, g * 3 + 2)
                V.tensor_tensor(q_hl[hh][DH:P, :], q_raw[DH:P, :], q_hl[hh][DH:P, :].bitcast(F32), ALU.subtract)\
                    .then_inc(split_dve, 1)

            def maxes(hp, j):
                dve.wait_ge(s_ready, hp * NI + (j + 1))
                V.reduce_max(nmx[:, j % 4:j % 4 + 1], s_view(j), AX_X, negate=True).then_inc(s_max, 1)

            def take_probT(hp, j):
                for g, kb, nb in groups(j):
                    if g % 2:
                        dve.wait_ge(pt_ready, gcount(hp, g + 1))
                        dve.wait_ge(pv_done, hp * NI + (j + 1))
                        V.tensor_copy(probT[j % 2][:, kb:kb + nb, :],
                                      psum[:, 6, 0:nb * P].rearrange("p (c t) -> p c t", c=nb)).then_inc(pt_dve, 1)

            def normed(hp, j):
                it = hp * NI
                hh, qb = ITEMS[j]
                dve.wait_ge(exp_done, it + (j + 5))
                V.reciprocal(rinv[:, j % 2:j % 2 + 1], rsum[:, j % 4:j % 4 + 1]).then_inc(rinv_s, 1)
                dve.wait_ge(rinv_s, it + (j + 1))
                dve.wait_ge(pv_done, it + (j + 3))
                V.tensor_scalar(o_pair[:, qb, DH * hh:DH * hh + DH], psum[:, 7, 0:DH], rinv[:, j % 2:j % 2 + 1],
                                None, ALU.mult).then_inc(o_taken, 1)

            def take_o(hp, g_ready):
                dve.wait_ge(pt_ready, g_ready)
                V.tensor_scalar(qo[:, ds(hp, 1), 0:512].rearrange("p o t -> p (o t)"), psum[:, 6, :], 1.0, None,
                                ALU.mult).then_inc(pt_dve, 1)

            def pair(hp, first, last):
                for j in range(NI):
                    if not (last and j >= NI - 2):
                        maxes(hp, j + 2)
                    take_probT(hp, j)
                    if j == 3:
                        split(hp, 1)
                    elif j == 11 and not last:
                        split(hp + 1, 0)
                    if j == 1 and not first:
                        take_o(hp - 1, gcount(hp, OT_AT + 1))
                        dve.wait_ge(pt_ready, gcount(hp, OT_AT + 2))
                    if j > 0:
                        normed(hp, j - 1)
                    elif not first:
                        normed(hp - 1, NI - 1)

            split(0, 0)
            maxes(0, 0)
            maxes(0, 1)
            pair(0, True, False)
            with dve.Fori(1, HP - 1) as hp:
                pair(hp, False, False)
            pair(HP - 1, False, True)
            normed(HP - 1, NI - 1)
            take_o(HP - 1, 26 * HP - 1)

            dve.sem_inc(st_dve, 1 + 1)
            dve.sem_inc(kpage_used, 4)

            def page_half(pg, count):
                dve.wait_ge(st_ready, count)
                dve.sem_inc(kpage_used, 1)
                V.tensor_copy(kT[pg // 4][:, 4:8, (pg % 4) * P:(pg % 4 + 1) * P],
                              psum[:, 5, :].rearrange("p (c t) -> p c t", c=4)).then_inc(st_dve, 1)

            def queries(b, par):
                cols = ds(b * NQ + SEQ, NQ)
                copy(qdiag[par][0:DH, :, 0:NQ], qo[0:DH, :, cols]).then_inc(qbd_ready, 1)
                copy(qdiag[par][DH:P, :, NQ:2 * NQ], qo[DH:P, :, cols]).then_inc(qbd_ready, 1)

            def sample_max(b, par):
                dve.wait_ge(ss_ready, b + 1)
                V.reduce_max(sstat[:, 0:1], psum[:, 2 * par:2 * par + 2, :].rearrange("p a b -> p (a b)"), AX_X,
                             negate=True).then_inc(sp_step, 1)
                V.reduce_max(sstat[:, 1:2], psum[:, 6, 0:NS], AX_X, negate=True).then_inc(sp_step, 1)
                dve.wait_ge(sp_step, b * 4 + 2)
                V.tensor_tensor(sstat[:, 2:3], sstat[:, 0:1], sstat[:, 1:2], ALU.min).then_inc(ss_max, 1)

            def row_sums(b):
                dve.wait_ge(ss_exp, b * 2 + 4)
                V.tensor_tensor(sstat[:, 5:6], sstat[:, 3:4], sstat[:, 4:5], ALU.add).then_inc(sp_step, 1)
                dve.wait_ge(sp_step, b * 4 + 3)
                V.reciprocal(sstat[:, 6:7], sstat[:, 5:6]).then_inc(sp_step, 1)

            def sample_out(b, count):
                dve.wait_ge(spv_done, b * 2 + 2)
                dve.wait_ge(st_ready, count + 2)
                V.tensor_copy(sprobT[:, 4:8, :], psum[:, 5, :].rearrange("p (c t) -> p c t", c=4)).then_inc(st_dve, 1)
                dve.wait_ge(spv_done, b * 2 + 4)
                V.tensor_scalar(o_rows[:, 512:1024], psum[:, 7, :], sstat[:, 6:7], None, ALU.mult).then_inc(so_rows, 1)

            def out_back(b):
                dve.wait_ge(so_tr, b * 2 + 2)
                cols = ds(b * NQ + SEQ, NQ)
                po = psum[:, 7, :].rearrange("p (c n) -> p c n", c=4)
                copy(qo[0:DH, 4:8, cols], po[0:DH, :, DH:DH + NQ]).then_inc(so_taken, 1)
                copy(qo[DH:P, 4:8, cols], po[DH:P, :, DH + NQ:DH + 2 * NQ]).then_inc(so_taken, 1)

            def next_in(b, par, count, act_count, dve_count):
                dve.wait_ge(st_ready, count + 2)
                if not (isinstance(b, int) and b == 0):
                    dve.wait_ge(cum_ready, b)
                V.tensor_copy(lf_pageT[:, 512:1024], psum[0:H, 5, :]).then_inc(st_dve, 1)
                for pg in range(4):
                    page_half(pg, count + (4 + 2 * pg))
                    if pg == 0:
                        dve.wait_ge(st_act, act_count + 2)
                        dve.wait_ge(st_dve, dve_count + 2)
                        V.tensor_tensor_scan(cum[:, :], one16[:, :].broadcast_to([H, NK]), lf_pageT[:, :], 0.0,
                                             ALU.mult, ALU.add).then_inc(cum_ready, 1)
                    elif pg == 1:
                        dve.wait_ge(cum_ready, b + 1)
                        V.tensor_scalar(cum_new[par][:, :], fsum_new[:, :], cum[:, NK - 1:NK], None, ALU.add)\
                            .then_inc(fb_ready, 1)
                    if pg == 0 and not (isinstance(b, int) and b < 2):
                        out_back(b - 2)

            def sequence(b, par, first, last):
                n0 = st_before(b)[0]
                for pg in range(4, 8):
                    page_half(pg, n0 + (2 * (pg - 4) + 2))
                    if pg == 4 and not first:
                        sample_max(b - 1, 1 - par)
                    elif pg == 6 and not first:
                        row_sums(b - 1)
                if not last:
                    queries(b + 1, 1 - par)
                if not first:
                    sample_out(b - 1, n0 + 8)
                if not last:
                    next_in(b + 1, 1 - par, *st_mid(b, first))

            dve.wait_ge(qbd_zero, 2)
            queries(0, 0)
            next_in(0, 0, 3, 2, 1)
            sequence(0, 0, True, False)
            with dve.Fori(0, NB // 2 - 1) as i:
                sequence(i * 2 + 1, 1, False, False)
                sequence(i * 2 + 2, 0, False, False)
            sequence(NB - 1, 1, False, True)
            out_back(NB - 2)
            sample_max(NB - 1, 1)
            row_sums(NB - 1)
            sample_out(NB - 1, 21 * NB)
            out_back(NB - 1)

            for t, (t0, n) in enumerate(TILES):
                dve.wait_ge(xs_hi_ready, XS0["o"] + t + 1)
                if t == 0:
                    dve.wait_ge(so_taken, 4 * NB)
                V.tensor_tensor(xs_lo[:, :, t0:t0 + n], qo[:, :, t0:t0 + n], xs_hi[:, :, t0:t0 + n].bitcast(F32),
                                ALU.subtract).then_inc(xs_ready, 1)
            plain("o", y, None, squares="n_att")
            dve.wait_ge(acc_free, ACCS + NT * (BLK0["o"] + 8))
            lo_run(SLAB0["ffn1"] + 1, 1)
            norm("n_att", PAIR, y, ROW_G + 5, ROW_G + 6, XS0["ffn1"])
            ffn(1)
            ple(1)
            dve.wait_ge(ple_added, 2 * C * NT)
            for tb in range(NTB):
                row(TR_Y, tb)

        @block.tensor
        def _(pe):
            M = nc.tensor.matmul

            def three(out, wh, wl, xh, xl, first, last):
                M(out, wh, xh, start=first, stop=False)
                M(out, wh, xl, start=False, stop=False)
                return M(out, wl, xh, start=False, stop=last)

            def slab(n, slot):
                pe.wait_ge(lo_ready, n + (RAWS + 1))

            def tile_in_parts(blocks, xh, xl, xs0, t):
                t0, n = TILES[t]
                pe.wait_ge(xs_hi_ready, xs0 + t + 1)
                for out, slot in blocks:
                    for c in range(C):
                        k = slice(c * P, (c + 1) * P)
                        M(out, w_hi[slot][:, k], xh[:, c, t0:t0 + n], start=c == 0, stop=False)
                        M(out, w_lo[slot][:, k], xh[:, c, t0:t0 + n], start=False, stop=False)
                pe.wait_ge(xs_ready, xs0 + t + 1)
                for out, slot in blocks:
                    for c in range(C):
                        k = slice(c * P, (c + 1) * P)
                        ins = M(out, w_hi[slot][:, k], xl[:, c, t0:t0 + n], start=False, stop=c == C - 1)
                    ins.then_inc(acc_ready, 1)

            def first_two(n, blk, xh, xl, xs0):
                slab(n, 0)
                slab(n + 1, 1)
                pe.wait_ge(acc_free, blk * NT + ACCS)
                for t in range(NT):
                    tile_in_parts([(acc(0, t), 0), (acc(1, t), 1)], xh, xl, xs0, t)

            def block8(blk, par, slot, xh, xl, xs0=None):
                for t, (t0, n) in enumerate(TILES):
                    pe.wait_ge(acc_free, blk * NT + (t + 1))
                    if xs0 is not None:
                        tile_in_parts([(acc(par, t), slot)], xh, xl, xs0, t)
                        continue
                    for c in range(C):
                        k = slice(c * P, (c + 1) * P)
                        ins = three(acc(par, t), w_hi[slot][:, k], w_lo[slot][:, k],
                                    xh[:, c, t0:t0 + n], xl[:, c, t0:t0 + n], c == 0, c == C - 1)
                    ins.then_inc(acc_ready, 1)

            def transposes_in(tr0, src_of):
                for tb, (t0, n) in enumerate(TOKB):
                    g = tr0 + tb
                    if g == TR_V + 2:
                        pe.wait_ge(f_step, 8)
                    if g >= 3:
                        pe.wait_ge(tr_act, g - 2)
                        pe.wait_ge(tr_dve, g - 2)
                    for half in range(2):
                        for c in range(4):
                            ins = src_of(tb, t0, n, half, c, 2 * (g % 3) + half)
                        ins.then_inc(tr_ready, 1)

            def norm(name, seq):
                all_ones = ones[:, 0:1].broadcast_to([P, P])
                for k, (kind, t) in enumerate(seq):
                    s = STEP0[name] + k
                    t0, n = TILES[t]
                    if s >= 2:
                        pe.wait_ge(rb_used, s - 1)
                    out = psum[:, 6 + s % 2, 0:n]
                    if kind == "post" or name == "n_kv":
                        pe.wait_ge(psq_added, 7 * PQ[name] + 7)
                        M(out, all_ones, SSUM[name][:, t0:t0 + n], start=True, stop=True).then_inc(post_sum, 1)
                        continue
                    for j in range(4):
                        q = SQ0[name] + 4 * t + j
                        pe.wait_ge(sq_ready, q + 1)
                        M(out, all_ones, sqp[q % 2][:, 0, 0:n], start=j == 0, stop=False)
                        M(out, all_ones, sqp[q % 2][:, 1, 0:n], start=False, stop=j == 3).then_inc(sq_used, 1)

            pe.sem_inc(sq_used, 2)
            pe.wait_ge(consts, 4)
            def x_in(tb, t0, n, half, c, bank):
                src = x_nat[:, tb, :] if tb < 8 else xs_nat[:, :]
                if half == 0 and c == 0:
                    pe.wait_ge(x_landed[tb], 16)
                f0 = (4 * half + c) * P
                return nc.tensor.transpose(psum[:, bank, c * P:c * P + n], src[:, f0:f0 + P], ident[0:n, 0:n])
            transposes_in(TR_X, x_in)
            pe.wait_ge(vec_landed, 64)
            for c in range(C):
                ins = nc.tensor.transpose(psum[:, 6, c * NVEC:(c + 1) * NVEC], vec_nat[:, c * P:(c + 1) * P],
                                          ident[0:NVEC, 0:NVEC])
            ins.then_inc(vec_tr, 1)
            pe.wait_ge(vec_done, 1)
            pe.wait_ge(tr_act, NTB)
            pe.wait_ge(tr_dve, NTB)
            norm("n_in", PRE)

            with pe.Fori(0, C // 2) as i:
                for u in range(6):
                    slab(i * 6 + u, u % 2)
                    block8(i * 6 + u, u, u % 2, xs_hi, xs_lo, XS0["in"])
            def plain(name, xh, xl, xs0=None, after=None, two=False, start=0):
                if two:
                    first_two(SLAB0[name], BLK0[name], xh, xl, xs0)
                for m in range(2 if two else start, C):
                    slab(SLAB0[name] + m, m % 2)
                    block8(BLK0[name] + m, m, m % 2, xh, xl, xs0)
                    if after:
                        after(m)

            slab(SLAB0["out"], 0)
            pe.wait_ge(mix_ready, C - 1)
            for t, (t0, n) in enumerate(TILES):
                pe.wait_ge(acc_free, BLK0["out"] * NT + (t + 1))
                for c in range(C - 1):
                    k = slice(c * P, (c + 1) * P)
                    three(acc(0, t), w_hi[0][:, k], w_lo[0][:, k], mix_hi[:, c, t0:t0 + n], mix_lo[:, c, t0:t0 + n],
                          c == 0, False)
            pe.wait_ge(mix_ready, C)
            for t, (t0, n) in enumerate(TILES):
                k = slice((C - 1) * P, C * P)
                three(acc(0, t), w_hi[0][:, k], w_lo[0][:, k], mix_hi[:, C - 1, t0:t0 + n], mix_lo[:, C - 1, t0:t0 + n],
                      False, True).then_inc(acc_ready, 1)
            for c in range(C):
                ins = nc.tensor.transpose(psum[0:2 + 2 * NB, 6 + c // 4, (c % 4) * P:(c % 4 + 1) * P],
                                          convT[:, c, :], ident[:, :])
                if c % 4 == 3:
                    ins.then_inc(conv_tr, 1)

            plain("out", mix_hi, mix_lo, start=1)
            pe.wait_ge(conv_rows_done, 2)
            norm("n_mix", PAIR)

            def ffn(layer):
                name = f"ffn{layer}"
                n0, b0, c0 = SLAB0[name], BLK0[name], layer * 22

                def gate_up(n, blk, first=False):
                    if first:
                        first_two(n, blk, xs_hi, xs_lo, XS0[name])
                    for u in range(2 if first else 0, 4):
                        slab(n + u, u % 2)
                        block8(blk + u, u, u % 2, xs_hi, xs_lo)

                def down(n, blk, chunks, par):
                    pe.wait_ge(hid_ready, chunks * NT + NT)
                    for s in range(2):
                        slab(n + s, s)
                        for m in range(4):
                            for t, (t0, nn) in enumerate(TILES):
                                pe.wait_ge(acc_free, blk * NT + ((4 * s + m) * NT + t + 1))
                                for c in range(2):
                                    k = slice(c * 512 + m * P, c * 512 + (m + 1) * P)
                                    ins = three(acc(m, t), w_hi[s][:, k], w_lo[s][:, k],
                                                hid_hi[par][:, c, t0:t0 + nn], hid_lo[par][:, c, t0:t0 + nn],
                                                c == 0, c == 1)
                                ins.then_inc(acc_ready, 1)

                gate_up(n0, b0, True)
                with pe.Fori(0, 5) as i:
                    gate_up(i * 12 + (n0 + 4), i * 24 + (b0 + 4))
                    down(i * 12 + (n0 + 8), i * 24 + (b0 + 8), i * 4 + (c0 + 2), 0)
                    gate_up(i * 12 + (n0 + 10), i * 24 + (b0 + 16))
                    down(i * 12 + (n0 + 14), i * 24 + (b0 + 20), i * 4 + (c0 + 4), 1)
                down(n0 + 64, b0 + 124, c0 + 22, 0)

            def ple(layer):
                pe.wait_ge(p_landed, 16 * NTB * (layer + 1))
                pe.wait_ge(acc_free, ACCS + NT * BLK0[f"pg{layer}"])
                for tb, (t0, n) in enumerate(TOKB):
                    if tb >= 6:
                        pe.wait_ge(p_ready, layer * NTB + tb - 5)
                    for c in range(2):
                        ins = nc.tensor.transpose(psum[:, tb % 6, c * P:c * P + n], p_nat[0:n, tb, c * P:(c + 1) * P],
                                                  ident[0:n, 0:n])
                    ins.then_inc(p_tr, 1)
                norm(f"n_ffn{layer}", POST)
                pe.wait_ge(p_ready, (layer + 1) * NTB)
                slab(SLAB0[f"pp{layer}"] + 1, 1)
                n0, b0 = SLAB0[f"pg{layer}"], BLK0[f"pg{layer}"]
                for m in range(C):
                    for t, (t0, n) in enumerate(TILES):
                        pe.wait_ge(acc_free, NT * b0 + (ACCS if m == 0 else 6 * m + 2 * t + 2))
                        for c in range(2):
                            k = slice(c * 512 + (m % 4) * P, c * 512 + (m % 4 + 1) * P)
                            ins = three(acc(0, t), wp_hi[:, m // 4, k], wp_lo[:, m // 4, k],
                                        pT_hi[:, c, t0:t0 + n], pT_lo[:, c, t0:t0 + n], c == 0, c == 1)
                        ins.then_inc(acc_ready, 1)
                    slab(n0 + m, m % 2)
                    for t, (t0, n) in enumerate(TILES):
                        if m == 0:
                            tile_in_parts([(acc(1, t), 0)], xs_hi, xs_lo, XS0[f"pg{layer}"], t)
                            continue
                        for c in range(C):
                            k = slice(c * P, (c + 1) * P)
                            ins = three(acc(1, t), w_hi[m % 2][:, k], w_lo[m % 2][:, k],
                                        xs_hi[:, c, t0:t0 + n], xs_lo[:, c, t0:t0 + n], c == 0, c == C - 1)
                        ins.then_inc(acc_ready, 1)

            ffn(0)
            ple(0)
            norm("n_kv", PRE)
            plain("k", xs_hi, xs_lo, XS0["kvq"], two=True)
            pe.wait_ge(wf_lo_s, 1)
            pe.wait_ge(rb_used, STEP0["n_kv"] + NT)
            for t, (t0, n) in enumerate(TILES):
                if t == 2:
                    pe.wait_ge(f_z, 1)
                for c in range(C):
                    ins = three(psum[0:H, 6 + t % 2, 0:n], wf_hi[:, c, :], wf_lo[:, c, :],
                                xs_hi[:, c, t0:t0 + n], xs_lo[:, c, t0:t0 + n], c == 0, c == C - 1)
                ins.then_inc(f_acc, 1)

            def out_of(src):
                def go(tb, t0, n, half, c, bank):
                    return nc.tensor.transpose(psum[0:n, bank, c * P:(c + 1) * P], src[:, 4 * half + c, t0:t0 + n],
                                               ident[:, :])
                return go
            def key_row(tb):
                g, (t0, n) = TR_K + tb, TOKB[tb]
                if tb == 0:
                    pe.wait_ge(f_step, 1)
                    for b in range(NTB):
                        b0 = min(b * P, T - P)
                        ins = nc.tensor.transpose(psum[:, 6, b * H:(b + 1) * H], flog[:, b0:b0 + P], ident[0:H, 0:H])
                    ins.then_inc(f_tr, 1)
                    pe.wait_ge(f_step, 2)
                pe.wait_ge(tr_act, g)
                pe.wait_ge(tr_dve, g)
                for half in range(2):
                    for c in range(4):
                        ins = out_of(y)(tb, t0, n, half, c, 6 + half)
                    ins.then_inc(tr_ready, 1)

            pe.wait_ge(acc_free, ACCS + NT * (BLK0["k"] + 8))
            plain("q", xs_hi, xs_lo, after=key_row)
            key_row(8)

            def forget_rows(m):
                if m:
                    return
                pe.wait_ge(tr_act, TR_V)
                pe.wait_ge(tr_dve, TR_V)
                for tb in range(8):
                    ins = nc.tensor.transpose(psum[0:H, 6 + tb // 4, (tb % 4) * P:(tb % 4 + 1) * P], lf[:, tb, :],
                                              ident[:, :])
                    if tb % 4 == 3:
                        ins.then_inc(f_tr, 1)

            plain("v", xs_hi, xs_lo, after=forget_rows)
            pe.wait_ge(acc_free, ACCS + NT * (BLK0["v"] + 8))
            nc.tensor.transpose(psum[0:H, 5, 0:P], lf[:, 8, :], ident[:, :]).then_inc(f_tr, 1)
            transposes_in(TR_V, out_of(vT))
            pe.wait_ge(tr_act, TR_Y)
            pe.wait_ge(tr_dve, TR_Y)

            pe.sem_inc(pv_done, 2)
            pe.wait_ge(mask_ready, 2)

            def scores(hp, j):
                (hh, qb), b = ITEMS[j % NI], s_banks(j)
                if j % 8 == 0:
                    pe.wait_ge(aug_landed[hh], hp * 32 + 32 * (1 + j // NI))
                    pe.wait_ge(split_act, hp * 6 + (6 * (j // NI) + 3 * hh + 3))
                    pe.wait_ge(split_dve, hp * 4 + (4 * (j // NI) + 2 * hh + 2))
                pe.wait_ge(exp_done, hp * NI + (j + 3 if j % 2 else j + 1))
                qs = slice(qb * P, (qb + 1) * P)
                for part in range((qb + 4) // 4):
                    k0 = 512 * part
                    k1 = min(k0 + 512, (qb + 1) * P)
                    diag = k1 == (qb + 1) * P
                    M(psum[:, b + part, 0:k1 - k0], q_hl[hh][:, qs], k_hh[hh][:, k0:k1], start=True, stop=False)
                    M(psum[:, b + part, 0:k1 - k0], q_high[hh][:, qs], k_low[hh][:, k0:k1], start=False, stop=not diag)
                    if diag:
                        M(psum[:, b + part, k1 - k0 - P:k1 - k0], ident_r[:, :], causal_r[:, :], start=False,
                          stop=True).then_inc(s_ready, 1)

            def transpose_probs(hp, j):
                pe.wait_ge(exp_done, hp * NI + (j + 5))
                for g, kb, nb in groups(j):
                    pe.wait_ge((pt_act, pt_dve)[g % 2], ghalf(hp, g - g % 2) + 1)
                    for c in range(nb):
                        ins = nc.tensor.transpose(psum[:, 5 + g % 2, c * P:(c + 1) * P],
                                                  prob[j % 2][:, (kb + c) * P:(kb + c + 1) * P], ident[:, :])
                    ins.then_inc(pt_ready, 1)

            def outputs(hp, j):
                hh, qb = ITEMS[j]
                for g, kb, nb in groups(j):
                    pe.wait_ge((pt_act, pt_dve)[g % 2], ghalf(hp, g - g % 2) + 2)
                pe.wait_ge(o_taken, hp * NI + (j + 1))
                for c in range(qb + 1):
                    ins = M(psum[:, 7, 0:DH], probT[j % 2][:, c, :],
                            v_keys[:, c, ds(hp * P + DH * hh, DH)], start=c == 0, stop=c == qb)
                ins.then_inc(pv_done, 1)

            def transpose_o(hp, dve0, act0):
                pe.wait_ge(o_taken, hp * NI + (NI + 1))
                for r in range(2):
                    pe.wait_ge((pt_dve, pt_act)[r], (dve0, act0)[r] + 1)
                    for c in range(4):
                        ins = nc.tensor.transpose(psum[:, 6 - r, c * P:(c + 1) * P], o_pair[:, 4 * r + c, :], ident[:, :])
                    ins.then_inc(pt_ready, 1)

            def pair(hp, first, last):
                for j in range(NI):
                    if not (last and j >= NI - 2):
                        scores(hp, j + 2)
                    transpose_probs(hp, j)
                    if j == 1 and not first:
                        transpose_o(hp - 1, hp * 13, hp * 13 + 1)
                    if j > 0:
                        outputs(hp, j - 1)
                    elif not first:
                        outputs(hp - 1, NI - 1)

            scores(0, 0)
            scores(0, 1)
            pair(0, True, False)
            with pe.Fori(1, HP - 1) as hp:
                pair(hp, False, False)
            pair(HP - 1, False, True)
            outputs(HP - 1, NI - 1)
            transpose_o(HP - 1, 13 * HP - 1, 13 * HP - 1)

            pe.sem_inc(st_ready, 3)
            pe.sem_inc(spv_done, 2)
            pe.wait_ge(pt_act, 1 + 13 * HP)
            pe.wait_ge(pt_dve, 1 + 13 * HP)
            pe.wait_ge(consts, 13)
            pe.wait_ge(new_landed, 32)

            def page(b, pg, na, nv):
                pe.wait_ge(kpage_landed[pg % 4], b * 32 + 16 * (pg // 4 + 1))
                for half in range(2):
                    pe.wait_ge((st_act, st_dve)[half], (na, nv)[half] + 1)
                    for c in range(4):
                        f0 = (4 * half + c) * P
                        ins = nc.tensor.transpose(psum[:, 4 + half, c * P:(c + 1) * P], kpage[pg % 4][:, f0:f0 + P],
                                                  ident[:, :])
                    ins.then_inc(st_ready, 1)

            def forget_values(b, na, nv):
                pe.wait_ge(lfpage_landed, b * (16 * NPG) + 16 * NPG)
                for r in range(2):
                    pe.wait_ge((st_act, st_dve)[r], (na, nv)[r] + 1)
                    for c in range(4):
                        ins = nc.tensor.transpose(psum[0:H, 4 + r, c * P:(c + 1) * P], lf_page[:, 4 * r + c, :],
                                                  ident[:, :])
                    ins.then_inc(st_ready, 1)

            def q_of(par, c):
                return qbd[par][:, c * P:(c + 1) * P]

            def sample_probs(b, na, nv):
                pe.wait_ge(ss_exp, b * 2 + 4)
                for g in range(3):
                    pe.wait_ge((st_act, st_dve, st_act)[g], (na, nv, na + 1)[g] + 1)
                    if g == 2:
                        pe.sem_inc(passed, 1)
                    for c in range(4 * g, min(4 * g + 4, 9)):
                        n = P if c < 8 else NS
                        ins = nc.tensor.transpose(psum[0:n, 4 + g % 2, (c % 4) * P:(c % 4 + 1) * P],
                                                  sprob[:, c * P:c * P + n], ident[:, :])
                    ins.then_inc(st_ready, 1)

            def sample_pv(b, na, nv):
                pe.wait_ge(st_act, na + 3)
                pe.wait_ge(st_dve, nv + 2)
                for f in range(2):
                    pe.wait_ge(vpage_landed[f], b * (16 * NPG) + 16 * NPG)
                    fs = slice(512 * f, 512 * f + 512)
                    for pg in range(NPG):
                        M(psum[:, 6 + f, :], sprobT[:, pg, :], v_page[:, pg, fs], start=pg == 0, stop=False)
                    M(psum[:, 6 + f, :], sprobT[0:NS, 8, :], v_new[:, fs], start=False, stop=True).then_inc(spv_done, 1)

            def out_back(b):
                for f in range(2):
                    pe.wait_ge(so_rows, b * 2 + 2)
                    for c in range(4):
                        f0 = (4 * f + c) * P
                        ins = nc.tensor.transpose(psum[:, 6 + f, 112 * c:112 * c + P], o_rows[:, f0:f0 + P], ident[:, :])
                    ins.then_inc(so_tr, 1)

            def sequence(b, par, first, last):
                _, na, nv = st_before(b)
                for i in range(4):
                    page(b, 4 + i, na + i, nv + i)
                    if i == 0:
                        pe.wait_ge(qbd_ready, b * 2 + 2)
                        if not first:
                            pe.wait_ge(ss_exp, b * 2)
                        pe.wait_ge(st_act, na + 1)
                        pe.wait_ge(st_dve, nv + 1)
                    for c in (2 * i, 2 * i + 1):
                        M(psum[:, 2 * par, :], q_of(par, c), kT[0][:, c, :], start=c == 0, stop=False)
                pe.wait_ge(fb_ready, b + 1)
                M(psum[:, 2 * par, :], nexpand[:, :], cum[:, 0:512], start=False, stop=True)
                if not first:
                    sample_probs(b - 1, na + 4, nv + 4)
                    sample_pv(b - 1, na + 4, nv + 4)
                M(psum[:, 2 * par + 1, :], nexpand[:, :], cum[:, 512:1024], start=True, stop=False)
                _, ma, mv = st_mid(b, first)
                if not last:
                    forget_values(b + 1, ma, mv)
                for i in range(4):
                    if not last:
                        page(b + 1, i, ma + (1 + i), mv + (1 + i))
                    if i == 0:
                        pe.wait_ge(st_act, na + 5)
                        pe.wait_ge(st_dve, nv + 5)
                    if i == 1 and not first:
                        out_back(b - 1)
                    for c in (2 * i, 2 * i + 1):
                        M(psum[:, 2 * par + 1, :], q_of(par, c), kT[1][:, c, :], start=False, stop=c == C - 1)
                if not first:
                    pe.wait_ge(so_taken, b * 4)
                for c in range(C):
                    M(psum[:, 6, 0:NS], q_of(par, c), k_newT[:, c, :], start=c == 0, stop=False)
                M(psum[:, 6, 0:NS], nexpand[:, :], cum_new[par][:, :], start=False, stop=False)
                M(psum[:, 6, 0:NS], qsel[:, :], wmask[:, ds(b * (-NQ) + 56, NS)], start=False, stop=True)\
                    .then_inc(ss_ready, 1)

            forget_values(0, 2, 1)
            for i in range(4):
                page(0, i, 3 + i, 2 + i)
            sequence(0, 0, True, False)
            with pe.Fori(0, NB // 2 - 1) as i:
                sequence(i * 2 + 1, 1, False, False)
                sequence(i * 2 + 2, 0, False, False)
            sequence(NB - 1, 1, False, True)
            _, na, nv = st_mid(NB - 1, False)
            sample_probs(NB - 1, na, nv)
            sample_pv(NB - 1, na, nv)
            out_back(NB - 1)

            plain("o", xs_hi, xs_lo, XS0["o"])
            norm("n_att", PAIR)
            ffn(1)
            ple(1)
            pe.wait_ge(ple_added, 2 * C * NT)
            pe.wait_ge(acc_free, ACCS + NT * BLKS)
            transposes_in(TR_Y, out_of(h))


_INS = ['x_prompt', 'x_sample', 'state_conv', 'cache_k', 'cache_v', 'cache_logf', 'page_table', 'p_prompt',
        'p_sample', 'norm_g', 'w_in', 'w_conv', 'w_out', 'g_kv', 'w_k', 'w_v', 'w_f', 'b_f', 'w_q', 'w_o',
        'w_gate', 'w_up', 'w_down', 'w_ple', 'w_ple_gate']
_OUTS = [(1, SEQ, D), (NB, NQ, D), (1, 1, 2, D), (1, SEQ, H, DH), (1, SEQ, H, DH), (1, SEQ, H), (1, NB, 2, D),
         (NB, NQ, H, DH), (NB, NQ, H, DH), (NB, NQ, H)]


def kernel(**inputs):
    import numpy as _np
    import concourse.bacc as _bacc
    from concourse import mybir as _mybir
    from concourse.bass_utils import run_bass_kernel_spmd as _run

    nc = _bacc.Bacc("TRN2", target_bir_lowering=False, num_devices=1)
    arrays, ins, outs = {}, [], []
    for name in _INS:
        a = _np.ascontiguousarray(inputs[name])
        arrays[f"in_{name}"] = a
        ins.append(nc.dram_tensor(f"in_{name}", a.shape, _mybir.dt.from_np(a.dtype), kind="ExternalInput").ap())
    for i, shape in enumerate(_OUTS):
        outs.append(nc.dram_tensor(f"out_{i}", shape, F32, kind="ExternalOutput").ap())
    trunk(nc, ins, outs)
    r = _run(nc, [arrays], core_ids=[0])
    return tuple(r.results[0][f"out_{i}"] for i in range(len(_OUTS)))
```
